# Optimizing a Trainium2 kernel written in Bass

```python
import jax, jax.numpy as jnp
from jax import lax
import numpy as np

D_MODEL = 1024
BATCH = 1
SEQ = 512
DEPTH = 2
DEC_BATCH = 8
DEC_SEQ = 8
PAST_LEN = 256
PAGE_SIZE = 128

N_A_LAYERS = DEPTH // 2
N_B_LAYERS = DEPTH - N_A_LAYERS
MIX_WIDTH = D_MODEL
MEM_LEN = 256
H_MEM = 4
HD_MEM = 64
D_MEM = H_MEM * HD_MEM
D_MAIN = MIX_WIDTH - D_MEM
H_A = 4
HD_A = D_MAIN // H_A
H_B = 12
HD_B = D_MAIN // H_B
CONV_W = 4
D_FF = ((8 * D_MODEL // 3 + 127) // 128) * 128
CHUNK = 64
Q_BLOCK = 128
EPS = 1e-6
F_BIAS = 3.0
SB_BIAS_INIT = -6.0
D_IN_A = 4 * D_MAIN + 2 * H_A + D_MEM
D_IN_B = D_MAIN + D_MEM

kernel_name = "yoco_mlstm_stickbreak_macaron_step"

def rms_norm(x, g):
    xf = x.astype(jnp.float32)
    y = xf * lax.rsqrt(jnp.mean(xf * xf, axis=-1, keepdims=True) + EPS)
    return (y * g.astype(jnp.float32)).astype(x.dtype)

def swiglu(h, w_up, w_down):
    g, u = jnp.split(h @ w_up, 2, axis=-1)
    return (jax.nn.silu(g) * u) @ w_down

def memory_kv(mem, g_mem, w_mem_kv, g_k_mem):
    B, M, _ = mem.shape
    mk, mv = jnp.split(rms_norm(mem, g_mem) @ w_mem_kv, 2, axis=-1)
    mk = rms_norm(mk.reshape(B, M, H_MEM, HD_MEM), g_k_mem)
    return mk, mv.reshape(B, M, H_MEM, HD_MEM)

def memory_attention(qm, g_q_mem, mem_k, mem_v):
    B, L, _ = qm.shape
    q = rms_norm(qm.reshape(B, L, H_MEM, HD_MEM), g_q_mem)
    s = jnp.einsum('blhd,bmhd->bhlm', q, mem_k.astype(q.dtype)).astype(jnp.float32) * (HD_MEM ** -0.5)
    p = jax.nn.softmax(s, axis=-1).astype(qm.dtype)
    return jnp.einsum('bhlm,bmhd->blhd', p, mem_v.astype(qm.dtype)).reshape(B, L, D_MEM)

def mlstm_chunk(carry, xs):
    C, n, m = carry
    q, k, v, ig, lf = xs
    L = q.shape[1]
    b = jnp.cumsum(lf, axis=1).transpose(0, 2, 1)
    i_ = ig.transpose(0, 2, 1)
    causal = jnp.tril(jnp.ones((L, L), dtype=bool))
    dlog = jnp.where(causal, b[..., :, None] - b[..., None, :] + i_[..., None, :], -jnp.inf)
    inter = b + m[..., None]
    m_t = jnp.maximum(inter, jnp.max(dlog, axis=-1))
    w = jnp.exp(dlog - m_t[..., None]) * jnp.einsum('bthd,bshd->bhts', q, k)
    w_inter = jnp.exp(inter - m_t)
    cq = jnp.einsum('bhed,bthd->bthe', C, q) * w_inter.transpose(0, 2, 1)[..., None]
    num = jnp.einsum('bhts,bshd->bthd', w, v) + cq
    den = jnp.sum(w, axis=-1) + w_inter * jnp.einsum('bhd,bthd->bht', n, q)
    den = jnp.maximum(jnp.abs(den), jnp.exp(-m_t)).transpose(0, 2, 1)[..., None]
    h = num / den
    m_new = m_t[..., -1]
    w_end = jnp.exp(b[..., -1:] - b + i_ - m_new[..., None])
    decay = jnp.exp(b[..., -1] + m - m_new)
    C_new = decay[..., None, None] * C + jnp.einsum('bhs,bshe,bshd->bhed', w_end, v, k)
    n_new = decay[..., None] * n + jnp.einsum('bhs,bshd->bhd', w_end, k)
    return (C_new, n_new, m_new), h

def mlstm_scan(q, k, v, ig, lf, C0, n0, m0):
    B, L, H, D = q.shape
    chunk = CHUNK if L % CHUNK == 0 else L
    nc = L // chunk

    def to_chunks(a):
        return a.reshape((B, nc, chunk) + a.shape[2:]).swapaxes(0, 1)

    init = (C0.astype(jnp.float32), n0.astype(jnp.float32), m0.astype(jnp.float32))
    carry, h = lax.scan(mlstm_chunk, init, tuple(to_chunks(a) for a in (q, k, v, ig, lf)))
    return h.swapaxes(0, 1).reshape(B, L, H, D), carry

def mlstm_mix(h, mem_k, mem_v, w_in, b_gate, conv_w, conv_b, g_h, g_q_mem, conv_prev, C0, n0, m0):
    B, L, _ = h.shape
    qk_pre, v, o_pre, gates, qm = jnp.split(h @ w_in, [2 * D_MAIN, 3 * D_MAIN, 4 * D_MAIN, 4 * D_MAIN + 2 * H_A], axis=-1)
    gates = gates.astype(jnp.float32) + b_gate.astype(jnp.float32)
    ig = gates[..., :H_A]
    lf = jax.nn.log_sigmoid(gates[..., H_A:])
    buf = jnp.concatenate([conv_prev.astype(qk_pre.dtype), qk_pre], axis=1)
    qk = conv_b
    for j in range(CONV_W):
        qk = qk + buf[:, j:j + L] * conv_w[j]
    qk = jax.nn.silu(qk)
    new_conv = buf[:, buf.shape[1] - (CONV_W - 1):]
    q, k = jnp.split(qk.astype(jnp.float32), 2, axis=-1)
    q = q.reshape(B, L, H_A, HD_A)
    k = k.reshape(B, L, H_A, HD_A) * (HD_A ** -0.5)
    v = v.astype(jnp.float32).reshape(B, L, H_A, HD_A)
    hA, (C, n, m) = mlstm_scan(q, k, v, ig, lf, C0, n0, m0)
    o = jax.nn.sigmoid(o_pre.astype(jnp.float32)).reshape(B, L, H_A, HD_A)
    hA = (rms_norm(hA, g_h) * o).reshape(B, L, D_MAIN).astype(h.dtype)
    mem_out = memory_attention(qm, g_q_mem, mem_k, mem_v)
    return jnp.concatenate([hA, mem_out], axis=-1), new_conv, C, n, m

def stick_breaking(q, k, v, q_offset, bias):
    B, Lq, H, D = q.shape
    Lk = k.shape[1]
    blk = Q_BLOCK if Lq % Q_BLOCK == 0 else Lq
    nb = Lq // blk
    k_pos = jnp.arange(Lk, dtype=jnp.int32)
    scale = HD_B ** -0.5
    bias = bias.astype(jnp.float32)[None, :, None, None]

    def block(args):
        qb, start = args
        q_pos = start + jnp.arange(blk, dtype=jnp.int32)
        mask = k_pos[None, :] < q_pos[:, None]
        z = jnp.einsum('bqhd,bkhd->bhqk', qb, k).astype(jnp.float32) * scale + bias
        log_keep = jnp.where(mask, jax.nn.log_sigmoid(-z), 0.0)
        later = lax.cumsum(log_keep, axis=3, reverse=True) - log_keep
        a = jnp.where(mask, jnp.exp(jax.nn.log_sigmoid(z) + later), 0.0)
        return jnp.einsum('bhqk,bkhd->bqhd', a.astype(v.dtype), v)

    qs = q.reshape(B, nb, blk, H, D).transpose(1, 0, 2, 3, 4)
    starts = q_offset + jnp.arange(nb, dtype=jnp.int32) * blk
    out = lax.map(block, (qs, starts))
    return out.transpose(1, 0, 2, 3, 4).reshape(B, Lq, H * D)

def sb_mix(h, k_all, v_all, q_offset, mem_k, mem_v, w_in, g_q_b, b_sb, g_q_mem):
    B, L, _ = h.shape
    qb, qm = jnp.split(h @ w_in, [D_MAIN], axis=-1)
    qb = rms_norm(qb.reshape(B, L, H_B, HD_B), g_q_b)
    out_b = stick_breaking(qb, k_all, v_all, q_offset, b_sb)
    mem_out = memory_attention(qm, g_q_mem, mem_k, mem_v)
    return jnp.concatenate([out_b.astype(h.dtype), mem_out], axis=-1)

def shared_kv(x, g_kv, w_kv, g_k_b):
    B, L, _ = x.shape
    k, v = jnp.split(rms_norm(x, g_kv) @ w_kv, 2, axis=-1)
    k = rms_norm(k.reshape(B, L, H_B, HD_B), g_k_b)
    return k, v.reshape(B, L, H_B, HD_B)

def run_trunk(x, mem_k, mem_v, conv0, C0, n0, m0, past_k, past_v,
              g_ffn1, w_ffn1_up, w_ffn1_down, g_mix, w_in_a, b_gate_a, conv_w_a, conv_b_a, g_h_a,
              g_kv, w_kv, g_k_b, w_in_b, g_q_b, b_sb, g_q_mem, w_out, g_ffn2, w_ffn2_up, w_ffn2_down):
    q_offset = past_k.shape[1]
    k_new = v_new = k_all = v_all = None
    convs, Cs, ns, ms = [], [], [], []
    for l in range(DEPTH):
        if l == N_A_LAYERS:
            k_new, v_new = shared_kv(x, g_kv, w_kv, g_k_b)
            k_all = jnp.concatenate([past_k.astype(k_new.dtype), k_new], axis=1)
            v_all = jnp.concatenate([past_v.astype(v_new.dtype), v_new], axis=1)
        x = x + 0.5 * swiglu(rms_norm(x, g_ffn1[l]), w_ffn1_up[l], w_ffn1_down[l])
        h = rms_norm(x, g_mix[l])
        if l < N_A_LAYERS:
            mix, cv, C, n, m = mlstm_mix(h, mem_k[l], mem_v[l], w_in_a[l], b_gate_a[l], conv_w_a[l], conv_b_a[l],
                                         g_h_a[l], g_q_mem[l], conv0[l], C0[l], n0[l], m0[l])
            convs.append(cv)
            Cs.append(C)
            ns.append(n)
            ms.append(m)
        else:
            j = l - N_A_LAYERS
            mix = sb_mix(h, k_all, v_all, q_offset, mem_k[l], mem_v[l], w_in_b[j], g_q_b[j], b_sb[j], g_q_mem[l])
        x = x + mix @ w_out[l]
        x = x + 0.5 * swiglu(rms_norm(x, g_ffn2[l]), w_ffn2_up[l], w_ffn2_down[l])
    return x, k_new, v_new, jnp.stack(convs), jnp.stack(Cs), jnp.stack(ns), jnp.stack(ms)

def setup_inputs(seed: int = 0) -> dict:
    key = jax.random.key(seed)
    ks = list(jax.random.split(key, 64))

    def nrm(shape, scale=1.0):
        return jax.random.normal(ks.pop(), shape, jnp.float32) * scale

    def gain(shape):
        return 1.0 + 0.05 * jax.random.normal(ks.pop(), shape, jnp.float32)

    n_pages = PAST_LEN // PAGE_SIZE
    n_used = DEC_BATCH * n_pages
    n_phys = n_used + max(1, n_used // 4)
    page_table = jax.random.permutation(ks.pop(), n_phys)[:n_used].reshape(DEC_BATCH, n_pages).astype(jnp.int32)
    b_gate_a = jnp.concatenate([nrm((N_A_LAYERS, H_A), 0.1), F_BIAS + nrm((N_A_LAYERS, H_A), 0.5)], axis=-1)
    d = D_MODEL ** -0.5
    return {
        "x_prompt": nrm((BATCH, SEQ, D_MODEL)),
        "x_sample": nrm((DEC_BATCH, DEC_SEQ, D_MODEL)),
        "cache_k": nrm((n_phys, PAGE_SIZE, H_B, HD_B)),
        "cache_v": nrm((n_phys, PAGE_SIZE, H_B, HD_B)),
        "cache_mem_k": nrm((DEPTH, DEC_BATCH, MEM_LEN, H_MEM, HD_MEM)),
        "cache_mem_v": nrm((DEPTH, DEC_BATCH, MEM_LEN, H_MEM, HD_MEM)),
        "state_C": nrm((N_A_LAYERS, DEC_BATCH, H_A, HD_A, HD_A), 0.05),
        "state_n": nrm((N_A_LAYERS, DEC_BATCH, H_A, HD_A), 0.5),
        "state_m": nrm((N_A_LAYERS, DEC_BATCH, H_A), 0.5),
        "state_conv": nrm((N_A_LAYERS, DEC_BATCH, CONV_W - 1, 2 * D_MAIN)),
        "page_table": page_table,
        "mem_prompt": nrm((BATCH, MEM_LEN, D_MODEL)),
        "g_ffn1": gain((DEPTH, D_MODEL)),
        "w_ffn1_up": nrm((DEPTH, D_MODEL, 2 * D_FF), d),
        "w_ffn1_down": nrm((DEPTH, D_FF, D_MODEL), D_FF ** -0.5),
        "g_mix": gain((DEPTH, D_MODEL)),
        "w_in_a": nrm((N_A_LAYERS, D_MODEL, D_IN_A), d),
        "b_gate_a": b_gate_a,
        "conv_w_a": nrm((N_A_LAYERS, CONV_W, 2 * D_MAIN), CONV_W ** -0.5),
        "conv_b_a": nrm((N_A_LAYERS, 2 * D_MAIN), 0.01),
        "g_h_a": gain((N_A_LAYERS, H_A, HD_A)),
        "g_kv": gain((D_MODEL,)),
        "w_kv": nrm((D_MODEL, 2 * D_MAIN), d),
        "g_k_b": gain((HD_B,)),
        "w_in_b": nrm((N_B_LAYERS, D_MODEL, D_IN_B), d),
        "g_q_b": gain((N_B_LAYERS, HD_B)),
        "b_sb": SB_BIAS_INIT + nrm((N_B_LAYERS, H_B), 0.5),
        "g_mem": gain((DEPTH, D_MODEL)),
        "w_mem_kv": nrm((DEPTH, D_MODEL, 2 * D_MEM), d),
        "g_q_mem": gain((DEPTH, HD_MEM)),
        "g_k_mem": gain((DEPTH, HD_MEM)),
        "w_out": nrm((DEPTH, MIX_WIDTH, D_MODEL), MIX_WIDTH ** -0.5),
        "g_ffn2": gain((DEPTH, D_MODEL)),
        "w_ffn2_up": nrm((DEPTH, D_MODEL, 2 * D_FF), d),
        "w_ffn2_down": nrm((DEPTH, D_FF, D_MODEL), D_FF ** -0.5),
    }

def reference(x_prompt, x_sample, cache_k, cache_v, cache_mem_k, cache_mem_v, state_C, state_n, state_m,
              state_conv, page_table, mem_prompt, g_ffn1, w_ffn1_up, w_ffn1_down, g_mix, w_in_a, b_gate_a,
              conv_w_a, conv_b_a, g_h_a, g_kv, w_kv, g_k_b, w_in_b, g_q_b, b_sb, g_mem, w_mem_kv, g_q_mem, g_k_mem,
              w_out, g_ffn2, w_ffn2_up, w_ffn2_down):
    mks, mvs = [], []
    for l in range(DEPTH):
        mk, mv = memory_kv(mem_prompt, g_mem[l], w_mem_kv[l], g_k_mem[l])
        mks.append(mk)
        mvs.append(mv)
    mem_k_prompt = jnp.stack(mks)
    mem_v_prompt = jnp.stack(mvs)
    Bp = x_prompt.shape[0]
    conv0 = jnp.zeros((N_A_LAYERS, Bp, CONV_W - 1, 2 * D_MAIN), x_prompt.dtype)
    C0 = jnp.zeros((N_A_LAYERS, Bp, H_A, HD_A, HD_A), jnp.float32)
    n0 = jnp.zeros((N_A_LAYERS, Bp, H_A, HD_A), jnp.float32)
    m0 = jnp.zeros((N_A_LAYERS, Bp, H_A), jnp.float32)
    empty = jnp.zeros((Bp, 0, H_B, HD_B), x_prompt.dtype)
    y_prompt, k_prompt, v_prompt, conv_prompt, C_prompt, n_prompt, m_prompt = run_trunk(
        x_prompt, mem_k_prompt, mem_v_prompt, conv0, C0, n0, m0, empty, empty,
        g_ffn1, w_ffn1_up, w_ffn1_down, g_mix, w_in_a, b_gate_a, conv_w_a, conv_b_a, g_h_a,
        g_kv, w_kv, g_k_b, w_in_b, g_q_b, b_sb, g_q_mem, w_out, g_ffn2, w_ffn2_up, w_ffn2_down)
    Bs = x_sample.shape[0]
    past_len = page_table.shape[1] * cache_k.shape[1]
    past_k = cache_k[page_table].reshape(Bs, past_len, H_B, HD_B)
    past_v = cache_v[page_table].reshape(Bs, past_len, H_B, HD_B)
    y_sample, k_sample, v_sample, conv_sample, C_sample, n_sample, m_sample = run_trunk(
        x_sample, cache_mem_k, cache_mem_v, state_conv, state_C, state_n, state_m, past_k, past_v,
        g_ffn1, w_ffn1_up, w_ffn1_down, g_mix, w_in_a, b_gate_a, conv_w_a, conv_b_a, g_h_a,
        g_kv, w_kv, g_k_b, w_in_b, g_q_b, b_sb, g_q_mem, w_out, g_ffn2, w_ffn2_up, w_ffn2_down)
    return (y_prompt, y_sample, k_prompt, v_prompt, k_sample, v_sample, mem_k_prompt, mem_v_prompt,
            conv_prompt, C_prompt, n_prompt, m_prompt, conv_sample, C_sample, n_sample, m_sample)


_drawn_inputs = setup_inputs


def setup_inputs(seed=0):
    import zlib

    import numpy as np

    out = dict(_drawn_inputs(seed))
    spreads = {}
    factors = {'conv_b_a': 2.887, 'g_q_b': 8.0, 'g_q_mem': 8.0}
    for name, (base, spread) in spreads.items():
        noise = np.random.default_rng([zlib.crc32(name.encode()), seed]).standard_normal(out[name].shape)
        drawn = base * np.exp(spread * noise) if base else spread * noise
        out[name] = __import__('jax').numpy.asarray(drawn.astype(out[name].dtype))
    for name, factor in factors.items():
        out[name] = (out[name] * factor).astype(out[name].dtype)
    return out
```

```python
from contextlib import ExitStack

import concourse.bass as bass
from concourse import mybir

ALU = mybir.AluOpType
ACT = mybir.ActivationFunctionType
F32 = mybir.dt.float32
F32R = mybir.dt.float32r
I32 = mybir.dt.int32
AX = mybir.AxisListType.X

P = 128
D = 1024
KD = D // P
NPR = 512
NB, NS = 8, 8
NSA = NB * NS
TOK = NPR + NSA
HALF = TOK // 2
TT = 5
FF = 2816
FF_PARTS = (12, 10)
M = 256
HM, DM = 4, 64
HA, DA = 4, 192
DH = DA // 2
HB, DB = 12, 64
D_MAIN = 768
PAST, PAGE = 256, 128
EPS = 1e-6
NEG = -1e30
SLOT = 2048

FFN_TILES = sum(n + KD for n in FF_PARTS)
BASE_MEM = 0
BASE_FFN = [4]
BASE_INA = BASE_FFN[0] + FFN_TILES
INA_TILES = 18
BASE_OUTA = BASE_INA + INA_TILES
BASE_FFN.append(BASE_OUTA + 4)
BASE_KV = BASE_FFN[1] + FFN_TILES
BASE_FFN.append(BASE_KV + 6)
BASE_INB = BASE_FFN[2] + FFN_TILES
BASE_OUTB = BASE_INB + 4
BASE_FFN.append(BASE_OUTB + 4)
N_TILES = BASE_FFN[3] + FFN_TILES


class Count:

    def __init__(self):
        self.at = {}

    def __call__(self, name, by=1):
        self.at[name] = self.at.get(name, 0) + by
        return self.at[name]


class Semaphores:

    def __init__(self, sem):
        self.consts_ready = sem("consts_ready")
        self.inputs_loaded = sem("inputs_loaded")
        self.setup_turned = sem("setup_turned")
        self.setup_copied = sem("setup_copied")
        self.mem_squared = sem("mem_squared")
        self.mem_rms_ready = sem("mem_rms_ready")
        self.mem_scaled = sem("mem_scaled")
        self.mem_split = sem("mem_split")
        self.mem_hi = sem("mem_hi")
        self.raw_loaded0 = sem("raw_loaded0")
        self.raw_loaded1 = sem("raw_loaded1")
        self.hi_ready = sem("hi_ready")
        self.lo_ready = sem("lo_ready")
        self.tile_done = sem("tile_done")
        self.region_free0 = sem("region_free0")
        self.region_free1 = sem("region_free1")
        self.dve_step = sem("dve_step")
        self.pool_step = sem("pool_step")
        self.act_step = sem("act_step")
        self.sq_ready = sem("sq_ready")
        self.sum_done = sem("sum_done")
        self.sumsq_ready = sem("sumsq_ready")
        self.rms_ready = sem("rms_ready")
        self.xn_ready = sem("xn_ready")
        self.nh_ready = sem("nh_ready")
        self.nl_ready = sem("nl_ready")
        self.sg_ready = sem("sg_ready")
        self.hh_ready = sem("hh_ready")
        self.hl_ready = sem("hl_ready")
        self.mk_sq = sem("mk_sq")
        self.mk_ms = sem("mk_ms")
        self.mk_rms = sem("mk_rms")
        self.mk_ready = sem("mk_ready")
        self.mkt_ready = sem("mkt_ready")
        self.mkt_copied = sem("mkt_copied")
        self.stored = sem("stored")
        self.y_turned = sem("y_turned")
        self.y_copied = sem("y_copied")
        self.y_stored = sem("y_stored")
        self.gate_abs = sem("gate_abs")
        self.gate_ln = sem("gate_ln")
        self.gate_m = sem("gate_m")
        self.gate_rows = sem("gate_rows")
        self.a_loaded = sem("a_loaded")
        self.hist_turned = sem("hist_turned")
        self.hist_ready = sem("hist_ready")
        self.conv_ready = sem("conv_ready")
        self.qk_silu = sem("qk_silu")
        self.k_scaled = sem("k_scaled")
        self.cols_turned = sem("cols_turned")
        self.dve_cols = sem("dve_cols")
        self.tails_turned = sem("tails_turned")
        self.tails_ready = sem("tails_ready")
        self.tails_stored = sem("tails_stored")
        self.gh_loaded = sem("gh_loaded")
        self.m_stored = sem("m_stored")
        self.head_stored = sem("head_stored")
        self.state_loaded0 = sem("state_loaded0")
        self.state_loaded1 = sem("state_loaded1")
        self.state_loaded2 = sem("state_loaded2")
        self.state_loaded3 = sem("state_loaded3")
        self.state_stored0 = sem("state_stored0")
        self.state_stored1 = sem("state_stored1")
        self.state_stored2 = sem("state_stored2")
        self.state_stored3 = sem("state_stored3")
        self.state_new = sem("state_new")
        self.heads_state = sem("heads_state")
        self.h_scaled = sem("h_scaled")
        self.h_squared = sem("h_squared")
        self.h_ms = sem("h_ms")
        self.h_rms = sem("h_rms")
        self.num_copied = sem("num_copied")
        self.qk_ready = sem("qk_ready")
        self.exponents_ready = sem("exponents_ready")
        self.exp_ready = sem("exp_ready")
        self.w_ready = sem("w_ready")
        self.num_prompt = sem("num_prompt")
        self.k_turned = sem("k_turned")
        self.wv_ready = sem("wv_ready")
        self.prompt_state = sem("prompt_state")
        self.state_turned = sem("state_turned")
        self.state_turned_copied = sem("state_turned_copied")
        self.num_sample = sem("num_sample")
        self.update_ready = sem("update_ready")
        self.q_squared = sem("q_squared")
        self.q_summed = sem("q_summed")
        self.q_rms = sem("q_rms")
        self.q_normed = sem("q_normed")
        self.ma_scores = sem("ma_scores")
        self.ma_max = sem("ma_max")
        self.ma_exp = sem("ma_exp")
        self.ma_p = sem("ma_p")
        self.ma_turned = sem("ma_turned")
        self.ma_pt = sem("ma_pt")
        self.ma_out = sem("ma_out")
        self.ma_out_hi = sem("ma_out_hi")
        self.ma_out_lo = sem("ma_out_lo")
        self.ms_qz = sem("ms_qz")
        self.ms_turned = sem("ms_turned")
        self.ms_kt = sem("ms_kt")
        self.ms_scores = sem("ms_scores")
        self.ms_max = sem("ms_max")
        self.ms_exp = sem("ms_exp")
        self.ms_p = sem("ms_p")
        self.ms_pturned = sem("ms_pturned")
        self.ms_pt = sem("ms_pt")
        self.ms_out = sem("ms_out")
        self.ks_loaded0 = sem("ks_loaded0")
        self.ks_loaded1 = sem("ks_loaded1")
        self.ks_loaded2 = sem("ks_loaded2")
        self.ks_loaded3 = sem("ks_loaded3")
        self.vs_loaded = sem("vs_loaded")
        self.mix_turned = sem("mix_turned")
        self.mix_hi = sem("mix_hi")
        self.mix_lo = sem("mix_lo")
        self.k_ready = sem("k_ready")
        self.kt_turned = sem("kt_turned")
        self.kt_copied = sem("kt_copied")
        self.kn_padded = sem("kn_padded")
        self.k_squared = sem("k_squared")
        self.k_ms = sem("k_ms")
        self.k_rms = sem("k_rms")
        self.kv_stored = sem("kv_stored")
        self.z_ready = sem("z_ready")
        self.z_read = sem("z_read")
        self.a_ready = sem("a_ready")
        self.a_turned = sem("a_turned")
        self.at_ready = sem("at_ready")
        self.stick_out = sem("stick_out")
        self.stick_hi = sem("stick_hi")
        self.stick_lo = sem("stick_lo")
        self.vp_loaded = sem("vp_loaded")
        self.table_loaded = sem("table_loaded")
        self.pages_loaded0 = sem("pages_loaded0")
        self.pages_loaded1 = sem("pages_loaded1")
        self.kpg_turned = sem("kpg_turned")
        self.kpt_ready = sem("kpt_ready")
        self.qzb_ready = sem("qzb_ready")
        self.zs_ready = sem("zs_ready")
        self.zs_read = sem("zs_read")
        self.as_ready = sem("as_ready")
        self.as_turned = sem("as_turned")
        self.ats_ready = sem("ats_ready")
        self.sb_out = sem("sb_out")
        self.sb_hi = sem("sb_hi")
        self.sb_lo = sem("sb_lo")


class MemoryBuffers:

    def __init__(self, normed, qn, e, pt, qz, ks, vs, kt):
        self.normed = normed
        self.qn, self.e, self.pt, self.qz, self.ks, self.vs, self.kt = qn, e, pt, qz, ks, vs, kt


def build(nc, I, O):
    ctx = ExitStack()
    with ctx:
        def sb(name, shape, dt=F32, scope=ctx):
            return scope.enter_context(nc.sbuf_tensor(name, shape, dt))

        def sem(name):
            return ctx.enter_context(nc.semaphore(name))

        S = Semaphores(sem)
        raw_loaded = (S.raw_loaded0, S.raw_loaded1)
        region_free = (S.region_free0, S.region_free1)

        psum = ctx.enter_context(nc.psum_tensor("psum", [P, 8, 512], F32))
        flat = psum[:, :, :].rearrange("p b n -> p (b n)")

        def region(j):
            return psum[:, 4 * j:4 * j + 4, :]

        x_t = sb("x_t", [P, KD, TOK])
        raw = [sb(f"raw{j}", [P, SLOT]) for j in range(2)]
        whi = [sb(f"whi{j}", [P, SLOT], F32R) for j in range(2)]
        wlo = [sb(f"wlo{j}", [P, SLOT], F32R) for j in range(2)]
        over = ExitStack()
        e_all = sb("e_all", [P, 1472], scope=over)
        w_all = sb("w_all", [P, 1408], scope=over)
        k_nat = sb("k_nat", [P, TT, DA], scope=over)
        wv = sb("wv", [P, 4, DA], scope=over)
        wv_b = sb("wv_b", [NSA, NB * DA], scope=over)
        h_nat = sb("h_nat", [P, TT, DA], scope=over)
        gh_b = sb("gh_b", [P, D_MAIN], scope=over)
        qm_a = sb("qm_a", [P, 2, TOK], scope=over)
        over.close()
        h_sq = w_all[:, 0:TT * DA].rearrange("p (t n) -> p t n", t=TT)
        act_hi = sb("act_hi", [P, KD, TOK], F32R)
        act_lo = sb("act_lo", [P, KD, TOK], F32R)
        sumsq = sb("sumsq", [P, TOK])
        rinv = sb("rinv", [P, TOK])
        tmp = [sb(f"tmp{j}", [P, TOK]) for j in range(2)]
        sqt = [sb(f"sqt{j}", [P, TOK]) for j in range(2)]
        mk_t = [sb(f"mk_t{l}", [P, 2, M]) for l in range(2)]
        mv = [sb(f"mv{l}", [P, 2, M]) for l in range(2)]
        ident = sb("ident", [P, P])
        ones = sb("ones", [P, P])
        vec_t = sb("vec_t", [P, 75])
        cw_t = sb("cw_t", [DH, 80])
        gk_mem = sb("gk_mem", [P, 2, DM])
        mrinv = sb("mrinv", [P, 2])
        small = sb("small", [P, 64])
        eps = sb("eps", [P, 1])

        def gain(which, l=0):
            at = 8 * {"ffn1": l, "mix": 2 + l, "kv": 4, "mem": 5 + l, "ffn2": 7 + l}[which]
            return vec_t[:, at:at + 8]

        ones_heads = sb("ones_heads", [P, P])
        causal = sb("causal", [P, P])
        causal_b = sb("causal_b", [NSA, NSA])
        own = sb("own", [NSA, NB])
        w_pad = sb("w_pad", [NSA, P])
        before = sb("before", [P, P])
        not_before = sb("not_before", [P, P])
        own_keys = sb("own_keys", [96, 2, NS])
        zero = sb("zero", [P, 1])
        gk_b = sb("gk_b", [P, DB])
        b_all = sb("b_all", [P, HB])
        b_neg = sb("b_neg", [P, HB])
        b_col = sb("b_col", [HB, 1])
        b_rows = sb("b_rows", [96, 2])
        table = sb("table", [1, NB * 2], I32)
        ks_loaded = (S.ks_loaded0, S.ks_loaded1, S.ks_loaded2, S.ks_loaded3)
        state_loaded = (S.state_loaded0, S.state_loaded1, S.state_loaded2, S.state_loaded3)
        state_stored = (S.state_stored0, S.state_stored1, S.state_stored2, S.state_stored3)
        pages_loaded = (S.pages_loaded0, S.pages_loaded1)

        setup = ExitStack()
        x_nat = sb("x_nat", [P, TT, D], scope=setup)
        mem_nat = sb("mem_nat", [P, 2, D], scope=setup)
        mem_t = sb("mem_t", [P, KD, M], scope=setup)
        mem_g = sb("mem_g", [P, KD, M], scope=setup)
        mem_hi = [sb(f"mem_hi{l}", [P, KD, M], F32R, scope=setup) for l in range(2)]
        mem_lo = [sb(f"mem_lo{l}", [P, KD, M], F32R, scope=setup) for l in range(2)]
        vec_rows = sb("vec_rows", [75, P], scope=setup)
        cw_rows = sb("cw_rows", [80, DH], scope=setup)
        pick = sb("pick", [96, HB, NS], scope=setup)
        rep = sb("rep", [HB, 96], scope=setup)
        mk_nat, mk_sq = (x_nat[:, 0, h * 512:(h + 1) * 512].rearrange("p (m n) -> p m n", m=2) for h in range(2))
        mk_out = [x_nat[:, 1, l * 512:(l + 1) * 512].rearrange("p (m n) -> p m n", m=2) for l in range(2)]
        setup.close()

        ffn = ExitStack()
        h_hi = sb("h_hi", [P, max(FF_PARTS), TOK], F32R, scope=ffn)
        h_lo = sb("h_lo", [P, max(FF_PARTS), TOK], F32R, scope=ffn)
        sg = [sb(f"sg{j}", [P, TOK], scope=ffn) for j in range(2)]
        h_raw = [sb(f"h_raw{j}", [P, TOK], scope=ffn) for j in range(2)]
        ffn.close()
        NC = 3

        mla = ExitStack()
        rows_t = sb("rows_t", [P, TOK + NSA], scope=mla)
        tails = sumsq[0:DH, 0:16 * 27].rearrange("p (k t) -> p k t", k=16)
        carry_all = sqt[0][0:DH, 0:HA * NSA].rearrange("p (h n) -> p h n", h=HA)
        hist = sqt[1][0:DH, 0:16 * 24].rearrange("p (k t) -> p k t", k=16)
        decay_b = sb("decay_b", [NB, HA], scope=mla)
        n_t = sb("n_t", [DH, 2, NB * HA], scope=mla)
        gate_bias = sb("gate_bias", [36, 1], scope=mla)
        m0_rows = sb("m0_rows", [HA, NB], scope=mla)
        w_end_b = sb("w_end_b", [NSA, NB], scope=mla)
        v_nat = sb("v_nat", [P, TT, HA, DA + 1], scope=mla)
        o_nat = sb("o_nat", [P, TT, HA, DA], scope=mla)
        mla_qk = ExitStack()
        qk = sb("qk", [DH, 16, TOK], scope=mla_qk)
        mla_cb = ExitStack()
        cb = [sb(f"cb{j}", [DH, 2, 3 + NPR + NB * 11], scope=mla_cb) for j in range(2)]
        mla_cb.close()
        mla_c = ExitStack()
        carried = sb("carried", [DH, NC, 2, DA], scope=mla_c)
        turned = sb("turned", [DH, 2, 2, DA + 1], scope=mla_c)
        cols = sb("cols", [P, TT, 68], scope=mla_c)
        mla_c.close()
        mla_qk.close()
        hist_nat = qk[0:24, :, :].rearrange("p k n -> p (k n)")[:, 0:1536]
        n_nat = qk[0:32, :, :].rearrange("p k n -> p (k n)")[:, 1536:1728]
        keep_rows, cut_rows = tmp
        o_flat = o_nat[:, :, :, :].rearrange("p t h d -> p t (h d)")

        def mem_scope(scope, l):
            return MemoryBuffers(
                normed=2 + 8 * l,
                qn=sb(f"qn{l}", [P, 2, TOK], scope=scope), e=sb(f"ma_e{l}", [P, HM, M], scope=scope),
                pt=sb(f"ma_pt{l}", [P, 8, P], scope=scope), qz=sb(f"ma_qz{l}", [P, 2, NB, 32], scope=scope),
                ks=sb(f"ma_ks{l}", [P, 4, 2, M], scope=scope), vs=sb(f"ma_vs{l}", [P, NB, 2, M], scope=scope),
                kt=sb(f"ma_kt{l}", [P, 2, 2, M], scope=scope))

        ma_scope = ExitStack()
        MA = mem_scope(ma_scope, 0)
        ma_scope.close()
        mla.close()

        kvs = ExitStack()
        kn = sb("kn", [P, TT, D_MAIN], scope=kvs)
        vn = sb("vn", [P, TT, D_MAIN], scope=kvs)
        ksq = sb("ksq", [P, TT, 256], scope=kvs)
        kvs.close()
        kts = ExitStack()
        sb("below_kt", [P, 16512], scope=kts)
        kt_b = sb("kt_b", [P, 6, TOK], scope=kts)
        kts.close()

        mb = ExitStack()
        qb_t = sb("qb_t", [P, 6, TOK], scope=mb)
        mb_mem = ExitStack()
        MB = mem_scope(mb_mem, 1)
        mb_mem.close()
        mb_p = ExitStack()
        vp = sb("vp", [P, 4, D_MAIN], scope=mb_p)
        take = [sb(f"take{j}", [P, 1280], scope=mb_p) for j in range(2)]
        keep = [sb(f"keep{j}", [P, 1280], scope=mb_p) for j in range(2)]
        rest = sb("rest", [P, 1280], scope=mb_p)
        a_t = sb("a_t", [P, 1280], scope=mb_p)
        mb_p.close()
        mb_s = ExitStack()
        kpg = sb("kpg", [P, 2, 2, D_MAIN], scope=mb_s)
        vpg = sb("vpg", [P, 2, 2, D_MAIN], scope=mb_s)
        vnew = sb("vnew", [NS, 2, D_MAIN], scope=mb_s)
        kpt = sb("kpt", [P, 6, PAST], scope=mb_s)
        qzb = [sb(f"qzb{j}", [P, 680], scope=mb_s) for j in range(2)]
        takes, keeps, rests = (sb(n, [96, PAST + NS], scope=mb_s) for n in ("takes", "keeps", "rests"))
        a_ts = sb("a_ts", [P, 288], scope=mb_s)
        mb_s.close()
        mb.close()

        y_scope = ExitStack()
        y_nat = sb("y_nat", [P, TT, D], scope=y_scope)
        y_scope.close()

        def weights(j, shape, cols=None):
            k, n = shape
            return [w[j][:, 0:k * n].rearrange("p (k n) -> p k n", k=k) for w in (whi, wlo)]

        def load(sp, n, j, src, dst):
            if not isinstance(n, int) or n >= 2:
                sp.wait_ge(S.lo_ready, n - 1)
            half = dst.shape[1] // 2
            for part in (slice(0, half), slice(half, 2 * half)):
                sp.dma_start(dst[:, part, :], src[:, part, :]).then_inc(raw_loaded[j], 16)

        def split_hi(act, n, j):
            if isinstance(n, int) and n >= N_TILES:
                return
            act.wait_ge(raw_loaded[j], (n - j) * 16 + 32)
            if not isinstance(n, int) or n >= 2:
                act.wait_ge(S.tile_done, n - 1)
            act.activation(whi[j][:, :], raw[j][:, :], ACT.Copy).then_inc(S.hi_ready, 1)

        def split_lo(dve, n, j):
            if isinstance(n, int) and n >= N_TILES:
                return
            dve.wait_ge(S.hi_ready, n + 1)
            dve.tensor_tensor(wlo[j][:, :], raw[j][:, :], whi[j][:, :].bitcast(F32), ALU.subtract) \
                .then_inc(S.lo_ready, 1)
            dve.wait_ge(S.lo_ready, n + 1)

        def start_tile(pe, n, j):
            pe.wait_ge(S.lo_ready, n + 1)
            if not isinstance(n, int) or n >= 2:
                pe.wait_ge(region_free[j], (n - j) // 2)

        def product(pe, n, j, w_hi, w_lo, a_hi, a_lo, chunks, outs, width, ready=None):
            start_tile(pe, n, j)
            last = None
            for k in range(chunks):
                if ready is not None and k < ready[2]:
                    pe.wait_ge(ready[0], ready[1] + k + 1)
                for m in range(outs):
                    cols = slice(m * width, (m + 1) * width)
                    for step, (w, a) in enumerate(((w_hi, a_hi), (w_hi, a_lo), (w_lo, a_hi))):
                        for h in range(2):
                            last = pe.matmul(psum[0:width, 4 * j + 2 * m + h, 0:HALF], w[:, k, cols],
                                             a[:, k, h * HALF:(h + 1) * HALF],
                                             start=(k == 0 and step == 0), stop=(k == chunks - 1 and step == 2))
            last.then_inc(S.tile_done, 1)

        def token_tiles():
            return [(t, t * P, P if t < 4 else NSA) for t in range(TT)]

        def natural_product(pe, n, j, w_hi, w_lo, width):
            start_tile(pe, n, j)
            last = None
            for t, at, rows in token_tiles():
                out = region(j)[0:rows, t // 2, (t % 2) * 256:(t % 2) * 256 + width]
                for k in range(KD):
                    for step, (w, a) in enumerate(((w_hi, act_hi), (w_hi, act_lo), (w_lo, act_hi))):
                        last = pe.matmul(out, a[:, k, at:at + rows], w[:, k, :],
                                         start=(k == 0 and step == 0), stop=(k == KD - 1 and step == 2))
            last.then_inc(S.tile_done, 1)

        def natural_view(j, width):
            return flat[:, 2048 * j:2048 * j + 5 * 256].rearrange("p (t n) -> p t n", n=256)[:, :, 0:width]


        def setup_sp(sp):
            sp.dma_start(vec_rows[0:16, :], I["g_ffn1"].rearrange("l (c p) -> (l c) p", p=P)).then_inc(S.inputs_loaded, 16)
            sp.dma_start(vec_rows[16:32, :], I["g_mix"].rearrange("l (c p) -> (l c) p", p=P)).then_inc(S.inputs_loaded, 16)
            sp.dma_start(vec_rows[32:40, :], I["g_kv"].rearrange("(c p) -> c p", p=P)).then_inc(S.inputs_loaded, 16)
            sp.dma_start(vec_rows[40:56, :], I["g_mem"].rearrange("l (c p) -> (l c) p", p=P)).then_inc(S.inputs_loaded, 16)
            sp.dma_start(vec_rows[56:72, :], I["g_ffn2"].rearrange("l (c p) -> (l c) p", p=P)).then_inc(S.inputs_loaded, 16)
            for r in range(2):
                half = slice(r * 64, r * 64 + 64)
                sp.dma_start(vec_rows[72:74, half], I["g_q_mem"]).then_inc(S.inputs_loaded, 16)
                sp.dma_start(vec_rows[74:75, half], I["g_q_b"]).then_inc(S.inputs_loaded, 16)
            sp.dma_start(cw_rows[0:64, :], I["conv_w_a"].rearrange("a j (c p) -> (a j c) p", p=DH)).then_inc(S.inputs_loaded, 16)
            sp.dma_start(cw_rows[64:80, :], I["conv_b_a"].rearrange("a (c p) -> (a c) p", p=DH)).then_inc(S.inputs_loaded, 16)
            sp.dma_start(mem_nat[:, :, :], I["mem_prompt"].rearrange("a (t p) d -> p (a t) d", p=P)).then_inc(S.inputs_loaded, 16)
            sp.dma_start(x_nat[:, 0:4, :], I["x_prompt"].rearrange("a (t p) d -> p (a t) d", p=P)).then_inc(S.inputs_loaded, 16)
            sp.dma_start(x_nat[0:NSA, 4, :], I["x_sample"].rearrange("b t d -> (b t) d")).then_inc(S.inputs_loaded, 16)
            sp.dma_start(gk_mem[:, :, :], I["g_k_mem"].partition_broadcast(P)).then_inc(S.inputs_loaded, 16)
            sp.dma_start(gk_b[:, :], I["g_k_b"].partition_broadcast(P)).then_inc(S.inputs_loaded, 16)
            sp.dma_start(b_all[:, :], I["b_sb"][0].partition_broadcast(P)).then_inc(S.inputs_loaded, 16)
            sp.dma_start(b_col[:, :], I["b_sb"].rearrange("a h -> h a")).then_inc(S.inputs_loaded, 16)
        SETUP_LOADS = 16 * 18

        def setup_pool(pool, c):
            pool.memset(ones[:, :], 1.0)
            pool.memset(eps[:, :], EPS)
            pool.memset(zero[:, :], 0.0)
            pool.memset(w_pad[:, :], 0.0)
            pool.memset(ones_heads[:, :], 0.0)
            for t, v in ((ident, 0.0), (causal, 0.0), (causal_b, 0.0), (own, 1.0), (before, 1.0), (not_before, 0.0), (rep, 0.0)):
                pool.memset(t[:, :], v)
            pool.memset(pick[:, :, :], 1.0).then_inc(S.pool_step, 1)
            pool.wait_ge(S.pool_step, c("pool_step"))
            for r in range(2):
                pool.memset(ones_heads[64 * r:64 * r + 64, 64 * r:64 * r + 64], 1.0).then_inc(S.pool_step, 1)
                pool.wait_ge(S.pool_step, c("pool_step"))

            def select(t, op, fill, base, pattern, row):
                return pool.affine_select(out=t, in_=t, compare_op=op, fill=fill, base=base, pattern=pattern,
                                          channel_multiplier=row)
            seq = causal_b[:, :].rearrange("p (b t) -> p b t", b=NB)
            select(causal[:, :], ALU.is_ge, NEG, 0, [[1, P]], -1)
            select(seq, ALU.is_ge, NEG, 0, [[8, NB], [1, NS]], -1)
            select(own[:, :], ALU.is_ge, 0.0, 0, [[-8, NB]], 1)
            select(before[:, :], ALU.is_ge, 0.0, -1, [[-1, P]], 1)
            select(not_before[:, :], ALU.is_ge, 1.0, -1, [[-1, P]], 1)
            select(pick[:, :, :], ALU.is_ge, 0.0, -1, [[-8, HB], [-1, NS]], 1)
            select(rep[:, :].rearrange("p (h t) -> p h t", t=NS), ALU.not_equal, 1.0, 0, [[-1, HB], [0, NS]], 1)
            select(ident[:, :], ALU.not_equal, 1.0, 0, [[-1, P]], 1).then_inc(S.pool_step, 1)
            pool.wait_ge(S.pool_step, c("pool_step"))
            select(seq, ALU.is_ge, NEG, 0, [[-8, NB], [0, NS]], 1)
            select(own[:, :], ALU.is_ge, 0.0, 7, [[8, NB]], -1)
            select(pick[:, :, :], ALU.is_ge, 0.0, 7, [[8, HB], [0, NS]], -1).then_inc(S.consts_ready, 1)

        def setup_pe(pe):
            pe.wait_ge(S.consts_ready, 1)
            pe.wait_ge(S.inputs_loaded, SETUP_LOADS)
            pe.transpose(psum[0:P, 0, 0:75], vec_rows[:, :], ident[0:75, 0:75])
            pe.matmul(psum[0:96, 1, 128:129], rep[:, :], b_col[:, :], start=True, stop=True)
            pe.transpose(psum[0:DH, 1, 0:80], cw_rows[:, :], ident[0:80, 0:80]).then_inc(S.setup_turned, 1)
            groups = [(mem_nat[:, t, :], P) for t in range(2)]
            groups += [(x_nat[0:rows, t, :], rows) for t, _, rows in token_tiles()]
            for g, (src, rows) in enumerate(groups, 1):
                if g >= 4:
                    pe.wait_ge(S.setup_copied, g - 3)
                for k in range(KD):
                    at = 1024 * (g % 4) + k * rows if rows == P else 1024 * (g % 4) + k * rows
                    last = pe.transpose(flat[:, at:at + rows], src[:, k * P:(k + 1) * P], ident[0:rows, 0:rows])
                last.then_inc(S.setup_turned, 1)

        def setup_dve(dve, c):
            dve.wait_ge(S.setup_turned, 1)
            dve.wait_ge(S.inputs_loaded, SETUP_LOADS)
            dve.tensor_copy(vec_t[:, :], psum[:, 0, 0:75])
            dve.tensor_scalar(b_rows[:, 0:1], psum[0:96, 1, 128:129], 1.0, None, ALU.mult)
            dve.tensor_scalar(b_rows[:, 1:2], psum[0:96, 1, 128:129], -1.0, None, ALU.mult)
            dve.tensor_scalar(b_neg[:, :], b_all[:, :], -1.0, None, ALU.mult)
            dve.tensor_reduce(own_keys[:, 0, :], pick[:, :, :].rearrange("p h j -> p j h"), AX, ALU.add).then_inc(S.dve_step, 1)
            dve.wait_ge(S.dve_step, c("dve_step"))
            dve.tensor_scalar(own_keys[:, 1, :], own_keys[:, 0, :], -1.0, 1.0, ALU.mult, ALU.add)
            dve.tensor_copy(cw_t[:, :], psum[0:DH, 1, 0:80]).then_inc(S.setup_copied, 1)
            for t in range(2):
                g = 1 + t
                dve.wait_ge(S.setup_turned, g + 1)
                dve.tensor_copy(mem_t[:, :, t * P:(t + 1) * P],
                                flat[:, 1024 * g:1024 * g + 1024].rearrange("p (k n) -> p k n", k=KD)) \
                    .then_inc(S.setup_copied, 1)
            dve.wait_ge(S.mem_rms_ready, 1)
            dve.reciprocal(mrinv[:, :], mrinv[:, :]).then_inc(S.dve_step, 1)
            dve.wait_ge(S.dve_step, c("dve_step"))
            dve.wait_ge(S.setup_copied, 3)
            for l in range(2):
                if l:
                    dve.wait_ge(S.mem_split, 1)
                dve.tensor_tensor(mem_g[:, :, :], mem_t[:, :, :],
                                  gain("mem", l).unsqueeze(2).broadcast_to([P, KD, M]), ALU.mult) \
                    .then_inc(S.mem_scaled, 1)
                dve.wait_ge(S.mem_hi, l + 1)
                dve.tensor_tensor(mem_lo[l][:, :, :], mem_g[:, :, :], mem_hi[l][:, :, :].bitcast(F32), ALU.subtract) \
                    .then_inc(S.mem_split, 1)
            for t, at, rows in token_tiles():
                g = 3 + t
                dve.wait_ge(S.setup_turned, g + 1)
                b = 1024 * (g % 4)
                dve.tensor_copy(x_t[:, :, at:at + rows],
                                flat[:, b:b + KD * rows].rearrange("p (k n) -> p k n", k=KD)) \
                    .then_inc(S.setup_copied, 1)
            sum_squares_start(dve, 0)
            for k in range(KD):
                sum_square(dve, k % 2, 0, k)

        def setup_act(act):
            act.wait_ge(S.inputs_loaded, SETUP_LOADS)
            for t in range(2):
                act.activation(mem_g[:, 0:4, :].rearrange("p k n -> p (k n)"), mem_nat[:, t, :], ACT.Square,
                               accum_out=mrinv[:, t:t + 1]).then_inc(S.mem_squared, 1)
                act.wait_ge(S.mem_squared, t + 1)
            act.wait_ge(S.consts_ready, 1)
            act.activation(mrinv[:, :], mrinv[:, :], ACT.Sqrt, scale=1.0 / D, bias=eps[:, :]).then_inc(S.mem_rms_ready, 1)
            for l in range(2):
                act.wait_ge(S.mem_scaled, l + 1)
                act.activation(mem_hi[l][:, :, :], mem_g[:, :, :], ACT.Copy).then_inc(S.mem_hi, 1)
            act.wait_ge(S.setup_copied, 8)
            for k in range(KD):
                square(act, k % 2, k, 0, k)

        def sum_squares_start(dve, g):
            if g:
                dve.wait_ge(S.sumsq_ready, g)
            dve.memset(sumsq[:, :], 0.0).then_inc(S.sum_done, 1)

        def square(act, slot, chunk, g, nth):
            if isinstance(nth, int) and nth >= 2:
                act.wait_ge(S.sum_done, 9 * g + nth)
            act.activation(sqt[slot][:, :], x_t[:, chunk, :], ACT.Square).then_inc(S.sq_ready, 1)

        def sum_square(dve, slot, g, nth):
            dve.wait_ge(S.sq_ready, 8 * g + nth + 1)
            dve.wait_ge(S.sum_done, 9 * g + nth + 1)
            dve.tensor_tensor(sumsq[:, :], sumsq[:, :], sqt[slot][:, :], ALU.add).then_inc(S.sum_done, 1)

        def halves(ap):
            return ap.rearrange("p (h n) -> p h n", h=2)

        def norm_pe(pe, g, n_next):
            pe.wait_ge(S.sum_done, 9 * g + 9)
            if n_next:
                pe.wait_ge(S.region_free0, n_next // 2)
            for h in range(2):
                last = pe.matmul(psum[:, h, 0:HALF], ones[:, :], sumsq[:, h * HALF:(h + 1) * HALF], start=True, stop=True)
            last.then_inc(S.sumsq_ready, 1)

        def norm_act(act, g, nth, again):
            if not again:
                act.wait_ge(S.sumsq_ready, g + 1)
                act.activation(halves(rinv[:, :]), psum[:, 0:2, 0:HALF], ACT.Sqrt, scale=1.0 / D, bias=eps[:, :]) \
                    .then_inc(S.rms_ready, 1)
            for k in range(KD):
                act.wait_ge(S.xn_ready, 8 * nth + k + 1)
                act.activation(act_hi[:, k, :], tmp[k % 2][:, :], ACT.Copy).then_inc(S.nh_ready, 1)

        def norm_dve(dve, g, nth, again, gains, c):
            if not again:
                dve.wait_ge(S.rms_ready, g + 1)
                dve.reciprocal(rinv[:, :], rinv[:, :]).then_inc(S.dve_step, 1)
                dve.wait_ge(S.dve_step, c("dve_step"))

            def lo(k):
                dve.wait_ge(S.nh_ready, 8 * nth + k + 1)
                dve.tensor_tensor(act_lo[:, k, :], tmp[k % 2][:, :], act_hi[:, k, :].bitcast(F32), ALU.subtract) \
                    .then_inc(S.nl_ready, 1)
            for k in range(KD):
                if k >= 2:
                    lo(k - 2)
                    dve.wait_ge(S.nl_ready, 8 * nth + k - 1)
                dve.scalar_tensor_tensor(tmp[k % 2][:, :], x_t[:, k, :], gains[:, k:k + 1], rinv[:, :],
                                         ALU.mult, ALU.mult).then_inc(S.xn_ready, 1)
            lo(KD - 2)
            lo(KD - 1)

        def mem_sp(sp):
            for n in range(4):
                src = I["w_mem_kv"][n // 2].rearrange("(k p) (s n) -> p k s n", p=P, s=2)[:, :, n % 2, :]
                load(sp, n, n % 2, src, raw[n % 2][:, :].rearrange("p (k n) -> p k n", k=KD))

        def mem_pe(pe):
            def turn_keys(l):
                pe.wait_ge(S.mk_ready, l + 1)
                for m in range(2):
                    for pair in range(2):
                        last = pe.transpose(psum[:, 2, (2 * pair + m) * P:(2 * pair + m + 1) * P],
                                            mk_out[l][:, m, pair * P:(pair + 1) * P], ident[:, :])
                last.then_inc(S.mkt_ready, 1)

            for n in range(4):
                j, l = n % 2, n // 2
                if n % 2 == 0:
                    pe.wait_ge(S.mem_split, l + 1)
                if n == 0:
                    pe.wait_ge(S.setup_copied, 8)
                start_tile(pe, n, j)
                w_hi, w_lo = weights(j, (KD, M))
                for m in range(2):
                    for k in range(KD):
                        for step, (w, a) in enumerate(((w_hi, mem_hi), (w_hi, mem_lo), (w_lo, mem_hi))):
                            last = pe.matmul(psum[:, 4 * j + m, 0:M], a[l][:, k, m * P:(m + 1) * P], w[:, k, :],
                                             start=(k == 0 and step == 0), stop=(k == KD - 1 and step == 2))
                last.then_inc(S.tile_done, 1)
                if n == 2:
                    turn_keys(0)
            pe.wait_ge(S.mkt_copied, 1)
            turn_keys(1)

        def mem_act(act):
            for n in range(4):
                split_hi(act, n + 1, (n + 1) % 2)
                if n % 2 == 0:
                    l = n // 2
                    act.wait_ge(region_free[0], l + 1)
                    act.activation(mk_sq, mk_nat, ACT.Square).then_inc(S.mk_sq, 1)
                    act.wait_ge(S.mk_ms, l + 1)
                    act.activation(small[:, 0:8], small[:, 0:8], ACT.Sqrt, scale=1.0 / DM, bias=eps[:, :]).then_inc(S.mk_rms, 1)

        def mem_dve(dve, c):
            def copy_keys(l):
                dve.wait_ge(S.mkt_ready, l + 1)
                dve.tensor_copy(mk_t[l][:, :, :].rearrange("p a m -> p (a m)"), psum[:, 2, :]).then_inc(S.mkt_copied, 1)

            def step(ins):
                ins.then_inc(S.dve_step, 1)
                dve.wait_ge(S.dve_step, c("dve_step"))

            for n in range(4):
                j, l = n % 2, n // 2
                split_lo(dve, n + 1, (n + 1) % 2)
                dve.wait_ge(S.tile_done, n + 1)
                scale = mrinv[:, :].unsqueeze(2).broadcast_to([P, 2, M])
                if n % 2:
                    dve.tensor_tensor(mv[l][:, :, :], psum[:, 4 * j:4 * j + 2, 0:M], scale, ALU.mult).then_inc(region_free[j], 1)
                    continue
                dve.tensor_tensor(mk_nat, psum[:, 4 * j:4 * j + 2, 0:M], scale, ALU.mult) \
                    .then_inc(region_free[j], 1)
                dve.wait_ge(region_free[j], l + 1)
                nat = mk_nat.rearrange("p m (h d) -> p (m h) d", d=DM)
                out = mk_out[l].rearrange("p m (h d) -> p (m h) d", d=DM)
                dve.wait_ge(S.mk_sq, l + 1)
                dve.tensor_reduce(small[:, 0:8], mk_sq.rearrange("p m (h d) -> p (m h) d", d=DM), AX, ALU.add) \
                    .then_inc(S.mk_ms, 1)
                dve.wait_ge(S.mk_rms, l + 1)
                step(dve.reciprocal(small[:, 0:8], small[:, 0:8]))
                step(dve.tensor_tensor(out, nat, small[:, 0:8].unsqueeze(2).broadcast_to([P, 8, DM]), ALU.mult))
                dve.tensor_tensor(out, out, gk_mem[:, l, :].unsqueeze(1).broadcast_to([P, 8, DM]), ALU.mult) \
                    .then_inc(S.mk_ready, 1)
                if l:
                    copy_keys(0)
            copy_keys(1)

        def mem_pool(pool, c):
            for l in range(2):
                pool.wait_ge(S.mk_ready, l + 1)
                pool.dma_start(O["mem_k_prompt"][l, 0].rearrange("(m p) h d -> p m (h d)", p=P), mk_out[l]).then_inc(S.stored, 16)
                pool.wait_ge(S.region_free1, l + 1)
                pool.dma_start(O["mem_v_prompt"][l, 0].rearrange("(m p) h d -> p m (h d)", p=P), mv[l][:, :, :]).then_inc(S.stored, 16)

        def ffn_weights(q):
            l = q // 2
            return ((I["w_ffn1_up"], I["w_ffn1_down"]), (I["w_ffn2_up"], I["w_ffn2_down"]))[q % 2][0][l], \
                ((I["w_ffn1_up"], I["w_ffn1_down"]), (I["w_ffn2_up"], I["w_ffn2_down"]))[q % 2][1][l]

        def ffn_parts(q):
            n, first = BASE_FFN[q], 0
            for part, chunks in enumerate(FF_PARTS):
                yield part, n, n + chunks, chunks, first, q * sum(FF_PARTS) + first
                n += chunks + KD
                first += chunks

        def ffn_sp(sp, q):
            up, down = ffn_weights(q)
            up_view = up.rearrange("(k p) (s n) -> p k s n", p=P, s=2)
            for part, n_up, n_down, chunks, first, _ in ffn_parts(q):
                with sp.Fori(0, chunks // 2) as i:
                    for j in range(2):
                        sp.wait_ge(S.lo_ready, n_up + 2 * i + (j - 1))
                        dst = raw[j][:, :].rearrange("p (k s n) -> p k s n", k=KD, s=2)
                        for s in range(2):
                            sp.dma_start(dst[:, :, s, :], up_view[:, :, s, bass.ds((2 * i + (first + j)) * P, P)]) \
                                .then_inc(raw_loaded[j], 16)
                down_view = down.rearrange("(k p) n -> p k n", p=P)[:, first:first + chunks, :]
                with sp.Fori(0, KD // 2) as i:
                    for j in range(2):
                        load(sp, n_down + 2 * i + j, j, down_view[:, :, bass.ds((2 * i + j) * P, P)],
                             raw[j][:, 0:chunks * P].rearrange("p (k n) -> p k n", k=chunks))

        def ffn_pe(pe, q, nth):
            for part, n_up, n_down, chunks, first, ups in ffn_parts(q):
                with pe.Fori(0, chunks // 2) as i:
                    for j in range(2):
                        w_hi, w_lo = weights(j, (KD, 256))
                        product(pe, n_up + 2 * i + j, j, w_hi, w_lo, act_hi, act_lo, KD, 2, P,
                                ready=(S.nl_ready, 8 * nth, KD))
                with pe.Fori(0, KD // 2) as i:
                    for j in range(2):
                        w_hi, w_lo = weights(j, (chunks, P))
                        product(pe, n_down + 2 * i + j, j, w_hi, w_lo, h_hi, h_lo, chunks, 1, P,
                                ready=(S.hl_ready, ups, chunks))

        def ffn_act(act, q, g):
            for part, n_up, n_down, chunks, first, ups in ffn_parts(q):
                if part == 0 and q % 2 == 0:
                    act.wait_ge(*((S.stored, 64), (S.kv_stored, 64))[q // 2])
                with act.Fori(0, chunks // 2) as i:
                    for j in range(2):
                        n = n_up + 2 * i + j
                        split_hi(act, n + 1, 1 - j)
                        act.wait_ge(S.tile_done, n + 1)
                        act.activation(halves(sg[j][:, :]), region(j)[:, 0:2, 0:HALF], ACT.Silu).then_inc(S.sg_ready, 1)
                        act.wait_ge(region_free[j], n_up // 2 + i + 1)
                        act.activation(h_hi[:, 2 * i + j, :], h_raw[j][:, :], ACT.Copy).then_inc(S.hh_ready, 1)

                def down(i, last=False):
                    for j in range(2):
                        n = n_down + 2 * i + j
                        split_hi(act, n + 1, 1 - j)
                        if part and g is not None:
                            act.wait_ge(region_free[j], n_down // 2 + i + 1)
                            square(act, j, 2 * i + j, g, 2 * i + j)
                if n_down + KD == N_TILES:
                    with act.Fori(0, KD // 2 - 1) as i:
                        down(i)
                    down(KD // 2 - 1)
                else:
                    with act.Fori(0, KD // 2) as i:
                        down(i)

        def ffn_dve(dve, q, g):
            for part, n_up, n_down, chunks, first, ups in ffn_parts(q):
                if part == 0 and q % 2 == 0:
                    dve.wait_ge(*((S.stored, 64), (S.kv_stored, 64))[q // 2])
                with dve.Fori(0, chunks // 2) as i:
                    for j in range(2):
                        n = n_up + 2 * i + j
                        split_lo(dve, n + 1, 1 - j)
                        dve.wait_ge(S.sg_ready, 2 * i + (ups + j + 1))
                        dve.tensor_tensor(halves(h_raw[j][:, :]), halves(sg[j][:, :]), region(j)[:, 2:4, 0:HALF], ALU.mult) \
                            .then_inc(region_free[j], 1)
                        dve.wait_ge(S.hh_ready, 2 * i + (ups + j + 1))
                        dve.tensor_tensor(h_lo[:, 2 * i + j, :], h_raw[j][:, :], h_hi[:, 2 * i + j, :].bitcast(F32),
                                          ALU.subtract).then_inc(S.hl_ready, 1)
                if part and g is not None:
                    sum_squares_start(dve, g)

                def down(i):
                    for j in range(2):
                        n = n_down + 2 * i + j
                        split_lo(dve, n + 1, 1 - j)
                        dve.wait_ge(S.tile_done, n + 1)
                        x = halves(x_t[:, 2 * i + j, :]) if isinstance(i, int) else \
                            x_t[:, 2 * i + j, :].rearrange("p (h n) -> p h n", h=2)
                        dve.scalar_tensor_tensor(x, region(j)[:, 0:2, 0:HALF], 0.5, x, ALU.mult, ALU.add) \
                            .then_inc(region_free[j], 1)
                        if part and g is not None:
                            sum_square(dve, j, g, 2 * i + j)
                if n_down + KD == N_TILES:
                    with dve.Fori(0, KD // 2 - 1) as i:
                        down(i)
                    down(KD // 2 - 1)
                else:
                    with dve.Fori(0, KD // 2) as i:
                        down(i)

        def out_sp(sp, base, l):
            view = I["w_out"][l].rearrange("(k p) n -> p k n", p=P)
            for t in range(4):
                j = t % 2
                load(sp, base + t, j, view[:, :, t * 256:(t + 1) * 256], raw[j][:, :].rearrange("p (k n) -> p k n", k=KD))

        def out_pe(pe, base):
            for t in range(4):
                w_hi, w_lo = weights(t % 2, (KD, 256))
                product(pe, base + t, t % 2, w_hi, w_lo, act_hi, act_lo, KD, 2, P)

        def out_act(act, base, g):
            for t in range(4):
                n, j = base + t, t % 2
                split_hi(act, n + 1, 1 - j)
                act.wait_ge(region_free[j], n // 2 + 1)
                for m in range(2):
                    square(act, m, 2 * t + m, g, 2 * t + m)

        def out_dve(dve, base, g):
            sum_squares_start(dve, g)
            for t in range(4):
                n, j = base + t, t % 2
                split_lo(dve, n + 1, 1 - j)
                dve.wait_ge(S.tile_done, n + 1)
                for m in range(2):
                    x = halves(x_t[:, 2 * t + m, :])
                    ins = dve.scalar_tensor_tensor(x, region(j)[:, 2 * m:2 * m + 2, 0:HALF], 1.0, x, ALU.mult, ALU.add)
                ins.then_inc(region_free[j], 1)
                for m in range(2):
                    sum_square(dve, m, g, 2 * t + m)

        def end_pe(pe):
            for t, at, rows in token_tiles():
                b = 2 * (t % 4)
                if t == 0:
                    pe.wait_ge(S.region_free0, N_TILES // 2)
                    pe.wait_ge(S.region_free1, N_TILES // 2)
                if t == 4:
                    pe.wait_ge(S.y_copied, 1)
                for k in range(KD):
                    last = pe.transpose(psum[0:rows, b + k // 4, (k % 4) * P:(k % 4 + 1) * P], x_t[:, k, at:at + rows], ident[:, :])
                last.then_inc(S.y_turned, 1)

        def end_dve(dve):
            for t, at, rows in token_tiles():
                b = 2 * (t % 4)
                dve.wait_ge(S.y_turned, t + 1)
                dve.tensor_copy(y_nat[0:rows, t, :], psum[0:rows, b:b + 2, :].rearrange("p b n -> p (b n)")).then_inc(S.y_copied, 1)

        def end_sp(sp):
            view = O["y_prompt"].rearrange("a (t p) d -> t p (a d)", p=P)
            for t, at, rows in token_tiles():
                sp.wait_ge(S.y_copied, t + 1)
                dst = view[t] if t < 4 else O["y_sample"].rearrange("b t d -> (b t) d")
                sp.dma_start(dst, y_nat[0:rows, t, :]).then_inc(S.y_stored, 16)
            sp.wait_ge(S.y_stored, 16 * TT)

        def ina_sp(sp):
            view = I["w_in_a"][0].rearrange("(k p) n -> p k n", p=P)
            for t in range(INA_TILES):
                n, j = BASE_INA + t, t % 2
                if t == 0:
                    sp.wait_ge(S.lo_ready, n - 1)
                    dst = raw[j][:, 0:KD * 64].rearrange("p (k n) -> p k n", k=KD)
                    for r in range(2):
                        sp.dma_start(dst[:, :, 32 * r:32 * r + 4], view[:, :, 4 * D_MAIN + 4 * r:4 * D_MAIN + 4 * r + 4]) \
                            .then_inc(raw_loaded[j], 16)
                elif t < INA_TILES - 1:
                    load(sp, n, j, view[:, :, (t - 1) * DA:t * DA], raw[j][:, 0:KD * DA].rearrange("p (k n) -> p k n", k=KD))
                else:
                    load(sp, n, j, view[:, :, 4 * D_MAIN + 8:4 * D_MAIN + 8 + 256], raw[j][:, :].rearrange("p (k n) -> p k n", k=KD))

        def ina_pe(pe, nth):
            for t in range(INA_TILES):
                n, j = BASE_INA + t, t % 2
                if t == 0:
                    w_hi, w_lo = weights(j, (KD, 64))
                    product(pe, n, j, w_hi[:, :, 0:36], w_lo[:, :, 0:36], act_hi, act_lo, KD, 1, 36, ready=(S.nl_ready, 8 * nth, KD))
                elif t <= 8:
                    if t == 1:
                        pe.wait_ge(S.hist_ready, 1)
                    w_hi, w_lo = weights(j, (KD, DA))
                    product(pe, n, j, w_hi, w_lo, act_hi, act_lo, KD, 2, DH)
                elif t <= 16:
                    w_hi, w_lo = weights(j, (KD, DA))
                    natural_product(pe, n, j, w_hi, w_lo, DA)
                else:
                    w_hi, w_lo = weights(j, (KD, 256))
                    product(pe, n, j, w_hi, w_lo, act_hi, act_lo, KD, 2, P)

        def ina_act(act, c):
            for t in range(INA_TILES):
                n, j = BASE_INA + t, t % 2
                free = n // 2 + 1
                split_hi(act, n + 1, 1 - j)
                if t == 0:
                    act.wait_ge(S.gate_abs, 1)
                    act.activation(sqt[1][32:36, :], sqt[1][32:36, :], ACT.Exp, scale=-1.0).then_inc(S.act_step, 1)
                    act.wait_ge(S.act_step, c("act_step"))
                    act.activation(sqt[1][32:36, :], sqt[1][32:36, :], ACT.Ln, bias=ones[32:36, 0:1]).then_inc(S.gate_ln, 1)
                    act.wait_ge(S.gate_m, 1)
                    act.activation(rows_t[64:68, 0:TOK], sqt[0][0:4, :], ACT.Exp, scale=-1.0)
                    act.activation(rows_t[32:36, 0:TOK], sqt[1][0:4, :], ACT.Exp)
                    act.activation(rows_t[96:100, TOK:TOK + NSA], rinv[0:4, 0:NSA], ACT.Exp).then_inc(S.gate_rows, 1)
                elif t <= 8:
                    head = t - 1
                    if t > 2:
                        act.wait_ge(S.conv_ready, head - 1)
                    act.wait_ge(S.tile_done, n + 1)
                    src = region(j)[0:DH, :, 0:HALF].rearrange("p (m h) n -> p m h n", h=2)
                    dst = cb[j]
                    act.activation(dst[:, :, 3:3 + HALF], src[:, :, 0, :], ACT.Copy)
                    act.activation(dst[:, :, 3 + HALF:3 + NPR], src[:, :, 1, 0:NPR - HALF], ACT.Copy)
                    for m in range(2):
                        ins = act.activation(cb_sample(j, m)[:, :, 3:3 + NS],
                                             src[:, m, 1, NPR - HALF:HALF].rearrange("p (b t) -> p b t", b=NB), ACT.Copy)
                    ins.then_inc(region_free[j], 1)
                    act.wait_ge(S.conv_ready, head + 1)
                    for m in range(2):
                        ins = act.activation(qk[:, 2 * head + m, :], tmp[m][0:DH, :], ACT.Silu)
                    ins.then_inc(S.qk_silu, 1)
                else:
                    if t >= 17:
                        break
                    head, is_o = (t - 9) % 4, t >= 13
                    act.wait_ge(S.tile_done, n + 1)
                    src = natural_view(j, DA)
                    if is_o:
                        act.activation(o_nat[:, 0:4, head, :], src[:, 0:4, :], ACT.Sigmoid)
                        act.activation(o_nat[0:NSA, 4, head, :], src[0:NSA, 4, :], ACT.Sigmoid).then_inc(region_free[j], 1)
                    else:
                        act.activation(v_nat[:, 0:4, head, 0:DA], src[:, 0:4, :], ACT.Copy)
                        act.activation(v_nat[0:NSA, 4, head, 0:DA], src[0:NSA, 4, :], ACT.Copy).then_inc(region_free[j], 1)
            act.wait_ge(S.tile_done, n + 1)
            act.activation(qm_a[:, :, :].rearrange("p m (h n) -> p (m h) n", h=2), region(1)[:, :, 0:HALF], ACT.Copy) \
                .then_inc(region_free[1], 1)

        def cb_sample(j, m):
            return cb[j][:, m, 3 + NPR:3 + NPR + NB * 11].rearrange("p (b t) -> p b t", b=NB)

        def ina_dve(dve, c):
            def step(ins):
                ins.then_inc(S.dve_step, 1)
                dve.wait_ge(S.dve_step, c("dve_step"))

            def seg(ap):
                return ap.rearrange("p (b t) -> p b t", b=NB)

            for t in range(INA_TILES):
                n, j = BASE_INA + t, t % 2
                split_lo(dve, n + 1, 1 - j)
                if t == 0:
                    gates, lf, b, am, big = sqt[0], sqt[1], rinv, sqt[1], sumsq
                    dve.wait_ge(S.consts_ready, 2)
                    dve.wait_ge(S.a_loaded, A_LOADS)
                    dve.wait_ge(S.tile_done, n + 1)
                    dve.tensor_scalar(halves(gates[0:36, :]), region(0)[0:36, 0:2, 0:HALF], gate_bias[:, :], None, ALU.add) \
                        .then_inc(region_free[0], 1)
                    dve.wait_ge(region_free[0], n // 2 + 1)
                    dve.scalar_tensor_tensor(lf[32:36, :], gates[32:36, :], -1.0, gates[32:36, :], ALU.mult, ALU.max) \
                        .then_inc(S.gate_abs, 1)
                    dve.wait_ge(S.gate_ln, 1)
                    step(dve.scalar_tensor_tensor(lf[32:36, :], gates[32:36, :], 0.0, lf[32:36, :], ALU.min, ALU.subtract))
                    step(dve.tensor_tensor_scan(b[0:4, :], keep_rows[32:36, :], lf[32:36, :], 0.0, ALU.mult, ALU.add))
                    step(dve.tensor_tensor(rows_t[0:4, 0:TOK], gates[0:4, :], b[0:4, :], ALU.subtract))
                    step(dve.tensor_copy(am[0:4, :], rows_t[0:4, 0:TOK]))
                    step(dve.tensor_tensor(am[0:4, NPR:TOK:NS], am[0:4, NPR:TOK:NS], m0_rows[:, :], ALU.max))
                    step(dve.tensor_tensor_scan(big[0:4, :], cut_rows[0:4, :], am[0:4, :], 0.0, ALU.add, ALU.max))
                    dve.tensor_scalar(rows_t[96:100, 0:TOK], big[0:4, :], -1.0, None, ALU.mult)
                    step(dve.tensor_tensor(gates[0:4, :], b[0:4, :], big[0:4, :], ALU.add))
                    dve.tensor_scalar(am[0:4, 0:NPR], rows_t[0:4, 0:NPR], big[0:4, NPR - 1:NPR], None, ALU.subtract)
                    dve.tensor_tensor(seg(am[0:4, NPR:TOK]), seg(rows_t[0:4, NPR:TOK]),
                                      big[0:4, NPR + NS - 1:TOK:NS].unsqueeze(2).broadcast_to([4, NB, NS]), ALU.subtract)
                    dve.tensor_tensor(seg(b[0:4, 0:NSA]), m0_rows[:, :].unsqueeze(2).broadcast_to([4, NB, NS]),
                                      seg(big[0:4, NPR:TOK]), ALU.subtract).then_inc(S.gate_m, 1)
                    dve.wait_ge(S.gate_rows, 1)
                    hist_dve(dve)
                    dve.wait_ge(S.hist_ready, 1)
                elif t <= 8:
                    head = t - 1
                    for m in range(2):
                        k = 2 * head + m
                        if t <= 2:
                            dve.memset(cb[j][:, m, 0:3], 0.0)
                        dve.tensor_copy(cb_sample(j, m)[:, :, 0:3], hist[:, k, :].rearrange("p (b t) -> p b t", t=3))
                    dve.wait_ge(region_free[j], n // 2 + 1)
                    for m in range(2):
                        k = 2 * head + m
                        dve.tensor_copy(tails[:, k, 0:3], cb[j][:, m, NPR:NPR + 3])
                        step(dve.tensor_copy(tails[:, k, 3:27].rearrange("p (b t) -> p b t", t=3), cb_sample(j, m)[:, :, NS:NS + 3]))
                    if head:
                        dve.wait_ge(S.qk_silu, head)
                    for tap in range(4):
                        for m in range(2):
                            k = 2 * head + m
                            taps, bias = cw_t[:, tap * 16 + k:tap * 16 + k + 1], cw_t[:, 64 + k:65 + k]
                            for dst, src in ((tmp[m][0:DH, 0:NPR], cb[j][:, m, tap:tap + NPR]),
                                             (seg(tmp[m][0:DH, NPR:TOK]), cb_sample(j, m)[:, :, tap:tap + NS])):
                                if tap == 0:
                                    ins = dve.tensor_scalar(dst, src, taps, bias, ALU.mult, ALU.add)
                                else:
                                    ins = dve.scalar_tensor_tensor(dst, src, taps, dst, ALU.mult, ALU.add)
                        if tap < 3:
                            step(ins)
                    ins.then_inc(S.conv_ready, 1)
                    dve.wait_ge(S.qk_silu, head + 1)
                    if head >= 4:
                        dve.tensor_scalar(qk[:, 2 * head:2 * head + 2, :], qk[:, 2 * head:2 * head + 2, :],
                                          float(DA) ** -0.5, None, ALU.mult).then_inc(S.k_scaled, 1)

        A_LOADS = 16 * 5

        def ina_pool(pool, c):
            pool.wait_ge(S.tile_done, BASE_INA)
            def step(ins):
                ins.then_inc(S.pool_step, 1)
                pool.wait_ge(S.pool_step, c("pool_step"))

            step(pool.memset(gate_bias[:, :], 0.0))
            step(pool.memset(rows_t[:, :], 0.0))
            for r in range(2):
                pool.dma_start(gate_bias[32 * r:32 * r + 4, :], I["b_gate_a"][:, 4 * r:4 * r + 4].rearrange("a h -> h a"), allow_slow_non_contiguous=True) \
                    .then_inc(S.a_loaded, 16)
            pool.dma_start(m0_rows[:, :], I["state_m"][0].rearrange("b h -> h b"), allow_slow_non_contiguous=True).then_inc(S.a_loaded, 16)
            pool.dma_start(hist_nat, I["state_conv"][0].rearrange("b t f -> (b t) f")).then_inc(S.a_loaded, 16)
            pool.dma_start(n_nat[:, :], I["state_n"][0].rearrange("b h d -> (b h) d")).then_inc(S.a_loaded, 16)
            pool.wait_ge(S.nl_ready, 16)
            step(pool.memset(keep_rows[32:36, :], 1.0))
            step(pool.memset(cut_rows[0:4, :], 0.0))
            step(pool.memset(v_nat[:, :, :, DA:DA + 1], 1.0))
            step(pool.memset(o_nat[64:P, 4, :, :], 0.0))
            step(pool.memset(keep_rows[32:36, NPR:TOK:NS], 0.0))
            pool.memset(cut_rows[0:4, NPR:TOK:NS], NEG).then_inc(S.consts_ready, 1)

        def hist_pe(pe):
            pe.wait_ge(S.a_loaded, A_LOADS)
            pe.wait_ge(region_free[1], BASE_INA // 2)
            for k in range(16):
                pe.transpose(psum[0:DH, 4, 24 * k:24 * k + 24], hist_nat[:, k * DH:(k + 1) * DH], ident[0:24, 0:24])
            for d in range(2):
                last = pe.transpose(psum[0:DH, 4, 384 + 32 * d:416 + 32 * d], n_nat[:, d * DH:(d + 1) * DH], ident[0:32, 0:32])
            last.then_inc(S.hist_turned, 1)

        def hist_dve(dve):
            dve.wait_ge(S.hist_turned, 1)
            dve.tensor_copy(sqt[1][0:DH, 0:384], psum[0:DH, 4, 0:384])
            dve.tensor_copy(n_t[:, :, :].rearrange("p d n -> p (d n)"), psum[0:DH, 4, 384:448]).then_inc(S.hist_ready, 1)

        S_AT = (0, 512, 1024, 1280)
        S_SAMPLE = 1408
        E_SPANS = ((P, 0, 896), (P, 1024, 1408), (NSA, 1408, 1472))

        def turned_rows_pe(pe):
            pe.wait_ge(S.gate_rows, 1)
            pe.wait_ge(region_free[0], BASE_OUTA // 2)
            pe.wait_ge(region_free[1], BASE_OUTA // 2)
            for t in range(TT):
                pe.transpose(flat[:, t * P:(t + 1) * P] if t < 4 else psum[0:NSA, 1, 0:P],
                             rows_t[:, t * P:(t + 1) * P] if t < 4 else rows_t[:, NPR:TOK], ident[:, :])
            for h in range(HA):
                pe.matmul(psum[0:DH, 2, 64 * h:64 * h + 64], ident[96:100, 96 + h:97 + h].broadcast_to([4, DH]),
                          rows_t[96:100, TOK:TOK + NSA], start=True, stop=True)
            pe.matmul(psum[0:NB, 2, 256:260], rows_t[96:100, TOK + NS - 1:TOK + NSA:NS], ident[96:100, 96:100],
                      start=True, stop=True).then_inc(S.cols_turned, 1)
            for k in range(16):
                last = pe.transpose(psum[0:27, 4 + k // 5, DH * (k % 5):DH * (k % 5) + DH], tails[:, k, :], ident[0:DH, 0:DH])
            last.then_inc(S.tails_turned, 1)

        def turned_rows_dve(dve):
            dve.wait_ge(S.cols_turned, 1)
            dve.tensor_copy(cols[:, 0:4, :], psum[:, 0, :].rearrange("p (t n) -> p t n", t=4)[:, :, 0:68])
            dve.memset(cols[:, 4, :], 1.0).then_inc(S.dve_cols, 1)
            dve.wait_ge(S.dve_cols, 1)
            dve.tensor_copy(cols[0:NSA, 4, :], psum[0:NSA, 1, 0:68])
            dve.tensor_copy(sqt[0][0:DH, 0:256], psum[0:DH, 2, 0:256])
            dve.tensor_copy(decay_b[:, :], psum[0:NB, 2, 256:260])
            dve.wait_ge(S.tails_turned, 1)
            dve.tensor_copy(wv_b[0:27, 0:1440].rearrange("p (b n) -> p b n", b=3), psum[0:27, 4:7, 0:480])
            dve.tensor_copy(wv_b[0:27, 1440:1536], psum[0:27, 7, 0:DH]).then_inc(S.tails_ready, 1)
            dve.memset(tmp[0][:, :], 0.0)
            dve.memset(tmp[1][:, :], 0.0).then_inc(S.dve_cols, 1)

        def n_old(h):
            return sqt[1][0:NB, h * DA:(h + 1) * DA] if h < 3 else sumsq[0:NB, 2 * DA:3 * DA]

        def mla_pool(pool):
            pool.wait_ge(S.tile_done, BASE_OUTA)
            pool.dma_start(gh_b[:, :], I["g_h_a"][0].rearrange("h d -> (h d)").partition_broadcast(P)).then_inc(S.gh_loaded, 16)
            pool.dma_start(O["m_prompt"][0].rearrange("a h -> h a"), sqt[0][0:4, NPR - 1:NPR], allow_slow_non_contiguous=True).then_inc(S.m_stored, 16)
            pool.dma_start(O["m_sample"][0].rearrange("b h -> h b"), sqt[0][0:4, NPR + NS - 1:TOK:NS], allow_slow_non_contiguous=True).then_inc(S.m_stored, 16)

            pool.wait_ge(S.tails_turned, 1)
            for h in range(HA):
                pool.dma_start(n_old(h), I["state_n"][0, :, h, :]).then_inc(S.gh_loaded, 16)

            def load_state(i):
                h, b, slot = i // NB, i % NB, i % NC
                if i >= NC:
                    pool.wait_ge(state_stored[slot], 16 * (i // NC))
                pool.dma_start(carried[:, slot, :, :], I["state_C"][0, b, h].rearrange("(e p) d -> p e d", p=DH)) \
                    .then_inc(state_loaded[slot], 16)

            for i in range(NC - 1):
                load_state(i)
            pool.wait_ge(S.tails_ready, 1)
            pool.dma_start(O["conv_prompt"][0, 0], wv_b[0:3, :]).then_inc(S.tails_stored, 16)
            pool.dma_start(O["conv_sample"][0].rearrange("b t f -> (b t) f"), wv_b[3:27, :]).then_inc(S.tails_stored, 16)
            for i in range(HA * NB):
                h, b, slot = i // NB, i % NB, i % NC
                pool.wait_ge(S.state_new, i + 1)
                pool.dma_start(O["C_sample"][0, b, h].rearrange("(e p) d -> p e d", p=DH), carried[:, slot, :, :]) \
                    .then_inc(state_stored[slot], 16)
                if i + NC - 1 < HA * NB:
                    load_state(i + NC - 1)
                if b == NB - 1:
                    pool.wait_ge(S.heads_state, h + 1)
                    pool.dma_start(O["C_prompt"][0, 0, h].rearrange("(e p) d -> p e d", p=DH), rinv[0:DH, 0:2 * DA].rearrange("p (e d) -> p e d", e=2)).then_inc(S.head_stored, 16)
                    pool.dma_start(O["n_prompt"][0, :, h], sumsq[0:1, 0:DA]).then_inc(S.head_stored, 16)
                    pool.dma_start(O["n_sample"][0, :, h], sumsq[0:NB, DA:2 * DA]).then_inc(S.head_stored, 16)

        def mla_pe(pe):
            for h in range(HA):
                q, k = (qk[:, o + 2 * h:o + 2 * h + 2, :] for o in (0, 8))
                if h == 0:
                    pe.wait_ge(S.k_scaled, 4)
                    pe.wait_ge(S.tails_ready, 1)
                else:
                    pe.wait_ge(S.h_scaled, h)
                    pe.wait_ge(S.heads_state, h)
                    pe.wait_ge(S.state_new, NB * h)
                big = ident[96:100, 96 + h:97 + h].broadcast_to([4, P])
                pe.matmul(psum[:, 7, :], big, rows_t[96:100, 0:NPR], start=True, stop=True)
                pe.matmul(psum[0:NSA, 3, 0:NSA], big[:, 0:NSA], rows_t[96:100, NPR:TOK], start=True, stop=True)
                for s in range(TT):
                    at, n = (S_AT[s], NPR - P * s) if s < 4 else (S_SAMPLE, NSA)
                    rows = P if s < 4 else NSA
                    for d in range(2):
                        last = pe.matmul(flat[0:rows, at:at + n], k[:, d, s * P:s * P + rows], q[:, d, s * P:s * P + n],
                                         start=(d == 0), stop=(d == 1))
                last.then_inc(S.qk_ready, 1)
                pe.wait_ge(S.w_ready, h + 1)
                pe.wait_ge(S.consts_ready, 2)
                pe.matmul(psum[:, 6, 0:DA + 1], w_pad[:, :], v_nat[0:NSA, 4, h, :], start=True, stop=False,
                          skip_group_check=True)
                for t in range(4):
                    out = psum[:, 4 + t // 2, (t % 2) * 256:(t % 2) * 256 + DA + 1]
                    for s in range(t + 1):
                        last = pe.matmul(out, w_all[:, S_AT[s] + (t - s) * P:S_AT[s] + (t - s + 1) * P], v_nat[:, s, h, :],
                                         start=(s == 0), stop=(s == t))
                last.then_inc(S.num_prompt, 1)
                for s in range(TT):
                    rows = P if s < 4 else NSA
                    for d in range(2):
                        last = pe.transpose(psum[0:rows, s // 2, (s % 2) * 256 + d * DH:(s % 2) * 256 + (d + 1) * DH],
                                            k[:, d, s * P:s * P + rows], ident[0:DH, 0:DH])
                last.then_inc(S.k_turned, 1)

                def turn_state(b):
                    i = h * NB + b
                    pe.wait_ge(state_loaded[i % NC], 16 * (i // NC + 1))
                    if b or h:
                        pe.wait_ge(S.state_turned_copied, i)
                    for d in range(2):
                        for e in range(2):
                            last = pe.transpose(psum[0:DH, 3, (2 * d + e) * DH:(2 * d + e + 1) * DH],
                                                carried[:, i % NC, e, d * DH:(d + 1) * DH], ident[0:DH, 0:DH])
                    last.then_inc(S.state_turned, 1)

                turn_state(0)
                pe.wait_ge(S.wv_ready, h + 1)
                for e in range(2):
                    for s in range(4):
                        pe.matmul(psum[0:DH, 0, e * DA:(e + 1) * DA], wv[:, s, e * DH:(e + 1) * DH], k_nat[:, s, :],
                                  start=(s == 0), stop=(s == 3))
                for s in range(4):
                    pe.matmul(psum[0:1, 7, 0:DA], cols[:, s, 32 + h:33 + h], k_nat[:, s, :], start=(s == 0), stop=(s == 3))
                pe.matmul(psum[0:NB, 7, DA:2 * DA], w_end_b[:, :], k_nat[0:NSA, 4, :], start=True, stop=True) \
                    .then_inc(S.prompt_state, 1)
                for b in range(NB):
                    i = h * NB + b
                    pe.wait_ge(S.state_turned_copied, i + 1)
                    for d in range(2):
                        last = pe.matmul(psum[0:NSA, 6, 0:DA + 1], tmp[d][0:DH, b * NSA:(b + 1) * NSA], turned[:, i % 2, d, :],
                                         start=False, stop=(b == NB - 1 and d == 1), skip_group_check=True)
                    last.then_inc(S.num_sample, 1)
                    if b < NB - 1:
                        turn_state(b + 1)
                    if b >= 2:
                        pe.wait_ge(S.state_new, i - 1)
                    for e in range(2):
                        last = pe.matmul(psum[0:DH, 1 + b % 2, e * DA:(e + 1) * DA],
                                         wv_b[0:NSA, b * DA + e * DH:b * DA + (e + 1) * DH], k_nat[0:NSA, 4, :],
                                         start=True, stop=True)
                    last.then_inc(S.update_ready, 1)

        def mla_act(act):
            for h in range(HA):
                act.wait_ge(S.exponents_ready, h + 1)
                for rows, at, to in E_SPANS:
                    ins = act.activation(e_all[0:rows, at:to], e_all[0:rows, at:to], ACT.Exp)
                ins.then_inc(S.exp_ready, 1)
                for b in range(NB):
                    i = h * NB + b
                    act.wait_ge(S.state_turned, i + 1)
                    if i >= 2:
                        act.wait_ge(S.num_sample, i - 1)
                    act.activation(turned[:, i % 2, :, DA:DA + 1], n_t[:, :, b * HA + h:b * HA + h + 1], ACT.Copy)
                    act.activation(turned[:, i % 2, :, 0:DA], psum[0:DH, 3, 0:2 * DA].rearrange("p (d n) -> p d n", d=2),
                                   ACT.Copy).then_inc(S.state_turned_copied, 1)
                act.wait_ge(S.h_scaled, h + 1)
                act.activation(h_sq, h_nat[:, :, :], ACT.Square).then_inc(S.h_squared, 1)
                act.wait_ge(S.h_ms, h + 1)
                act.activation(small[:, 16:21], small[:, 16:21], ACT.Sqrt, scale=1.0 / DA, bias=eps[:, :]).then_inc(S.h_rms, 1)

        def mla_dve(dve, c):
            def step(ins):
                ins.then_inc(S.dve_step, 1)
                dve.wait_ge(S.dve_step, c("dve_step"))

            num = flat[:, 2048:2048 + 5 * 256].rearrange("p (t n) -> p t n", n=256)
            for h in range(HA):
                v = v_nat[:, :, h, :]
                if h == 0:
                    dve.wait_ge(S.dve_cols, 2)
                dve.wait_ge(S.qk_ready, h + 1)
                for s in range(4):
                    at, a = S_AT[s], cols[:, s, h:h + 1]
                    dve.scalar_tensor_tensor(e_all[:, at:at + P], psum[:, 7, s * P:(s + 1) * P], a, causal[:, :], ALU.add, ALU.add)
                    if s < 3:
                        dve.tensor_scalar(e_all[:, at + P:at + NPR - s * P], psum[:, 7, (s + 1) * P:NPR], a, None, ALU.add)
                dve.scalar_tensor_tensor(e_all[0:NSA, S_SAMPLE:S_SAMPLE + NSA], psum[0:NSA, 3, 0:NSA], cols[0:NSA, 4, h:h + 1],
                                         causal_b[:, :], ALU.add, ALU.add).then_inc(S.exponents_ready, 1)
                carry = carry_all[:, h, :]
                for d in range(2):
                    dve.tensor_tensor(tmp[d][0:DH, :].rearrange("p (b x) -> p b x", b=NB)[:, :, 0:NS],
                                      qk[:, 2 * h + d, NPR:TOK].rearrange("p (b t) -> p b t", b=NB),
                                      carry.rearrange("p (b t) -> p b t", b=NB), ALU.mult)
                dve.wait_ge(S.exp_ready, h + 1)
                for rows, at, to in E_SPANS[:2]:
                    dve.tensor_tensor(w_all[0:rows, at:to], e_all[0:rows, at:to], flat[0:rows, at:to], ALU.mult)
                dve.tensor_tensor(w_pad[:, 0:NSA], e_all[0:NSA, S_SAMPLE:S_SAMPLE + NSA], flat[0:NSA, S_SAMPLE:S_SAMPLE + NSA],
                                  ALU.mult).then_inc(S.w_ready, 1)
                w_end = cols[:, :, 32 + h:33 + h]
                dve.wait_ge(S.k_turned, h + 1)
                if h == 0:
                    dve.wait_ge(S.tails_stored, 32)
                k_psum = flat[:, 0:5 * 256].rearrange("p (t n) -> p t n", n=256)
                dve.tensor_copy(k_nat[:, 0:4, :], k_psum[:, 0:4, 0:DA])
                dve.tensor_copy(k_nat[0:NSA, 4, :], k_psum[0:NSA, 4, 0:DA])
                dve.tensor_tensor(wv[:, :, :], v[:, 0:4, 0:DA], w_end[:, 0:4, :].broadcast_to([P, 4, DA]), ALU.mult)
                step(dve.tensor_scalar(w_end_b[:, :], own[:, :], w_end[0:NSA, 4, :], None, ALU.mult))
                dve.tensor_tensor(wv_b[0:NSA, :].rearrange("p (b n) -> p b n", b=NB),
                                  v[0:NSA, 4, 0:DA].unsqueeze(1).broadcast_to([NSA, NB, DA]),
                                  w_end_b[:, :].unsqueeze(2).broadcast_to([NSA, NB, DA]), ALU.mult).then_inc(S.wv_ready, 1)
                dve.wait_ge(S.prompt_state, h + 1)
                if h:
                    dve.wait_ge(S.head_stored, 48 * h)
                else:
                    dve.wait_ge(S.gh_loaded, 16 * (1 + HA))
                dve.tensor_copy(rinv[0:DH, 0:2 * DA], psum[0:DH, 0, 0:2 * DA])
                dve.tensor_copy(sumsq[0:1, 0:DA], psum[0:1, 7, 0:DA])
                dve.scalar_tensor_tensor(sumsq[0:NB, DA:2 * DA], n_old(h), decay_b[:, h:h + 1], psum[0:NB, 7, DA:2 * DA],
                                         ALU.mult, ALU.add).then_inc(S.heads_state, 1)
                for b in range(NB):
                    i = h * NB + b
                    dve.wait_ge(S.update_ready, i + 1)
                    s = carried[:, i % NC, :, :].rearrange("p e d -> p (e d)")
                    dve.scalar_tensor_tensor(s, s, carry[:, b * NS + NS - 1:b * NS + NS], psum[0:DH, 1 + b % 2, 0:2 * DA],
                                             ALU.mult, ALU.add).then_inc(S.state_new, 1)
                den, least = small[:, 24:29], cols[:, :, 64 + h]
                dve.wait_ge(S.num_sample, NB * (h + 1))
                step(dve.tensor_copy(den, num[:, :, DA]))
                step(dve.scalar_tensor_tensor(den, den, -1.0, den, ALU.mult, ALU.max))
                step(dve.tensor_tensor(den, den, least, ALU.max))
                step(dve.reciprocal(den, den))
                dve.tensor_tensor(h_nat[:, :, :], num[:, :, 0:DA], den.unsqueeze(2).broadcast_to([P, TT, DA]), ALU.mult) \
                    .then_inc(S.h_scaled, 1)
                dve.wait_ge(S.h_squared, h + 1)
                dve.tensor_reduce(small[:, 16:21], h_sq, AX, ALU.add).then_inc(S.h_ms, 1)
                dve.wait_ge(S.h_rms, h + 1)
                step(dve.reciprocal(small[:, 16:21], small[:, 16:21]))
                step(dve.tensor_tensor(h_nat[:, :, :], h_nat[:, :, :], small[:, 16:21].unsqueeze(2).broadcast_to([P, TT, DA]), ALU.mult))
                step(dve.tensor_tensor(h_nat[:, :, :], h_nat[:, :, :],
                                       gh_b[:, h * DA:(h + 1) * DA].unsqueeze(1).broadcast_to([P, TT, DA]), ALU.mult))
                dve.tensor_tensor(o_nat[:, :, h, :], o_nat[:, :, h, :], h_nat[:, :, :], ALU.mult).then_inc(S.num_copied, 1)

        def qnorm_pe(pe, at, chunks):
            for k in range(chunks):
                i = at + k
                pe.wait_ge(S.q_squared, i + 1)
                for h in range(2):
                    last = pe.matmul(psum[:, 2 * (k % 2) + h, 0:HALF], ones_heads[:, :], sqt[k % 2][:, h * HALF:(h + 1) * HALF],
                                     start=True, stop=True)
                last.then_inc(S.q_summed, 1)

        def qnorm_act(act, at, chunks, src):
            for k in range(chunks):
                i = at + k
                if i >= 2:
                    act.wait_ge(S.q_summed, i - 1)
                act.activation(sqt[k % 2][:, :], src(k), ACT.Square).then_inc(S.q_squared, 1)
                act.wait_ge(S.q_summed, i + 1)
                if i >= 2:
                    act.wait_ge(S.q_normed, i - 1)
                act.activation(halves(tmp[k % 2][:, :]), psum[:, 2 * (k % 2):2 * (k % 2) + 2, 0:HALF], ACT.Sqrt,
                               scale=1.0 / DM, bias=eps[:, :]).then_inc(S.q_rms, 1)

        def qnorm_dve(dve, at, chunks, src, dst, gain_col, c):
            for k in range(chunks):
                dve.wait_ge(S.q_rms, at + k + 1)
                dve.reciprocal(tmp[k % 2][:, :], tmp[k % 2][:, :]).then_inc(S.dve_step, 1)
                dve.wait_ge(S.dve_step, c("dve_step"))
                dve.scalar_tensor_tensor(dst(k), src(k), gain_col, tmp[k % 2][:, :], ALU.mult, ALU.mult).then_inc(S.q_normed, 1)

        def place(h):
            return 2 * (h % 2) + h // 2

        def mem_attention_pe(pe, l, B):
            pe.wait_ge(S.q_normed, B.normed)

            def scores(t):
                i = 4 * l + t
                if t >= 2:
                    pe.wait_ge(S.ma_exp, i - 1)
                for h in range(HM):
                    r = slice(64 * (h % 2), 64 * (h % 2) + 64)
                    last = pe.matmul(psum[:, 2 * (t % 2) + h % 2, 256 * (h // 2):256 * (h // 2) + M],
                                     B.qn[r, h // 2, t * P:(t + 1) * P], mk_t[l][r, h // 2, :], start=True, stop=True)
                last.then_inc(S.ma_scores, 1)

            scores(0)
            for t in range(4):
                i = 4 * l + t
                if t < 3:
                    scores(t + 1)
                pe.wait_ge(S.ma_p, i + 1)
                for x in range(8):
                    last = pe.transpose(psum[:, 4 + x // 4, (x % 4) * P:(x % 4 + 1) * P],
                                        B.e[:, x // 2, (x % 2) * P:(x % 2 + 1) * P], ident[:, :])
                last.then_inc(S.ma_turned, 1)
                pe.wait_ge(S.ma_pt, i + 1)
                if t:
                    pe.wait_ge(S.ma_out_lo, 5 * l + t)
                for h in range(HM):
                    for m in range(2):
                        last = pe.matmul(psum[64 * (h % 2):64 * (h % 2) + 64, 6, (h // 2) * P:(h // 2 + 1) * P],
                                         mv[l][:, m, h * DM:(h + 1) * DM], B.pt[:, 2 * place(h) + m, :], start=(m == 0), stop=(m == 1))
                last.then_inc(S.ma_out, 1)

            for g in range(2):
                for b in range(4 * g, 4 * g + 4):
                    i = NB * l + b
                    pe.wait_ge(ks_loaded[b % 4], 16 * (2 * l + b // 4 + 1))
                    if b == 0:
                        pe.wait_ge(S.ma_p, 4 * l + 4)
                    if b >= 2:
                        pe.wait_ge(S.ms_kt, i - 1)
                    for pair in range(2):
                        for m in range(2):
                            last = pe.transpose(psum[:, b % 2, (2 * pair + m) * P:(2 * pair + m + 1) * P],
                                                B.ks[:, b % 4, m, pair * P:(pair + 1) * P], ident[:, :])
                    last.then_inc(S.ms_turned, 1)
                    pe.wait_ge(S.ms_kt, i + 1)
                    if b == 0:
                        pe.wait_ge(S.ms_qz, l + 1)
                    if b == 4:
                        pe.wait_ge(S.ms_exp, 2 * l + g)
                    for pair in range(2):
                        last = pe.matmul(psum[32 * (b % 4):32 * (b % 4) + 32, 2, 0:M], B.qz[:, pair, b, :], B.kt[:, b % 2, pair, :],
                                         start=(pair == 0), stop=(pair == 1))
                    last.then_inc(S.ms_scores, 1)
                pe.wait_ge(S.ms_p, 2 * l + g + 1)
                for m in range(2):
                    last = pe.transpose(psum[:, 3, m * P:(m + 1) * P], B.e[:, 0, m * P:(m + 1) * P], ident[:, :])
                last.then_inc(S.ms_pturned, 1)
                pe.wait_ge(S.ms_pt, 2 * l + g + 1)
                if g == 0:
                    pe.wait_ge(S.vs_loaded, 128 * (l + 1))
                for b in range(4 * g, 4 * g + 4):
                    for pair in range(2):
                        at = (b * 2 + pair) * 16
                        row = 32 * (b % 4) + 16 * pair
                        for m in range(2):
                            last = pe.matmul(psum[:, 7, at:at + 16], B.vs[:, b, m, pair * P:(pair + 1) * P],
                                             B.pt[:, m, row:row + 16], start=(m == 0), stop=(m == 1))
                last.then_inc(S.ms_out, 1)

        def mem_attention_act(act, l, B):
            scale = float(DM) ** -0.5
            for t in range(4):
                i = 4 * l + t
                if t:
                    act.wait_ge(S.ma_turned, i)
                act.wait_ge(S.ma_max, i + 1)
                for h in range(HM):
                    x = place(h)
                    ins = act.activation(B.e[:, x, :], psum[:, 2 * (t % 2) + h % 2, 256 * (h // 2):256 * (h // 2) + M], ACT.Exp,
                                         scale=scale, bias=small[:, 32 + x:33 + x], accum_out=small[:, 36 + x:37 + x])
                ins.then_inc(S.ma_exp, 1)
                act.wait_ge(S.ma_turned, i + 1)
                act.activation(B.pt[:, :, :].rearrange("p x n -> p (x n)"), flat[:, 2048:3072], ACT.Copy).then_inc(S.ma_pt, 1)
                act.wait_ge(S.ma_out, i + 1)
                act.activation(act_hi[:, 6:8, t * P:(t + 1) * P], psum[:, 6, 0:256].rearrange("p (a n) -> p a n", a=2),
                               ACT.Copy).then_inc(S.ma_out_hi, 1)
            for g in range(2):
                for b in range(4 * g, 4 * g + 4):
                    i = NB * l + b
                    act.wait_ge(S.ms_turned, i + 1)
                    if b >= 2:
                        act.wait_ge(S.ms_scores, i - 1)
                    act.activation(B.kt[:, b % 2, :, :].rearrange("p a m -> p (a m)"), psum[:, b % 2, :], ACT.Copy).then_inc(S.ms_kt, 1)
                act.wait_ge(S.ms_max, 2 * l + g + 1)
                act.activation(B.e[:, 0, :], psum[:, 2, 0:M], ACT.Exp, scale=scale, bias=small[:, 32:33],
                               accum_out=small[:, 36:37]).then_inc(S.ms_exp, 1)
                act.wait_ge(S.ms_pturned, 2 * l + g + 1)
                act.activation(B.pt[:, 0:2, :].rearrange("p x n -> p (x n)"), psum[:, 3, 0:256], ACT.Copy).then_inc(S.ms_pt, 1)
            act.wait_ge(S.ms_out, 2 * l + 2)
            for r in range(2):
                ins = act.activation(sample_mix(act_hi, r, 6, 2), mem_out_view(r), ACT.Copy)
            ins.then_inc(S.ma_out_hi, 1)

        def sample_mix(t, r, c0, n):
            return t[64 * r:64 * r + 64, c0:c0 + n, NPR:TOK].rearrange("p c (b t) -> p c b t", b=NB)

        def mem_out_view(r):
            return psum[64 * r:64 * r + 64, 7, 0:256].rearrange("p (b c x) -> p c b x", b=NB, c=2)[:, :, :, 8 * r:8 * r + 8]

        def mem_attention_dve(dve, l, B, c):
            scale = float(DM) ** -0.5

            def step(ins):
                ins.then_inc(S.dve_step, 1)
                dve.wait_ge(S.dve_step, c("dve_step"))

            step(dve.memset(B.qz[:, :, :, :], 0.0))
            for pair in range(2):
                for r in range(2):
                    h = 2 * pair + r
                    ins = dve.tensor_copy(B.qz[64 * r:64 * r + 64, pair, :, h * NS:(h + 1) * NS],
                                          B.qn[64 * r:64 * r + 64, pair, NPR:TOK].rearrange("p (b t) -> p b t", b=NB))
            ins.then_inc(S.ms_qz, 1)
            for t in range(4):
                i = 4 * l + t
                dve.wait_ge(S.ma_scores, i + 1)
                s = flat[:, 1024 * (t % 2):1024 * (t % 2) + 1024].rearrange("p (h m) -> p h m", h=HM)
                step(dve.tensor_reduce(small[:, 32:36], s, AX, ALU.max))
                dve.tensor_scalar(small[:, 32:36], small[:, 32:36], -scale, None, ALU.mult).then_inc(S.ma_max, 1)
                dve.wait_ge(S.ma_exp, i + 1)
                step(dve.reciprocal(small[:, 36:40], small[:, 36:40]))
                dve.tensor_tensor(B.e[:, :, :], B.e[:, :, :], small[:, 36:40].unsqueeze(2).broadcast_to([P, HM, M]), ALU.mult) \
                    .then_inc(S.ma_p, 1)
                dve.wait_ge(S.ma_out_hi, 5 * l + t + 1)
                dve.tensor_tensor(act_lo[:, 6:8, t * P:(t + 1) * P], psum[:, 6, 0:256].rearrange("p (a n) -> p a n", a=2),
                                  act_hi[:, 6:8, t * P:(t + 1) * P].bitcast(F32), ALU.subtract).then_inc(S.ma_out_lo, 1)
            for g in range(2):
                i = 2 * l + g
                dve.wait_ge(S.ms_scores, NB * l + 4 * g + 4)
                step(dve.tensor_reduce(small[:, 32:33], psum[:, 2, 0:M], AX, ALU.max))
                dve.tensor_scalar(small[:, 32:33], small[:, 32:33], -scale, None, ALU.mult).then_inc(S.ms_max, 1)
                dve.wait_ge(S.ms_exp, i + 1)
                step(dve.reciprocal(small[:, 36:37], small[:, 36:37]))
                dve.tensor_scalar(B.e[:, 0, :], B.e[:, 0, :], small[:, 36:37], None, ALU.mult).then_inc(S.ms_p, 1)
            dve.wait_ge(S.ma_out_hi, 5 * l + 5)
            for r in range(2):
                ins = dve.tensor_tensor(sample_mix(act_lo, r, 6, 2), mem_out_view(r), sample_mix(act_hi, r, 6, 2).bitcast(F32),
                                        ALU.subtract)
            ins.then_inc(S.ma_out_lo, 1)

        def mem_attention_pool(pool, l, B, c):
            if l:
                pool.wait_ge(S.kv_stored, 64)
                pool.wait_ge(S.tile_done, BASE_INB)
            for b in range(NB):
                if b >= 4:
                    pool.wait_ge(S.ms_turned, NB * l + b - 3)
                pool.dma_start(B.ks[:, b % 4, :, :], I["cache_mem_k"][l, b].rearrange("(m p) h d -> p m (h d)", p=P)) \
                    .then_inc(ks_loaded[b % 4], 16)
                pool.dma_start(B.vs[:, b, :, :], I["cache_mem_v"][l, b].rearrange("(m p) h d -> p m (h d)", p=P)) \
                    .then_inc(S.vs_loaded, 16)

        def ha_pe(pe):
            pe.wait_ge(S.num_copied, HA)
            pe.wait_ge(S.ma_out_lo, 5)
            for k in range(6):
                if k >= 3:
                    pe.wait_ge(S.mix_lo, k - 2)
                b = 2 * (k % 3)
                for t, at, rows in token_tiles():
                    last = pe.transpose(psum[:, b, t * P:(t + 1) * P] if t < 4 else psum[:, b + 1, 0:NSA],
                                        o_flat[0:rows, t, k * P:(k + 1) * P], ident[0:rows, 0:rows])
                last.then_inc(S.mix_turned, 1)

        def ha_act(act):
            for k in range(6):
                act.wait_ge(S.mix_turned, k + 1)
                act.activation(act_hi[:, k, :], flat[:, 1024 * (k % 3):1024 * (k % 3) + TOK], ACT.Copy).then_inc(S.mix_hi, 1)

        def ha_dve(dve):
            for k in range(6):
                dve.wait_ge(S.mix_hi, k + 1)
                dve.tensor_tensor(act_lo[:, k, :], flat[:, 1024 * (k % 3):1024 * (k % 3) + TOK], act_hi[:, k, :].bitcast(F32),
                                  ALU.subtract).then_inc(S.mix_lo, 1)

        def kv_sp(sp):
            view = I["w_kv"].rearrange("(k p) n -> p k n", p=P)
            for t in range(6):
                load(sp, BASE_KV + t, t % 2, view[:, :, t * 256:(t + 1) * 256], raw[t % 2][:, :].rearrange("p (k n) -> p k n", k=KD))

        def kv_pe(pe, nth):
            pe.wait_ge(S.nl_ready, 8 * nth + 8)
            for t in range(6):
                w_hi, w_lo = weights(t % 2, (KD, 256))
                natural_product(pe, BASE_KV + t, t % 2, w_hi, w_lo, 256)
            pe.wait_ge(S.k_ready, 3)
            for k in range(6):
                b = 2 * (k % 3)
                if k < 3:
                    pe.wait_ge(S.region_free0, BASE_FFN[2] // 2)
                    pe.wait_ge(S.region_free1, BASE_FFN[2] // 2)
                else:
                    pe.wait_ge(S.kt_copied, k - 2)
                for t, at, rows in token_tiles():
                    last = pe.transpose(psum[:, b, t * P:(t + 1) * P] if t < 4 else psum[:, b + 1, 0:NSA],
                                        kn[0:rows, t, k * P:(k + 1) * P], ident[0:rows, 0:rows])
                last.then_inc(S.kt_turned, 1)
            pe.wait_ge(S.kt_copied, 6)

        def kv_act(act):
            for t in range(6):
                n, j = BASE_KV + t, t % 2
                split_hi(act, n + 1, 1 - j)
                act.wait_ge(S.tile_done, n + 1)
                dst, src = (kn, vn)[t // 3], natural_view(j, 256)
                cols_ = slice((t % 3) * 256, (t % 3) * 256 + 256)
                act.activation(dst[:, 0:4, cols_], src[:, 0:4, :], ACT.Copy)
                act.activation(dst[0:NSA, 4, cols_], src[0:NSA, 4, :], ACT.Copy).then_inc(region_free[j], 1)
                if t < 3:
                    act.wait_ge(S.kn_padded, 1)
                    if t:
                        act.wait_ge(S.k_ms, t)
                    act.wait_ge(region_free[j], n // 2 + 1)
                    act.activation(ksq[:, :, :], kn[:, :, cols_], ACT.Square).then_inc(S.k_squared, 1)
                    act.wait_ge(S.k_ms, t + 1)
                    act.activation(small[:, 40:60], small[:, 40:60], ACT.Sqrt, scale=1.0 / DB, bias=eps[:, :]).then_inc(S.k_rms, 1)

        def kv_dve(dve, c):
            def step(ins):
                ins.then_inc(S.dve_step, 1)
                dve.wait_ge(S.dve_step, c("dve_step"))

            dve.wait_ge(S.tile_done, BASE_KV)
            dve.memset(kn[NSA:P, 4, :], 0.0).then_inc(S.kn_padded, 1)
            for t in range(6):
                n, j = BASE_KV + t, t % 2
                split_lo(dve, n + 1, 1 - j)
                if t < 3:
                    dve.wait_ge(S.k_squared, t + 1)
                    sq = ksq[:, :, :].rearrange("p t (h d) -> p t h d", d=DB)
                    dve.tensor_reduce(small[:, 40:60].rearrange("p (t h) -> p t h", h=4), sq, AX, ALU.add).then_inc(S.k_ms, 1)
                    dve.wait_ge(S.k_rms, t + 1)
                    step(dve.reciprocal(small[:, 40:60], small[:, 40:60]))
                    for i in range(TT):
                        k = kn[:, i, t * 256:(t + 1) * 256].rearrange("p (h d) -> p h d", d=DB)
                        step(dve.tensor_tensor(k, k, small[:, 40 + 4 * i:44 + 4 * i].unsqueeze(2).broadcast_to([P, 4, DB]), ALU.mult))
                        ins = dve.tensor_tensor(k, k, gk_b[:, :].unsqueeze(1).broadcast_to([P, 4, DB]), ALU.mult)
                    ins.then_inc(S.k_ready, 1)
            for k in range(6):
                dve.wait_ge(S.kt_turned, k + 1)
                dve.tensor_copy(kt_b[:, k, :], flat[:, 1024 * (k % 3):1024 * (k % 3) + TOK]).then_inc(S.kt_copied, 1)

        def kv_pool(pool):
            def store(dst_p, dst_s, src):
                pool.dma_start(dst_p.rearrange("a (t p) h d -> p (a t) (h d)", p=P), src[:, 0:4, :]).then_inc(S.kv_stored, 16)
                pool.dma_start(dst_s.rearrange("b t h d -> (b t) (h d)"), src[0:NSA, 4, :]).then_inc(S.kv_stored, 16)
            pool.wait_ge(S.k_ready, 3)
            store(O["k_prompt"], O["k_sample"], kn)
            pool.wait_ge(S.region_free0, BASE_FFN[2] // 2)
            pool.wait_ge(S.region_free1, BASE_FFN[2] // 2)
            store(O["v_prompt"], O["v_sample"], vn)

        def inb_sp(sp):
            view = I["w_in_b"][0].rearrange("(k p) n -> p k n", p=P)
            for t in range(4):
                load(sp, BASE_INB + t, t % 2, view[:, :, t * 256:(t + 1) * 256], raw[t % 2][:, :].rearrange("p (k n) -> p k n", k=KD))

        def inb_pe(pe, nth):
            for t in range(4):
                w_hi, w_lo = weights(t % 2, (KD, 256))
                product(pe, BASE_INB + t, t % 2, w_hi, w_lo, act_hi, act_lo, KD, 2, P, ready=(S.nl_ready, 8 * nth, KD))

        def inb_act(act):
            for t in range(4):
                n, j = BASE_INB + t, t % 2
                split_hi(act, n + 1, 1 - j)
                act.wait_ge(S.tile_done, n + 1)
                dst = qb_t[:, 2 * t:2 * t + 2, :] if t < 3 else MB.qn[:, :, :]
                act.activation(dst.rearrange("p m (h n) -> p (m h) n", h=2), region(j)[:, :, 0:HALF], ACT.Copy) \
                    .then_inc(region_free[j], 1)
            act.wait_ge(S.region_free0, BASE_OUTB // 2)
            act.wait_ge(S.region_free1, BASE_OUTB // 2)

        Z_AT = (896, 1024, 512, 0)
        A_AT = (0, 512, 1024, 896)
        ZW = 1280

        def stick_pe(pe):
            pe.wait_ge(S.ma_out_lo, 10)
            pe.wait_ge(S.vp_loaded, 16)

            def z(h):
                r = slice(64 * (h % 2), 64 * (h % 2) + 64)
                if h:
                    pe.wait_ge(S.z_read, h)
                for t in range(4):
                    last = pe.matmul(flat[:, Z_AT[t]:Z_AT[t] + (t + 1) * P], qb_t[r, h // 2, t * P:(t + 1) * P],
                                     kt_b[r, h // 2, 0:(t + 1) * P], start=True, stop=True)
                last.then_inc(S.z_ready, 1)

            def outputs(h):
                pe.wait_ge(S.at_ready, h + 1)
                if h >= 4 and h % 2 == 0:
                    pe.wait_ge(S.stick_lo, h // 2 - 1)
                for k in range(4):
                    last = pe.matmul(psum[64 * (h % 2):64 * (h % 2) + 64, 6 + (h // 2) % 2, k * P:NPR], vp[:, k, h * DB:(h + 1) * DB],
                                     a_t[:, A_AT[k]:A_AT[k] + NPR - k * P], start=(k == 0), stop=(k == 3), skip_group_check=True)
                last.then_inc(S.stick_out, 1)

            z(0)
            for h in range(HB):
                if h + 1 < HB:
                    z(h + 1)
                if h:
                    outputs(h - 1)
                pe.wait_ge(S.a_ready, h + 1)
                for t in range(4):
                    for k in range(t + 1):
                        at = 1536 + A_AT[k] + (t - k) * P
                        last = pe.transpose(flat[:, at:at + P], keep[h % 2][:, Z_AT[t] + k * P:Z_AT[t] + (k + 1) * P], ident[:, :])
                last.then_inc(S.a_turned, 1)
            outputs(HB - 1)

        def stick_act(act):
            scale = float(DB) ** -0.5
            for h in range(HB):
                act.wait_ge(S.z_ready, h + 1)
                if h >= 2:
                    act.wait_ge(S.a_turned, h - 1)
                act.activation(take[h % 2][:, :], flat[:, 0:ZW], ACT.Sigmoid, scale=scale, bias=b_all[:, h:h + 1])
                act.activation(keep[h % 2][:, :], flat[:, 0:ZW], ACT.Sigmoid, scale=-scale, bias=b_neg[:, h:h + 1]).then_inc(S.z_read, 1)
                if h:
                    stick_act_tail(act, h - 1)
            stick_act_tail(act, HB - 1)

        def stick_act_tail(act, h):
            act.wait_ge(S.a_turned, h + 1)
            if h:
                act.wait_ge(S.stick_out, h)
            act.activation(a_t[:, 0:ZW], flat[:, 1536:1536 + ZW], ACT.Copy).then_inc(S.at_ready, 1)
            if h % 2 == 1 and h > 1:
                stick_hi(act, h // 2 - 1)
            if h == HB - 1:
                stick_hi(act, h // 2)

        def stick_hi(act, p):
            act.wait_ge(S.stick_out, 2 * p + 2)
            act.activation(act_hi[:, p, 0:NPR], psum[:, 6 + p % 2, :], ACT.Copy).then_inc(S.stick_hi, 1)

        def stick_lo(dve, p):
            dve.wait_ge(S.stick_hi, p + 1)
            dve.tensor_tensor(act_lo[:, p, 0:NPR], psum[:, 6 + p % 2, :], act_hi[:, p, 0:NPR].bitcast(F32), ALU.subtract) \
                .then_inc(S.stick_lo, 1)

        def stick_dve(dve, c):
            def step(ins):
                ins.then_inc(S.dve_step, 1)
                dve.wait_ge(S.dve_step, c("dve_step"))

            for h in range(HB):
                tk, kp = take[h % 2], keep[h % 2]
                dve.wait_ge(S.z_read, h + 1)
                three = slice(384, 384 + 3 * 384)
                for x, m, op in ((tk, before, ALU.mult), (kp, not_before, ALU.max)):
                    for at in (384, 768, 1152, 896):
                        ins = dve.tensor_tensor(x[:, at:at + P], x[:, at:at + P], m[:, :], op)
                step(ins)
                for t in range(4):
                    a, n = Z_AT[t], (t + 1) * P
                    ins = dve.tensor_tensor_scan(backwards(rest, a, n), backwards(kp, a, n), zero[:, :].broadcast_to([P, n]), 1.0,
                                                 ALU.mult, ALU.add)
                step(ins)
                dve.tensor_tensor(kp[:, 0:ZW - 1], tk[:, 0:ZW - 1], rest[:, 1:ZW], ALU.mult)
                dve.tensor_copy(kp[:, ZW - 1:ZW], tk[:, ZW - 1:ZW]).then_inc(S.a_ready, 1)
                dve.wait_ge(S.a_ready, h + 1)
                if h % 2 == 1 and h > 4:
                    stick_lo(dve, h // 2 - 2)
            stick_lo(dve, HB // 2 - 2)
            stick_lo(dve, HB // 2 - 1)

        def backwards(t, a, n):
            return t[:, a:a + n][:, ::-1]

        KEYS = PAST + NS

        def pages_pool(pool):
            pool.dma_start(table[:, :], I["page_table"].rearrange("b n -> (b n)").unsqueeze(0)).then_inc(S.table_loaded, 16)
            pool.wait_ge(S.kv_stored, 64)
            pool.wait_ge(S.ma_out_lo, 10)
            pool.dma_start(vp[:, :, :], O["v_prompt"].rearrange("a (t p) h d -> p (a t) (h d)", p=P)).then_inc(S.vp_loaded, 16)
            pool.wait_ge(S.table_loaded, 16)
            pool.wait_ge(S.stick_lo, HB // 2)
            for b in range(NB):
                j = b % 2
                if b >= 2:
                    pool.wait_ge(S.sb_out, b - 1)
                for g in range(PAST // PAGE):
                    page = pool.value_load(table[0:1, 2 * b + g:2 * b + g + 1], min_val=0, max_val=I["cache_k"].shape[0] - 1)
                    for dst, cache in ((kpg, I["cache_k"]), (vpg, I["cache_v"])):
                        pool.dma_start(dst[:, j, g, :], cache[bass.ds(page, 1), :, :, :].rearrange("a p h d -> (a p) (h d)")) \
                            .then_inc(pages_loaded[j], 16)
                pool.dma_start(vnew[:, j, :], O["v_sample"][b].rearrange("t h d -> t (h d)")).then_inc(pages_loaded[j], 16)

        def stick_sample_pe(pe):
            pe.wait_ge(S.stick_lo, HB // 2)
            for b in range(NB):
                j = b % 2
                pe.wait_ge(pages_loaded[j], 80 * (b // 2 + 1))
                if b:
                    pe.wait_ge(S.kpt_ready, b)
                for p in range(6):
                    for g in range(2):
                        at = p * 256 + g * P
                        last = pe.transpose(flat[:, at:at + P], kpg[:, j, g, p * P:(p + 1) * P], ident[:, :])
                last.then_inc(S.kpg_turned, 1)
                pe.wait_ge(S.kpt_ready, b + 1)
                pe.wait_ge(S.qzb_ready, b + 1)
                if b:
                    pe.wait_ge(S.zs_read, b)
                for part in range(2):
                    for p in range(6):
                        lhs = qzb[j][:, p * 96:(p + 1) * 96]
                        if part == 0:
                            last = pe.matmul(psum[0:96, 3, 0:PAST], lhs, kpt[:, p, :], start=(p == 0), stop=(p == 5))
                        else:
                            last = pe.matmul(psum[0:96, 3, PAST:KEYS], lhs, kt_b[:, p, NPR + b * NS:NPR + (b + 1) * NS],
                                             start=(p == 0), stop=(p == 5))
                last.then_inc(S.zs_ready, 1)
                pe.wait_ge(S.as_ready, b + 1)
                for g in range(2):
                    pe.transpose(psum[:, 4, g * 96:(g + 1) * 96], keeps[:, g * P:(g + 1) * P], ident[0:96, 0:96])
                pe.transpose(psum[0:NS, 4, 192:288], keeps[:, PAST:KEYS], ident[0:96, 0:96]).then_inc(S.as_turned, 1)
                pe.wait_ge(S.ats_ready, b + 1)
                if b >= 2:
                    pe.wait_ge(S.sb_lo, b - 1)
                for p in range(6):
                    out = psum[:, 5 + j, 16 * p:16 * p + 16]
                    for g in range(2):
                        pe.matmul(out, vpg[:, j, g, p * P:(p + 1) * P], a_ts[:, g * 96 + 16 * p:g * 96 + 16 * p + 16], start=(g == 0), stop=False)
                    last = pe.matmul(out, vnew[:, j, p * P:(p + 1) * P], a_ts[0:NS, 192 + 16 * p:208 + 16 * p], start=False, stop=True)
                last.then_inc(S.sb_out, 1)

        def stick_sample_act(act):
            scale = float(DB) ** -0.5
            for b in range(NB):
                act.wait_ge(S.kpg_turned, b + 1)
                if b:
                    act.wait_ge(S.zs_ready, b)
                act.activation(kpt[:, :, :].rearrange("p c k -> p (c k)"), flat[:, 0:1536], ACT.Copy).then_inc(S.kpt_ready, 1)
                act.wait_ge(S.zs_ready, b + 1)
                if b:
                    act.wait_ge(S.as_turned, b)
                act.activation(takes[:, :], psum[0:96, 3, 0:KEYS], ACT.Sigmoid, scale=scale, bias=b_rows[:, 0:1])
                act.activation(keeps[:, :], psum[0:96, 3, 0:KEYS], ACT.Sigmoid, scale=-scale, bias=b_rows[:, 1:2]).then_inc(S.zs_read, 1)
                act.wait_ge(S.as_turned, b + 1)
                if b:
                    act.wait_ge(S.sb_out, b)
                act.activation(a_ts[:, 0:192], psum[:, 4, 0:192], ACT.Copy)
                act.activation(a_ts[0:NS, 192:288], psum[0:NS, 4, 192:288], ACT.Copy).then_inc(S.ats_ready, 1)
                act.wait_ge(S.sb_out, b + 1)
                for r in range(2):
                    ins = act.activation(act_hi[64 * r:64 * r + 64, 0:6, NPR + b * NS:NPR + (b + 1) * NS], out_rows(b, r), ACT.Copy)
                ins.then_inc(S.sb_hi, 1)

        def out_rows(b, r):
            return psum[64 * r:64 * r + 64, 5 + b % 2, 0:96].rearrange("p (c x) -> p c x", c=6)[:, :, 8 * r:8 * r + 8]

        def stick_sample_dve(dve, c):
            def step(ins):
                ins.then_inc(S.dve_step, 1)
                dve.wait_ge(S.dve_step, c("dve_step"))

            for j in range(2):
                ins = dve.memset(qzb[j][:, :], 0.0)
            step(ins)
            for b in range(NB):
                if b >= 2:
                    dve.wait_ge(S.zs_ready, b - 1)
                for r in range(2):
                    dst = qzb[b % 2][64 * r:64 * r + 64, 0:672].rearrange("p (c x) -> p c x", c=6)[:, :, 8 * r:8 * r + 8]
                    ins = dve.tensor_copy(dst, qb_t[64 * r:64 * r + 64, 0:6, NPR + b * NS:NPR + (b + 1) * NS])
                ins.then_inc(S.qzb_ready, 1)
                dve.wait_ge(S.zs_read, b + 1)
                dve.tensor_tensor(takes[:, PAST:KEYS], takes[:, PAST:KEYS], own_keys[:, 0, :], ALU.mult)
                step(dve.tensor_tensor(keeps[:, PAST:KEYS], keeps[:, PAST:KEYS], own_keys[:, 1, :], ALU.max))
                step(dve.tensor_tensor_scan(rests[:, ::-1], keeps[:, ::-1], zero[0:96, :].broadcast_to([96, KEYS]), 1.0, ALU.mult, ALU.add))
                dve.tensor_tensor(keeps[:, 0:KEYS - 1], takes[:, 0:KEYS - 1], rests[:, 1:KEYS], ALU.mult)
                dve.tensor_copy(keeps[:, KEYS - 1:KEYS], takes[:, KEYS - 1:KEYS]).then_inc(S.as_ready, 1)
                dve.wait_ge(S.sb_hi, b + 1)
                for r in range(2):
                    half = slice(64 * r, 64 * r + 64), slice(0, 6), slice(NPR + b * NS, NPR + (b + 1) * NS)
                    ins = dve.tensor_tensor(act_lo[half], out_rows(b, r), act_hi[half].bitcast(F32), ALU.subtract)
                ins.then_inc(S.sb_lo, 1)

        block = ctx.enter_context(nc.Block())

        @block.sync
        def _(sp):
            setup_sp(sp)
            mem_sp(sp)
            ffn_sp(sp, 0)
            ina_sp(sp)
            out_sp(sp, BASE_OUTA, 0)
            ffn_sp(sp, 1)
            kv_sp(sp)
            ffn_sp(sp, 2)
            inb_sp(sp)
            out_sp(sp, BASE_OUTB, 1)
            ffn_sp(sp, 3)
            end_sp(sp)

        @block.gpsimd
        def _(pool):
            c = Count()
            setup_pool(pool, c)
            mem_pool(pool, c)
            ina_pool(pool, c)
            mla_pool(pool)
            mem_attention_pool(pool, 0, MA, c)
            kv_pool(pool)
            mem_attention_pool(pool, 1, MB, c)
            pages_pool(pool)
            pool.wait_ge(S.stored, 64)
            pool.wait_ge(S.m_stored, 32)
            pool.wait_ge(S.tails_stored, 32)
            pool.wait_ge(S.head_stored, 48 * HA)
            for slot in range(NC):
                pool.wait_ge(state_stored[slot], 16 * ((HA * NB - slot + NC - 1) // NC))
            pool.wait_ge(S.kv_stored, 64)

        @block.scalar
        def _(act):
            c = Count()
            setup_act(act)
            split_hi(act, 0, 0)
            mem_act(act)
            norm_act(act, 0, 0, False)
            ffn_act(act, 0, 1)
            norm_act(act, 1, 1, False)
            ina_act(act, c)
            mla_act(act)
            qnorm_act(act, 0, 2, lambda k: qm_a[:, k, :])
            mem_attention_act(act, 0, MA)
            ha_act(act)
            out_act(act, BASE_OUTA, 2)
            norm_act(act, 2, 2, False)
            ffn_act(act, 1, 3)
            norm_act(act, 3, 3, False)
            kv_act(act)
            norm_act(act, 3, 4, True)
            ffn_act(act, 2, 4)
            norm_act(act, 4, 5, False)
            inb_act(act)
            qnorm_act(act, 2, 2, lambda k: MB.qn[:, k, :])
            qnorm_act(act, 4, 6, lambda k: qb_t[:, k, :])
            mem_attention_act(act, 1, MB)
            stick_act(act)
            stick_sample_act(act)
            out_act(act, BASE_OUTB, 5)
            norm_act(act, 5, 6, False)
            ffn_act(act, 3, None)

        @block.vector
        def _(dve):
            c = Count()
            setup_dve(dve, c)
            split_lo(dve, 0, 0)
            mem_dve(dve, c)
            norm_dve(dve, 0, 0, False, gain("ffn1", 0), c)
            ffn_dve(dve, 0, 1)
            norm_dve(dve, 1, 1, False, gain("mix", 0), c)
            ina_dve(dve, c)
            turned_rows_dve(dve)
            mla_dve(dve, c)
            qnorm_dve(dve, 0, 2, lambda k: qm_a[:, k, :], lambda k: MA.qn[:, k, :], vec_t[:, 72:73], c)
            mem_attention_dve(dve, 0, MA, c)
            ha_dve(dve)
            out_dve(dve, BASE_OUTA, 2)
            norm_dve(dve, 2, 2, False, gain("ffn2", 0), c)
            ffn_dve(dve, 1, 3)
            norm_dve(dve, 3, 3, False, gain("kv"), c)
            kv_dve(dve, c)
            norm_dve(dve, 3, 4, True, gain("ffn1", 1), c)
            ffn_dve(dve, 2, 4)
            norm_dve(dve, 4, 5, False, gain("mix", 1), c)
            for n in range(BASE_INB, BASE_OUTB):
                split_lo(dve, n + 1, (n + 1) % 2)
            qnorm_dve(dve, 2, 2, lambda k: MB.qn[:, k, :], lambda k: MB.qn[:, k, :], vec_t[:, 73:74], c)
            qnorm_dve(dve, 4, 6, lambda k: qb_t[:, k, :], lambda k: qb_t[:, k, :], vec_t[:, 74:75], c)
            mem_attention_dve(dve, 1, MB, c)
            stick_dve(dve, c)
            stick_sample_dve(dve, c)
            out_dve(dve, BASE_OUTB, 5)
            norm_dve(dve, 5, 6, False, gain("ffn2", 1), c)
            ffn_dve(dve, 3, None)
            end_dve(dve)

        @block.tensor
        def _(pe):
            setup_pe(pe)
            mem_pe(pe)
            norm_pe(pe, 0, BASE_FFN[0])
            ffn_pe(pe, 0, 0)
            hist_pe(pe)
            norm_pe(pe, 1, BASE_INA)
            ina_pe(pe, 1)
            turned_rows_pe(pe)
            mla_pe(pe)
            qnorm_pe(pe, 0, 2)
            mem_attention_pe(pe, 0, MA)
            ha_pe(pe)
            pe.wait_ge(S.mix_lo, 6)
            out_pe(pe, BASE_OUTA)
            norm_pe(pe, 2, BASE_FFN[1])
            ffn_pe(pe, 1, 2)
            norm_pe(pe, 3, BASE_KV)
            kv_pe(pe, 3)
            ffn_pe(pe, 2, 4)
            norm_pe(pe, 4, BASE_INB)
            inb_pe(pe, 5)
            pe.wait_ge(S.region_free0, BASE_OUTB // 2)
            pe.wait_ge(S.region_free1, BASE_OUTB // 2)
            qnorm_pe(pe, 2, 2)
            qnorm_pe(pe, 4, 6)
            mem_attention_pe(pe, 1, MB)
            stick_pe(pe)
            stick_sample_pe(pe)
            pe.wait_ge(S.sb_lo, NB)
            out_pe(pe, BASE_OUTB)
            norm_pe(pe, 5, BASE_FFN[3])
            ffn_pe(pe, 3, 6)
            end_pe(pe)


INS = ["x_prompt", "x_sample", "cache_k", "cache_v", "cache_mem_k", "cache_mem_v", "state_C", "state_n", "state_m",
       "state_conv", "page_table", "mem_prompt", "g_ffn1", "w_ffn1_up", "w_ffn1_down", "g_mix", "w_in_a", "b_gate_a",
       "conv_w_a", "conv_b_a", "g_h_a", "g_kv", "w_kv", "g_k_b", "w_in_b", "g_q_b", "b_sb", "g_mem", "w_mem_kv",
       "g_q_mem", "g_k_mem", "w_out", "g_ffn2", "w_ffn2_up", "w_ffn2_down"]
OUTS = [("y_prompt", (1, NPR, D)), ("y_sample", (NB, NS, D)),
        ("k_prompt", (1, NPR, HB, DB)), ("v_prompt", (1, NPR, HB, DB)),
        ("k_sample", (NB, NS, HB, DB)), ("v_sample", (NB, NS, HB, DB)),
        ("mem_k_prompt", (2, 1, M, HM, DM)), ("mem_v_prompt", (2, 1, M, HM, DM)),
        ("conv_prompt", (1, 1, 3, 2 * D_MAIN)), ("C_prompt", (1, 1, HA, DA, DA)), ("n_prompt", (1, 1, HA, DA)),
        ("m_prompt", (1, 1, HA)),
        ("conv_sample", (1, NB, 3, 2 * D_MAIN)), ("C_sample", (1, NB, HA, DA, DA)), ("n_sample", (1, NB, HA, DA)),
        ("m_sample", (1, NB, HA))]


def kernel(**inputs):
    import numpy as np
    from concourse import bacc
    from concourse.bass_utils import run_bass_kernel_spmd

    nc = bacc.Bacc("TRN2", target_bir_lowering=False, num_devices=1)
    arrays, ins, outs = {}, {}, {}
    for name in INS:
        a = np.ascontiguousarray(inputs[name])
        arrays[f"in_{name}"] = a
        ins[name] = nc.dram_tensor(f"in_{name}", a.shape, mybir.dt.from_np(a.dtype), kind="ExternalInput").ap()
    for name, shape in OUTS:
        outs[name] = nc.dram_tensor(f"out_{name}", shape, F32, kind="ExternalOutput").ap()
    build(nc, ins, outs)
    r = run_bass_kernel_spmd(nc, [arrays], core_ids=[0])
    return tuple(r.results[0][f"out_{name}"] for name, _ in OUTS)
```

```python
from contextlib import ExitStack

import concourse.bass as bass
from concourse import mybir

ALU = mybir.AluOpType
ACT = mybir.ActivationFunctionType
F32 = mybir.dt.float32
F32R = mybir.dt.float32r
I32 = mybir.dt.int32
AX = mybir.AxisListType.X

P = 128
D = 1024
KD = D // P
NPR = 512
NB, NS = 8, 8
NSA = NB * NS
TOK = NPR + NSA
HALF = TOK // 2
TT = 5
FF = 2816
FF_PARTS = (12, 10)
M = 256
HM, DM = 4, 64
HA, DA = 4, 192
DH = DA // 2
HB, DB = 12, 64
D_MAIN = 768
PAST, PAGE = 256, 128
EPS = 1e-6
NEG = -1e30
SLOT = 2048

FFN_TILES = sum(n + KD for n in FF_PARTS)
BASE_MEM = 0
BASE_FFN = [4]
BASE_INA = BASE_FFN[0] + FFN_TILES
INA_TILES = 18
BASE_OUTA = BASE_INA + INA_TILES
BASE_FFN.append(BASE_OUTA + 4)
BASE_KV = BASE_FFN[1] + FFN_TILES
BASE_FFN.append(BASE_KV + 6)
BASE_INB = BASE_FFN[2] + FFN_TILES
BASE_OUTB = BASE_INB + 4
BASE_FFN.append(BASE_OUTB + 4)
N_TILES = BASE_FFN[3] + FFN_TILES


class Count:

    def __init__(self):
        self.at = {}

    def __call__(self, name, by=1):
        self.at[name] = self.at.get(name, 0) + by
        return self.at[name]


class Semaphores:

    def __init__(self, sem):
        self.consts_ready = sem("consts_ready")
        self.inputs_loaded = sem("inputs_loaded")
        self.mem_loaded = sem("mem_loaded")
        self.x_loaded = sem("x_loaded")
        self.setup_turned = sem("setup_turned")
        self.setup_copied = sem("setup_copied")
        self.mem_squared = sem("mem_squared")
        self.mem_rms_ready = sem("mem_rms_ready")
        self.mem_scaled = sem("mem_scaled")
        self.mem_split = sem("mem_split")
        self.mem_hi = sem("mem_hi")
        self.raw_loaded0 = sem("raw_loaded0")
        self.raw_loaded1 = sem("raw_loaded1")
        self.hi_ready = sem("hi_ready")
        self.lo_ready = sem("lo_ready")
        self.tile_done = sem("tile_done")
        self.region_free0 = sem("region_free0")
        self.region_free1 = sem("region_free1")
        self.dve_step = sem("dve_step")
        self.pool_step = sem("pool_step")
        self.act_step = sem("act_step")
        self.sq_ready = sem("sq_ready")
        self.sum_done = sem("sum_done")
        self.sumsq_ready = sem("sumsq_ready")
        self.rms_ready = sem("rms_ready")
        self.rinv_kept = sem("rinv_kept")
        self.rinv_cols = sem("rinv_cols")
        self.rinv_spread = sem("rinv_spread")
        self.xn_ready = sem("xn_ready")
        self.nh_ready = sem("nh_ready")
        self.nl_ready = sem("nl_ready")
        self.sg_ready = sem("sg_ready")
        self.hh_ready = sem("hh_ready")
        self.hl_ready = sem("hl_ready")
        self.mk_sq = sem("mk_sq")
        self.mk_ms = sem("mk_ms")
        self.mk_rms = sem("mk_rms")
        self.mk_ready = sem("mk_ready")
        self.mkt_ready = sem("mkt_ready")
        self.mkt_copied = sem("mkt_copied")
        self.stored = sem("stored")
        self.y_turned = sem("y_turned")
        self.y_copied = sem("y_copied")
        self.y_stored = sem("y_stored")
        self.gate_abs = sem("gate_abs")
        self.gate_ln = sem("gate_ln")
        self.gate_m = sem("gate_m")
        self.gate_rows = sem("gate_rows")
        self.a_loaded = sem("a_loaded")
        self.hist_turned = sem("hist_turned")
        self.hist_ready = sem("hist_ready")
        self.conv_ready = sem("conv_ready")
        self.qk_silu = sem("qk_silu")
        self.k_scaled = sem("k_scaled")
        self.cols_turned = sem("cols_turned")
        self.dve_cols = sem("dve_cols")
        self.tails_turned = sem("tails_turned")
        self.tails_ready = sem("tails_ready")
        self.tails_stored = sem("tails_stored")
        self.gh_loaded = sem("gh_loaded")
        self.m_stored = sem("m_stored")
        self.head_stored = sem("head_stored")
        self.state_loaded0 = sem("state_loaded0")
        self.state_loaded1 = sem("state_loaded1")
        self.state_loaded2 = sem("state_loaded2")
        self.state_loaded3 = sem("state_loaded3")
        self.state_stored0 = sem("state_stored0")
        self.state_stored1 = sem("state_stored1")
        self.state_stored2 = sem("state_stored2")
        self.state_stored3 = sem("state_stored3")
        self.state_new = sem("state_new")
        self.heads_state = sem("heads_state")
        self.h_scaled = sem("h_scaled")
        self.h_squared = sem("h_squared")
        self.h_ms = sem("h_ms")
        self.h_rms = sem("h_rms")
        self.num_copied = sem("num_copied")
        self.qk_ready = sem("qk_ready")
        self.exponents_ready = sem("exponents_ready")
        self.exp_ready = sem("exp_ready")
        self.w_ready = sem("w_ready")
        self.num_prompt = sem("num_prompt")
        self.k_turned = sem("k_turned")
        self.wv_ready = sem("wv_ready")
        self.prompt_state = sem("prompt_state")
        self.state_turned = sem("state_turned")
        self.state_turned_copied = sem("state_turned_copied")
        self.num_sample = sem("num_sample")
        self.update_ready = sem("update_ready")
        self.q_squared = sem("q_squared")
        self.q_summed = sem("q_summed")
        self.q_rms = sem("q_rms")
        self.q_cols = sem("q_cols")
        self.q_wide = sem("q_wide")
        self.q_spread = sem("q_spread")
        self.q_normed = sem("q_normed")
        self.ma_scores = sem("ma_scores")
        self.ma_max = sem("ma_max")
        self.ma_exp = sem("ma_exp")
        self.ma_p = sem("ma_p")
        self.ma_turned = sem("ma_turned")
        self.ma_pt = sem("ma_pt")
        self.ma_out = sem("ma_out")
        self.ma_out_hi = sem("ma_out_hi")
        self.ma_out_lo = sem("ma_out_lo")
        self.ms_qz = sem("ms_qz")
        self.ms_turned = sem("ms_turned")
        self.ms_kt = sem("ms_kt")
        self.ms_scores = sem("ms_scores")
        self.ms_max = sem("ms_max")
        self.ms_exp = sem("ms_exp")
        self.ms_p = sem("ms_p")
        self.ms_pturned = sem("ms_pturned")
        self.ms_pt = sem("ms_pt")
        self.ms_out = sem("ms_out")
        self.ks_loaded0 = sem("ks_loaded0")
        self.ks_loaded1 = sem("ks_loaded1")
        self.ks_loaded2 = sem("ks_loaded2")
        self.ks_loaded3 = sem("ks_loaded3")
        self.vs_loaded = sem("vs_loaded")
        self.mix_turned = sem("mix_turned")
        self.mix_hi = sem("mix_hi")
        self.mix_lo = sem("mix_lo")
        self.k_ready = sem("k_ready")
        self.kt_turned = sem("kt_turned")
        self.kt_copied = sem("kt_copied")
        self.kn_padded = sem("kn_padded")
        self.k_squared = sem("k_squared")
        self.k_ms = sem("k_ms")
        self.k_rms = sem("k_rms")
        self.kv_stored = sem("kv_stored")
        self.z_ready = sem("z_ready")
        self.z_read = sem("z_read")
        self.a_ready = sem("a_ready")
        self.a_turned = sem("a_turned")
        self.at_ready = sem("at_ready")
        self.stick_out = sem("stick_out")
        self.stick_hi = sem("stick_hi")
        self.stick_lo = sem("stick_lo")
        self.vp_loaded = sem("vp_loaded")
        self.table_loaded = sem("table_loaded")
        self.keys_loaded0 = sem("keys_loaded0")
        self.keys_loaded1 = sem("keys_loaded1")
        self.values_loaded0 = sem("values_loaded0")
        self.values_loaded1 = sem("values_loaded1")
        self.kpg_turned = sem("kpg_turned")
        self.kpt_ready = sem("kpt_ready")
        self.qzb_ready = sem("qzb_ready")
        self.zs_ready = sem("zs_ready")
        self.zs_read = sem("zs_read")
        self.as_ready = sem("as_ready")
        self.as_turned = sem("as_turned")
        self.ats_ready = sem("ats_ready")
        self.sb_out = sem("sb_out")
        self.sb_hi = sem("sb_hi")
        self.sb_lo = sem("sb_lo")


class MemoryBuffers:

    def __init__(self, normed, qn, e, pt, qz, ks, vs, kt):
        self.normed = normed
        self.qn, self.e, self.pt, self.qz, self.ks, self.vs, self.kt = qn, e, pt, qz, ks, vs, kt


def build(nc, I, O):
    ctx = ExitStack()
    with ctx:
        def sb(name, shape, dt=F32, scope=ctx):
            return scope.enter_context(nc.sbuf_tensor(name, shape, dt))

        def sem(name):
            return ctx.enter_context(nc.semaphore(name))

        S = Semaphores(sem)
        raw_loaded = (S.raw_loaded0, S.raw_loaded1)
        region_free = (S.region_free0, S.region_free1)

        psum = ctx.enter_context(nc.psum_tensor("psum", [P, 8, 512], F32))
        flat = psum[:, :, :].rearrange("p b n -> p (b n)")

        def region(j):
            return psum[:, 4 * j:4 * j + 4, :]

        x_t = sb("x_t", [P, KD, TOK])
        raw = [sb(f"raw{j}", [P, SLOT]) for j in range(2)]
        whi, wlo, spare_parts = [], [], []
        for parts, name in ((whi, "whi"), (wlo, "wlo")):
            parts.append(sb(f"{name}0", [P, SLOT], F32R))
            spare = ExitStack()
            spare_parts.append(sb(f"spare_{name}", [P, SLOT], scope=spare))
            spare.close()
            parts.append(sb(f"{name}1", [P, SLOT], F32R))
        spare_hi, spare_lo = spare_parts
        over = ExitStack()
        e_all = sb("e_all", [P, 1472], scope=over)
        w_all = sb("w_all", [P, 1408], scope=over)
        k_nat = sb("k_nat", [P, TT, DA], scope=over)
        wv = sb("wv", [P, 4, DA], scope=over)
        wv_b = sb("wv_b", [NSA, NB * DA], scope=over)
        h_nat = sb("h_nat", [P, TT, DA], scope=over)
        gh_b = sb("gh_b", [P, D_MAIN], scope=over)
        qm_a = sb("qm_a", [P, 2, TOK], scope=over)
        over.close()
        h_sq = w_all[:, 0:TT * DA].rearrange("p (t n) -> p t n", t=TT)
        act_hi = sb("act_hi", [P, KD, TOK], F32R)
        act_lo = sb("act_lo", [P, KD, TOK], F32R)
        sumsq = sb("sumsq", [P, TOK])
        rinv = sb("rinv", [P, TOK])
        tmp = [sb(f"tmp{j}", [P, TOK]) for j in range(2)]
        sqt = [sb(f"sqt{j}", [P, TOK]) for j in range(2)]
        mk_t = [sb(f"mk_t{l}", [P, 2, M]) for l in range(2)]
        mv = [sb(f"mv{l}", [P, 2, M]) for l in range(2)]
        ident = sb("ident", [P, P])
        ones = sb("ones", [P, P])
        vec_t = sb("vec_t", [P, 75])
        cw_t = sb("cw_t", [DH, 80])
        gk_mem = sb("gk_mem", [P, 2, DM])
        mrinv = sb("mrinv", [P, 2])
        small = sb("small", [P, 64])
        eps = sb("eps", [P, 1])
        rcols = sb("rcols", [P, TT])

        def gain(which, l=0):
            at = 8 * {"ffn1": l, "mix": 2 + l, "kv": 4, "mem": 5 + l, "ffn2": 7 + l}[which]
            return vec_t[:, at:at + 8]

        ones_heads = sb("ones_heads", [P, P])
        causal = sb("causal", [P, P])
        causal_b = sb("causal_b", [NSA, NSA])
        own = sb("own", [NSA, NB])
        w_pad = sb("w_pad", [NSA, P])
        before = sb("before", [P, P])
        not_before = sb("not_before", [P, P])
        own_keys = sb("own_keys", [96, 2, NS])
        zero = sb("zero", [P, 1])
        gk_b = sb("gk_b", [P, DB])
        b_all = sb("b_all", [P, HB])
        b_neg = sb("b_neg", [P, HB])
        b_col = sb("b_col", [HB, 1])
        b_rows = sb("b_rows", [96, 2])
        table = sb("table", [1, NB * 2], I32)
        ks_loaded = (S.ks_loaded0, S.ks_loaded1, S.ks_loaded2, S.ks_loaded3)
        state_loaded = (S.state_loaded0, S.state_loaded1, S.state_loaded2, S.state_loaded3)
        state_stored = (S.state_stored0, S.state_stored1, S.state_stored2, S.state_stored3)
        keys_loaded = (S.keys_loaded0, S.keys_loaded1)
        values_loaded = (S.values_loaded0, S.values_loaded1)

        setup = ExitStack()
        x_nat = sb("x_nat", [P, TT, D], scope=setup)
        mem_nat = sb("mem_nat", [P, 2, D], scope=setup)
        mem_t = sb("mem_t", [P, KD, M], scope=setup)
        mem_g = sb("mem_g", [P, KD, M], scope=setup)
        mem_hi = [sb(f"mem_hi{l}", [P, KD, M], F32R, scope=setup) for l in range(2)]
        mem_lo = [sb(f"mem_lo{l}", [P, KD, M], F32R, scope=setup) for l in range(2)]
        vec_rows = sb("vec_rows", [75, P], scope=setup)
        cw_rows = sb("cw_rows", [80, DH], scope=setup)
        pick = sb("pick", [96, HB, NS], scope=setup)
        rep = sb("rep", [HB, 96], scope=setup)
        mk_nat, mk_sq = (x_nat[:, 0, h * 512:(h + 1) * 512].rearrange("p (m n) -> p m n", m=2) for h in range(2))
        mk_out = [x_nat[:, 1, l * 512:(l + 1) * 512].rearrange("p (m n) -> p m n", m=2) for l in range(2)]
        mem_sq = spare_hi[:, 0:D]
        setup.close()

        ffn = ExitStack()
        h_hi = sb("h_hi", [P, max(FF_PARTS), TOK], F32R, scope=ffn)
        h_lo = sb("h_lo", [P, max(FF_PARTS), TOK], F32R, scope=ffn)
        sg = [sb(f"sg{j}", [P, TOK], scope=ffn) for j in range(2)]
        h_raw = [sb(f"h_raw{j}", [P, TOK], scope=ffn) for j in range(2)]
        ffn.close()
        NC, NG = 8, 4

        def carried(i):
            slot = i % NC
            at = 2 * DA * (slot % 4)
            return spare_parts[slot // 4][0:DH, at:at + 2 * DA].rearrange("p (e d) -> p e d", e=2)

        mla = ExitStack()
        rows_t = sb("rows_t", [P, TOK + NSA], scope=mla)
        tails = sumsq[0:DH, 0:16 * 27].rearrange("p (k t) -> p k t", k=16)
        carry_all = sqt[0][0:DH, 0:HA * NSA].rearrange("p (h n) -> p h n", h=HA)
        hist = sqt[1][0:DH, 0:16 * 24].rearrange("p (k t) -> p k t", k=16)
        decay_b = sb("decay_b", [NB, HA], scope=mla)
        n_t = sb("n_t", [DH, 2, NB * HA], scope=mla)
        gate_bias = sb("gate_bias", [36, 1], scope=mla)
        m0_rows = sb("m0_rows", [HA, NB], scope=mla)
        w_end_b = sb("w_end_b", [NSA, NB], scope=mla)
        v_nat = sb("v_nat", [P, TT, HA, DA + 1], scope=mla)
        o_nat = sb("o_nat", [P, TT, HA, DA], scope=mla)
        mla_qk = ExitStack()
        qk = sb("qk", [DH, 16, TOK], scope=mla_qk)
        mla_cb = ExitStack()
        cb = [sb(f"cb{j}", [DH, 2, 3 + NPR + NB * 11], scope=mla_cb) for j in range(2)]
        mla_cb.close()
        mla_c = ExitStack()
        turned = sb("turned", [DH, 2, 2, DA + 1], scope=mla_c)
        cols = sb("cols", [P, TT, 68], scope=mla_c)
        mla_c.close()
        mla_qk.close()
        hist_nat = qk[0:24, :, :].rearrange("p k n -> p (k n)")[:, 0:1536]
        n_nat = qk[0:32, :, :].rearrange("p k n -> p (k n)")[:, 1536:1728]
        keep_rows, cut_rows = tmp
        o_flat = o_nat[:, :, :, :].rearrange("p t h d -> p t (h d)")

        def mem_scope(scope, l):
            return MemoryBuffers(
                normed=2 + 8 * l,
                qn=sb(f"qn{l}", [P, 2, TOK], scope=scope),
                e=(sb(f"ma_e{l}", [P, HM, M], scope=scope), spare_hi[:, 0:1024].rearrange("p (h m) -> p h m", h=HM)),
                pt=(sb(f"ma_pt{l}", [P, 8, P], scope=scope), spare_hi[:, 1024:2048].rearrange("p (x n) -> p x n", x=8)),
                qz=sb(f"ma_qz{l}", [P, 2, NB, 32], scope=scope),
                ks=sb(f"ma_ks{l}", [P, 4, 2, M], scope=scope), vs=sb(f"ma_vs{l}", [P, NB, 2, M], scope=scope),
                kt=sb(f"ma_kt{l}", [P, 2, 2, M], scope=scope))

        ma_scope = ExitStack()
        MA = mem_scope(ma_scope, 0)
        ma_scope.close()
        mla.close()

        kvs = ExitStack()
        kn = sb("kn", [P, TT, D_MAIN], scope=kvs)
        vn = sb("vn", [P, TT, D_MAIN], scope=kvs)
        ksq = sb("ksq", [P, TT, 256], scope=kvs)
        kvs.close()
        kts = ExitStack()
        sb("below_kt", [P, 16512], scope=kts)
        kt_b = sb("kt_b", [P, 6, TOK], scope=kts)
        kts.close()

        mb = ExitStack()
        qb_t = sb("qb_t", [P, 6, TOK], scope=mb)
        vpg0 = sb("vpg0", [P, 2, D_MAIN], scope=mb)
        mb_mem = ExitStack()
        MB = mem_scope(mb_mem, 1)
        mb_mem.close()
        mb_p = ExitStack()
        vp = sb("vp", [P, 4, D_MAIN], scope=mb_p)
        take = [sb(f"take{j}", [P, 1280], scope=mb_p) for j in range(2)]
        keep = [sb(f"keep{j}", [P, 1280], scope=mb_p) for j in range(2)]
        rest = sb("rest", [P, 1280], scope=mb_p)
        a_t = sb("a_t", [P, 1280], scope=mb_p)
        vnew0 = sb("vnew0", [NS, D_MAIN], scope=mb_p)
        mb_p.close()
        mb_s = ExitStack()
        kpg = [w[:, 0:2 * D_MAIN].rearrange("p (g n) -> p g n", g=2) for w in spare_parts]
        vpg = [vpg0, sb("vpg1", [P, 2, D_MAIN], scope=mb_s)]
        vnew = [vnew0, sb("vnew1", [NS, D_MAIN], scope=mb_s)]
        kpt = sb("kpt", [P, 6, PAST], scope=mb_s)
        qzb = [sb(f"qzb{j}", [P, 680], scope=mb_s) for j in range(2)]
        takes, keeps, rests = (sb(n, [96, PAST + NS], scope=mb_s) for n in ("takes", "keeps", "rests"))
        a_ts = sb("a_ts", [P, 288], scope=mb_s)
        mb_s.close()
        mb.close()

        y_scope = ExitStack()
        y_nat = sb("y_nat", [P, TT, D], scope=y_scope)
        y_scope.close()

        def weights(j, shape, cols=None):
            k, n = shape
            return [w[j][:, 0:k * n].rearrange("p (k n) -> p k n", k=k) for w in (whi, wlo)]

        def load(sp, n, j, src, dst):
            if not isinstance(n, int) or n >= 2:
                sp.wait_ge(S.lo_ready, n - 1)
            half = dst.shape[1] // 2
            for part in (slice(0, half), slice(half, 2 * half)):
                sp.dma_start(dst[:, part, :], src[:, part, :]).then_inc(raw_loaded[j], 16)

        def split_hi(act, n, j):
            if isinstance(n, int) and n >= N_TILES:
                return
            act.wait_ge(raw_loaded[j], (n - j) * 16 + 32)
            if not isinstance(n, int) or n >= 2:
                act.wait_ge(S.tile_done, n - 1)
            act.activation(whi[j][:, :], raw[j][:, :], ACT.Copy).then_inc(S.hi_ready, 1)

        def split_lo(dve, n, j):
            if isinstance(n, int) and n >= N_TILES:
                return
            dve.wait_ge(S.hi_ready, n + 1)
            dve.tensor_tensor(wlo[j][:, :], raw[j][:, :], whi[j][:, :].bitcast(F32), ALU.subtract) \
                .then_inc(S.lo_ready, 1)
            dve.wait_ge(S.lo_ready, n + 1)

        def start_tile(pe, n, j):
            pe.wait_ge(S.lo_ready, n + 1)
            if not isinstance(n, int) or n >= 2:
                pe.wait_ge(region_free[j], (n - j) // 2)

        def product(pe, n, j, w_hi, w_lo, a_hi, a_lo, chunks, outs, width, ready=None):
            start_tile(pe, n, j)
            last = None
            for k in range(chunks):
                if ready is not None and k < ready[2]:
                    pe.wait_ge(ready[0], ready[1] + k + 1)
                for m in range(outs):
                    cols = slice(m * width, (m + 1) * width)
                    for step, (w, a) in enumerate(((w_hi, a_hi), (w_hi, a_lo), (w_lo, a_hi))):
                        for h in range(2):
                            last = pe.matmul(psum[0:width, 4 * j + 2 * m + h, 0:HALF], w[:, k, cols],
                                             a[:, k, h * HALF:(h + 1) * HALF],
                                             start=(k == 0 and step == 0), stop=(k == chunks - 1 and step == 2))
            last.then_inc(S.tile_done, 1)

        def token_tiles():
            return [(t, t * P, P if t < 4 else NSA) for t in range(TT)]

        def natural_product(pe, n, j, w_hi, w_lo, width, ready=None):
            start_tile(pe, n, j)
            last = None
            for t, at, rows in token_tiles():
                out = region(j)[0:rows, t // 2, (t % 2) * 256:(t % 2) * 256 + width]
                for k in range(KD):
                    if ready is not None and t == 0:
                        pe.wait_ge(ready[0], ready[1] + k + 1)
                    for step, (w, a) in enumerate(((w_hi, act_hi), (w_hi, act_lo), (w_lo, act_hi))):
                        last = pe.matmul(out, a[:, k, at:at + rows], w[:, k, :],
                                         start=(k == 0 and step == 0), stop=(k == KD - 1 and step == 2))
            last.then_inc(S.tile_done, 1)

        def natural_view(j, width):
            return flat[:, 2048 * j:2048 * j + 5 * 256].rearrange("p (t n) -> p t n", n=256)[:, :, 0:width]


        def setup_sp(sp):
            sp.dma_start(mem_nat[:, :, :], I["mem_prompt"].rearrange("a (t p) d -> p (a t) d", p=P)).then_inc(S.mem_loaded, 16)
            sp.dma_start(x_nat[:, 0:4, :], I["x_prompt"].rearrange("a (t p) d -> p (a t) d", p=P)).then_inc(S.x_loaded, 16)
            sp.dma_start(x_nat[0:NSA, 4, :], I["x_sample"].rearrange("b t d -> (b t) d")).then_inc(S.x_loaded, 16)

        def small_inputs(act):
            act.dma_start(vec_rows[0:16, :], I["g_ffn1"].rearrange("l (c p) -> (l c) p", p=P)).then_inc(S.inputs_loaded, 16)
            act.dma_start(vec_rows[16:32, :], I["g_mix"].rearrange("l (c p) -> (l c) p", p=P)).then_inc(S.inputs_loaded, 16)
            act.dma_start(vec_rows[32:40, :], I["g_kv"].rearrange("(c p) -> c p", p=P)).then_inc(S.inputs_loaded, 16)
            act.dma_start(vec_rows[40:56, :], I["g_mem"].rearrange("l (c p) -> (l c) p", p=P)).then_inc(S.inputs_loaded, 16)
            act.dma_start(vec_rows[56:72, :], I["g_ffn2"].rearrange("l (c p) -> (l c) p", p=P)).then_inc(S.inputs_loaded, 16)
            for r in range(2):
                half = slice(r * 64, r * 64 + 64)
                act.dma_start(vec_rows[72:74, half], I["g_q_mem"]).then_inc(S.inputs_loaded, 16)
                act.dma_start(vec_rows[74:75, half], I["g_q_b"]).then_inc(S.inputs_loaded, 16)
            act.dma_start(cw_rows[0:64, :], I["conv_w_a"].rearrange("a j (c p) -> (a j c) p", p=DH)).then_inc(S.inputs_loaded, 16)
            act.dma_start(cw_rows[64:80, :], I["conv_b_a"].rearrange("a (c p) -> (a c) p", p=DH)).then_inc(S.inputs_loaded, 16)
            act.dma_start(gk_mem[:, :, :], I["g_k_mem"].partition_broadcast(P)).then_inc(S.inputs_loaded, 16)
            act.dma_start(gk_b[:, :], I["g_k_b"].partition_broadcast(P)).then_inc(S.inputs_loaded, 16)
            act.dma_start(b_all[:, :], I["b_sb"][0].partition_broadcast(P)).then_inc(S.inputs_loaded, 16)
            act.dma_start(b_col[:, :], I["b_sb"].rearrange("a h -> h a")).then_inc(S.inputs_loaded, 16)
        SETUP_LOADS = 16 * 15

        def setup_pool(pool, c):
            pool.memset(ones[:, :], 1.0)
            pool.memset(eps[:, :], EPS)
            pool.memset(zero[:, :], 0.0)
            pool.memset(w_pad[:, :], 0.0)
            pool.memset(ones_heads[:, :], 0.0)
            for t, v in ((ident, 0.0), (causal, 0.0), (causal_b, 0.0), (own, 1.0), (before, 1.0), (not_before, 0.0), (rep, 0.0)):
                pool.memset(t[:, :], v)
            pool.memset(pick[:, :, :], 1.0).then_inc(S.pool_step, 1)
            pool.wait_ge(S.pool_step, c("pool_step"))
            for r in range(2):
                pool.memset(ones_heads[64 * r:64 * r + 64, 64 * r:64 * r + 64], 1.0).then_inc(S.pool_step, 1)
                pool.wait_ge(S.pool_step, c("pool_step"))

            def select(t, op, fill, base, pattern, row):
                return pool.affine_select(out=t, in_=t, compare_op=op, fill=fill, base=base, pattern=pattern,
                                          channel_multiplier=row)
            seq = causal_b[:, :].rearrange("p (b t) -> p b t", b=NB)
            select(causal[:, :], ALU.is_ge, NEG, 0, [[1, P]], -1)
            select(seq, ALU.is_ge, NEG, 0, [[8, NB], [1, NS]], -1)
            select(own[:, :], ALU.is_ge, 0.0, 0, [[-8, NB]], 1)
            select(before[:, :], ALU.is_ge, 0.0, -1, [[-1, P]], 1)
            select(not_before[:, :], ALU.is_ge, 1.0, -1, [[-1, P]], 1)
            select(pick[:, :, :], ALU.is_ge, 0.0, -1, [[-8, HB], [-1, NS]], 1)
            select(rep[:, :].rearrange("p (h t) -> p h t", t=NS), ALU.not_equal, 1.0, 0, [[-1, HB], [0, NS]], 1)
            select(ident[:, :], ALU.not_equal, 1.0, 0, [[-1, P]], 1).then_inc(S.pool_step, 1)
            pool.wait_ge(S.pool_step, c("pool_step"))
            select(seq, ALU.is_ge, NEG, 0, [[-8, NB], [0, NS]], 1)
            select(own[:, :], ALU.is_ge, 0.0, 7, [[8, NB]], -1)
            select(pick[:, :, :], ALU.is_ge, 0.0, 7, [[8, HB], [0, NS]], -1).then_inc(S.consts_ready, 1)

        SETUP_BANKS = (2, 4, 0, 6, 0, 2, 4, 6)

        def setup_pe(pe):
            pe.wait_ge(S.consts_ready, 1)
            for g, bank in enumerate(SETUP_BANKS):
                if g == 2:
                    pe.wait_ge(S.inputs_loaded, SETUP_LOADS)
                    pe.transpose(psum[0:P, 0, 0:75], vec_rows[:, :], ident[0:75, 0:75])
                    pe.matmul(psum[0:96, 1, 128:129], rep[:, :], b_col[:, :], start=True, stop=True)
                    pe.transpose(psum[0:DH, 1, 0:80], cw_rows[:, :], ident[0:80, 0:80]).then_inc(S.setup_turned, 1)
                    continue
                if g < 2:
                    pe.wait_ge(S.mem_loaded, 16)
                    src, rows = mem_nat[:, g, :], P
                else:
                    pe.wait_ge(S.x_loaded, 32)
                    rows = P if g < 7 else NSA
                    src = x_nat[0:rows, g - 3, :]
                if g >= 4:
                    pe.wait_ge(S.setup_copied, SETUP_BANKS.index(bank) + 1)
                for k in range(KD):
                    at = 512 * bank + k * rows
                    last = pe.transpose(flat[:, at:at + rows], src[:, k * P:(k + 1) * P], ident[0:rows, 0:rows])
                last.then_inc(S.setup_turned, 1)

        def setup_dve(dve, c):
            def turned(g, dst, n):
                at = 512 * SETUP_BANKS[g]
                dve.wait_ge(S.setup_turned, g + 1)
                dve.tensor_copy(dst, flat[:, at:at + KD * n].rearrange("p (k n) -> p k n", k=KD)).then_inc(S.setup_copied, 1)

            def x_turned(t):
                n = P if t < 4 else NSA
                turned(3 + t, x_t[:, :, t * P:t * P + n], n)

            def memory_gained(l):
                dve.tensor_tensor(mem_g[:, :, :], mem_t[:, :, :],
                                  gain("mem", l).unsqueeze(2).broadcast_to([P, KD, M]), ALU.mult) \
                    .then_inc(S.mem_scaled, 1)

            def memory_lo(l):
                dve.wait_ge(S.mem_hi, l + 1)
                dve.tensor_tensor(mem_lo[l][:, :, :], mem_g[:, :, :], mem_hi[l][:, :, :].bitcast(F32), ALU.subtract) \
                    .then_inc(S.mem_split, 1)

            for t in range(2):
                turned(t, mem_t[:, :, t * P:(t + 1) * P], P)
            dve.wait_ge(S.setup_turned, 3)
            dve.wait_ge(S.inputs_loaded, SETUP_LOADS)
            dve.tensor_copy(vec_t[:, :], psum[:, 0, 0:75])
            dve.tensor_scalar(b_rows[:, 0:1], psum[0:96, 1, 128:129], 1.0, None, ALU.mult)
            dve.tensor_scalar(b_rows[:, 1:2], psum[0:96, 1, 128:129], -1.0, None, ALU.mult)
            dve.tensor_scalar(b_neg[:, :], b_all[:, :], -1.0, None, ALU.mult)
            dve.tensor_copy(cw_t[:, :], psum[0:DH, 1, 0:80]).then_inc(S.setup_copied, 1)
            dve.wait_ge(S.setup_copied, 3)
            memory_gained(0)
            for t in range(2):
                x_turned(t)
            memory_lo(0)
            split_lo(dve, 0, 0)
            for t in range(2, TT):
                x_turned(t)
            split_lo(dve, 1, 1)
            dve.wait_ge(S.mem_split, 1)
            memory_gained(1)
            dve.wait_ge(S.mem_rms_ready, 1)
            dve.reciprocal(mrinv[:, :], mrinv[:, :]).then_inc(S.dve_step, 1)
            dve.wait_ge(S.dve_step, c("dve_step"))
            memory_lo(1)
            sum_squares_start(dve, 0)
            for k in range(KD):
                sum_square(dve, k % 2, 0, k)
            dve.tensor_reduce(own_keys[:, 0, :], pick[:, :, :].rearrange("p h j -> p j h"), AX, ALU.add).then_inc(S.dve_step, 1)
            dve.wait_ge(S.dve_step, c("dve_step"))
            dve.tensor_scalar(own_keys[:, 1, :], own_keys[:, 0, :], -1.0, 1.0, ALU.mult, ALU.add)

        def setup_act(act):
            act.wait_ge(S.mem_loaded, 16)
            for t in range(2):
                act.activation(mem_sq, mem_nat[:, t, :], ACT.Square, accum_out=mrinv[:, t:t + 1]).then_inc(S.mem_squared, 1)
                act.wait_ge(S.mem_squared, t + 1)
            act.wait_ge(S.consts_ready, 1)
            act.activation(mrinv[:, :], mrinv[:, :], ACT.Sqrt, scale=1.0 / D, bias=eps[:, :]).then_inc(S.mem_rms_ready, 1)
            for l in range(2):
                act.wait_ge(S.mem_scaled, l + 1)
                act.activation(mem_hi[l][:, :, :], mem_g[:, :, :], ACT.Copy).then_inc(S.mem_hi, 1)
                if l == 0:
                    split_hi(act, 0, 0)
                    split_hi(act, 1, 1)
            act.wait_ge(S.setup_copied, 8)
            for k in range(KD):
                square(act, k % 2, k, 0, k)

        def sum_squares_start(dve, g):
            if g:
                dve.wait_ge(S.sumsq_ready, g)
            dve.memset(sumsq[:, :], 0.0).then_inc(S.sum_done, 1)

        def square(act, slot, chunk, g, nth):
            if isinstance(nth, int) and nth >= 2:
                act.wait_ge(S.sum_done, 9 * g + nth)
            act.activation(sqt[slot][:, :], x_t[:, chunk, :], ACT.Square).then_inc(S.sq_ready, 1)

        def sum_square(dve, slot, g, nth):
            dve.wait_ge(S.sq_ready, 8 * g + nth + 1)
            dve.wait_ge(S.sum_done, 9 * g + nth + 1)
            dve.tensor_tensor(sumsq[:, :], sumsq[:, :], sqt[slot][:, :], ALU.add).then_inc(S.sum_done, 1)

        def halves(ap):
            return ap.rearrange("p (h n) -> p h n", h=2)

        def rinv_at(g):
            return 2048 if g else 3072

        def norm_cols(g):
            return flat[:, rinv_at(g) + 640:rinv_at(g) + 640 + TT]

        def norm_pe(pe, g, n_next):
            pe.wait_ge(S.sum_done, 9 * g + 9)
            if g:
                pe.wait_ge(S.region_free1, n_next // 2)
            for t in range(TT):
                at = t * P if t < 4 else TOK - P
                last = pe.matmul(norm_cols(g)[:, t:t + 1], sumsq[:, at:at + P], ones[:, 0:1], start=True, stop=True)
            last.then_inc(S.sumsq_ready, 1)
            pe.wait_ge(S.rinv_cols, g + 1)
            for t in range(TT):
                n = P if t < 4 else NSA
                last = pe.matmul(flat[:, rinv_at(g) + t * P:rinv_at(g) + t * P + n], rcols[:, t:t + 1].broadcast_to([P, P]),
                                 ident[:, P - n:P], start=True, stop=True)
            last.then_inc(S.rinv_spread, 1)

        def norm_act(act, g, nth, again):
            if not again:
                act.activation(small[:, 63:64], eps[:, :], ACT.Sqrt)
                act.wait_ge(S.sumsq_ready, g + 1)
                act.activation(rcols[:, :], norm_cols(g), ACT.Sqrt, scale=1.0 / D, bias=eps[:, :]).then_inc(S.rms_ready, 1)
            for k in range(KD):
                act.wait_ge(S.xn_ready, 8 * nth + k + 1)
                act.activation(act_hi[:, k, :], tmp[k % 2][:, :], ACT.Copy).then_inc(S.nh_ready, 1)

        def norm_dve(dve, g, nth, again, gains, keep=False):
            scale = rinv[:, :] if again or keep else flat[:, rinv_at(g):rinv_at(g) + TOK]
            if not again:
                dve.wait_ge(S.rms_ready, g + 1)
                dve.reciprocal(rcols[:, :], rcols[:, :]).then_inc(S.rinv_cols, 1)
                dve.wait_ge(S.rinv_spread, g + 1)
                if keep:
                    dve.tensor_copy(rinv[:, :], flat[:, rinv_at(g):rinv_at(g) + TOK]).then_inc(S.rinv_kept, 1)
                    dve.wait_ge(S.rinv_kept, 1)

            def lo(k):
                dve.wait_ge(S.nh_ready, 8 * nth + k + 1)
                dve.tensor_tensor(act_lo[:, k, :], tmp[k % 2][:, :], act_hi[:, k, :].bitcast(F32), ALU.subtract) \
                    .then_inc(S.nl_ready, 1)
            for k in range(KD):
                if k >= 2:
                    lo(k - 2)
                    dve.wait_ge(S.nl_ready, 8 * nth + k - 1)
                dve.scalar_tensor_tensor(tmp[k % 2][:, :], x_t[:, k, :], gains[:, k:k + 1], scale,
                                         ALU.mult, ALU.mult).then_inc(S.xn_ready, 1)
            lo(KD - 2)
            lo(KD - 1)

        def mem_sp(sp):
            for n in range(4):
                src = I["w_mem_kv"][n // 2].rearrange("(k p) (s n) -> p k s n", p=P, s=2)[:, :, n % 2, :]
                load(sp, n, n % 2, src, raw[n % 2][:, :].rearrange("p (k n) -> p k n", k=KD))

        def mem_pe(pe):
            def turn_keys(l):
                pe.wait_ge(S.mk_ready, l + 1)
                for m in range(2):
                    for pair in range(2):
                        last = pe.transpose(psum[:, 2, (2 * pair + m) * P:(2 * pair + m + 1) * P],
                                            mk_out[l][:, m, pair * P:(pair + 1) * P], ident[:, :])
                last.then_inc(S.mkt_ready, 1)

            for n in range(4):
                j, l = n % 2, n // 2
                if n % 2 == 0:
                    pe.wait_ge(S.mem_split, l + 1)
                if n < 2:
                    pe.wait_ge(S.setup_copied, (5, 8)[n])
                start_tile(pe, n, j)
                w_hi, w_lo = weights(j, (KD, M))
                for m in range(2):
                    for k in range(KD):
                        for step, (w, a) in enumerate(((w_hi, mem_hi), (w_hi, mem_lo), (w_lo, mem_hi))):
                            last = pe.matmul(psum[:, 4 * j + m, 0:M], a[l][:, k, m * P:(m + 1) * P], w[:, k, :],
                                             start=(k == 0 and step == 0), stop=(k == KD - 1 and step == 2))
                last.then_inc(S.tile_done, 1)
                if n == 1:
                    norm_pe(pe, 0, BASE_FFN[0])
                if n == 2:
                    turn_keys(0)
            pe.wait_ge(S.mkt_copied, 1)
            turn_keys(1)
            pe.wait_ge(S.mkt_copied, 2)

        def mem_act(act):
            for n in range(4):
                if n == 1:
                    split_hi(act, 2, 0)
                    split_hi(act, 3, 1)
                    norm_act(act, 0, 0, False)
                if n == 3:
                    split_hi(act, 4, 0)
                if n % 2 == 0:
                    l = n // 2
                    act.wait_ge(region_free[0], l + 1)
                    act.activation(mk_sq, mk_nat, ACT.Square).then_inc(S.mk_sq, 1)
                    act.wait_ge(S.mk_ms, l + 1)
                    act.activation(small[:, 0:8], small[:, 0:8], ACT.Sqrt, scale=1.0 / DM, bias=eps[:, :]).then_inc(S.mk_rms, 1)

        def mem_dve(dve, c):
            def copy_keys(l):
                dve.wait_ge(S.mkt_ready, l + 1)
                dve.tensor_copy(mk_t[l][:, :, :].rearrange("p a m -> p (a m)"), psum[:, 2, :]).then_inc(S.mkt_copied, 1)

            def step(ins):
                ins.then_inc(S.dve_step, 1)
                dve.wait_ge(S.dve_step, c("dve_step"))

            for n in range(4):
                j, l = n % 2, n // 2
                if n == 1:
                    split_lo(dve, 2, 0)
                if n == 3:
                    split_lo(dve, 4, 0)
                dve.wait_ge(S.tile_done, n + 1)
                scale = mrinv[:, :].unsqueeze(2).broadcast_to([P, 2, M])
                if n % 2:
                    dve.tensor_tensor(mv[l][:, :, :], psum[:, 4 * j:4 * j + 2, 0:M], scale, ALU.mult).then_inc(region_free[j], 1)
                    if n == 1:
                        split_lo(dve, 3, 1)
                        norm_dve(dve, 0, 0, False, gain("ffn1", 0))
                    continue
                dve.tensor_tensor(mk_nat, psum[:, 4 * j:4 * j + 2, 0:M], scale, ALU.mult) \
                    .then_inc(region_free[j], 1)
                dve.wait_ge(region_free[j], l + 1)
                nat = mk_nat.rearrange("p m (h d) -> p (m h) d", d=DM)
                out = mk_out[l].rearrange("p m (h d) -> p (m h) d", d=DM)
                dve.wait_ge(S.mk_sq, l + 1)
                dve.tensor_reduce(small[:, 0:8], mk_sq.rearrange("p m (h d) -> p (m h) d", d=DM), AX, ALU.add) \
                    .then_inc(S.mk_ms, 1)
                dve.wait_ge(S.mk_rms, l + 1)
                step(dve.reciprocal(small[:, 0:8], small[:, 0:8]))
                step(dve.tensor_tensor(out, nat, small[:, 0:8].unsqueeze(2).broadcast_to([P, 8, DM]), ALU.mult))
                dve.tensor_tensor(out, out, gk_mem[:, l, :].unsqueeze(1).broadcast_to([P, 8, DM]), ALU.mult) \
                    .then_inc(S.mk_ready, 1)
                if l:
                    copy_keys(0)
            copy_keys(1)

        def mem_pool(pool, c):
            for l in range(2):
                pool.wait_ge(S.mk_ready, l + 1)
                pool.dma_start(O["mem_k_prompt"][l, 0].rearrange("(m p) h d -> p m (h d)", p=P), mk_out[l]).then_inc(S.stored, 16)
                pool.wait_ge(S.region_free1, l + 1)
                pool.dma_start(O["mem_v_prompt"][l, 0].rearrange("(m p) h d -> p m (h d)", p=P), mv[l][:, :, :]).then_inc(S.stored, 16)

        def ffn_weights(q):
            l = q // 2
            return ((I["w_ffn1_up"], I["w_ffn1_down"]), (I["w_ffn2_up"], I["w_ffn2_down"]))[q % 2][0][l], \
                ((I["w_ffn1_up"], I["w_ffn1_down"]), (I["w_ffn2_up"], I["w_ffn2_down"]))[q % 2][1][l]

        def ffn_parts(q):
            n, first = BASE_FFN[q], 0
            for part, chunks in enumerate(FF_PARTS):
                yield part, n, n + chunks, chunks, first, q * sum(FF_PARTS) + first
                n += chunks + KD
                first += chunks

        def ffn_sp(sp, q):
            up, down = ffn_weights(q)
            up_view = up.rearrange("(k p) (s n) -> p k s n", p=P, s=2)
            for part, n_up, n_down, chunks, first, _ in ffn_parts(q):
                with sp.Fori(0, chunks // 2) as i:
                    for j in range(2):
                        sp.wait_ge(S.lo_ready, n_up + 2 * i + (j - 1))
                        dst = raw[j][:, :].rearrange("p (k s n) -> p k s n", k=KD, s=2)
                        for s in range(2):
                            sp.dma_start(dst[:, :, s, :], up_view[:, :, s, bass.ds((2 * i + (first + j)) * P, P)]) \
                                .then_inc(raw_loaded[j], 16)
                down_view = down.rearrange("(k p) n -> p k n", p=P)[:, first:first + chunks, :]
                with sp.Fori(0, KD // 2) as i:
                    for j in range(2):
                        load(sp, n_down + 2 * i + j, j, down_view[:, :, bass.ds((2 * i + j) * P, P)],
                             raw[j][:, 0:chunks * P].rearrange("p (k n) -> p k n", k=chunks))

        def ffn_pe(pe, q, nth):
            for part, n_up, n_down, chunks, first, ups in ffn_parts(q):
                with pe.Fori(0, chunks // 2) as i:
                    for j in range(2):
                        w_hi, w_lo = weights(j, (KD, 256))
                        product(pe, n_up + 2 * i + j, j, w_hi, w_lo, act_hi, act_lo, KD, 2, P,
                                ready=(S.nl_ready, 8 * nth, KD))
                with pe.Fori(0, KD // 2) as i:
                    for j in range(2):
                        w_hi, w_lo = weights(j, (chunks, P))
                        product(pe, n_down + 2 * i + j, j, w_hi, w_lo, h_hi, h_lo, chunks, 1, P,
                                ready=(S.hl_ready, ups, chunks))

        def ffn_act(act, q, g):
            for part, n_up, n_down, chunks, first, ups in ffn_parts(q):
                if part == 0 and q % 2 == 0:
                    act.wait_ge(*((S.stored, 64), (S.kv_stored, 64))[q // 2])
                with act.Fori(0, chunks // 2) as i:
                    for j in range(2):
                        n = n_up + 2 * i + j
                        split_hi(act, n + 1, 1 - j)
                        act.wait_ge(S.tile_done, n + 1)
                        act.activation(halves(sg[j][:, :]), region(j)[:, 0:2, 0:HALF], ACT.Silu).then_inc(S.sg_ready, 1)
                        act.wait_ge(region_free[j], n_up // 2 + i + 1)
                        act.activation(h_hi[:, 2 * i + j, :], h_raw[j][:, :], ACT.Copy).then_inc(S.hh_ready, 1)

                def down(i, last=False):
                    for j in range(2):
                        n = n_down + 2 * i + j
                        split_hi(act, n + 1, 1 - j)
                        if part and g is not None:
                            act.wait_ge(region_free[j], n_down // 2 + i + 1)
                            square(act, j, 2 * i + j, g, 2 * i + j)
                if n_down + KD == N_TILES:
                    with act.Fori(0, KD // 2 - 1) as i:
                        down(i)
                    down(KD // 2 - 1)
                else:
                    with act.Fori(0, KD // 2) as i:
                        down(i)

        def ffn_dve(dve, q, g):
            for part, n_up, n_down, chunks, first, ups in ffn_parts(q):
                if part == 0 and q % 2 == 0:
                    dve.wait_ge(*((S.stored, 64), (S.kv_stored, 64))[q // 2])
                with dve.Fori(0, chunks // 2) as i:
                    for j in range(2):
                        n = n_up + 2 * i + j
                        split_lo(dve, n + 1, 1 - j)
                        dve.wait_ge(S.sg_ready, 2 * i + (ups + j + 1))
                        dve.tensor_tensor(halves(h_raw[j][:, :]), halves(sg[j][:, :]), region(j)[:, 2:4, 0:HALF], ALU.mult) \
                            .then_inc(region_free[j], 1)
                        dve.wait_ge(S.hh_ready, 2 * i + (ups + j + 1))
                        dve.tensor_tensor(h_lo[:, 2 * i + j, :], h_raw[j][:, :], h_hi[:, 2 * i + j, :].bitcast(F32),
                                          ALU.subtract).then_inc(S.hl_ready, 1)
                if part and g is not None:
                    sum_squares_start(dve, g)

                def down(i):
                    for j in range(2):
                        n = n_down + 2 * i + j
                        split_lo(dve, n + 1, 1 - j)
                        dve.wait_ge(S.tile_done, n + 1)
                        x = halves(x_t[:, 2 * i + j, :]) if isinstance(i, int) else \
                            x_t[:, 2 * i + j, :].rearrange("p (h n) -> p h n", h=2)
                        dve.scalar_tensor_tensor(x, region(j)[:, 0:2, 0:HALF], 0.5, x, ALU.mult, ALU.add) \
                            .then_inc(region_free[j], 1)
                        if part and g is not None:
                            sum_square(dve, j, g, 2 * i + j)
                if n_down + KD == N_TILES:
                    with dve.Fori(0, KD // 2 - 1) as i:
                        down(i)
                    down(KD // 2 - 1)
                else:
                    with dve.Fori(0, KD // 2) as i:
                        down(i)

        def out_sp(sp, base, l, tiles):
            view = I["w_out"][l].rearrange("(k p) n -> p k n", p=P)
            for t in tiles:
                j = t % 2
                load(sp, base + t, j, view[:, :, t * 256:(t + 1) * 256], raw[j][:, :].rearrange("p (k n) -> p k n", k=KD))

        def out_pe(pe, base):
            for t in range(4):
                w_hi, w_lo = weights(t % 2, (KD, 256))
                product(pe, base + t, t % 2, w_hi, w_lo, act_hi, act_lo, KD, 2, P)

        def out_act(act, base, g):
            for t in range(4):
                n, j = base + t, t % 2
                split_hi(act, n + 1, 1 - j)
                act.wait_ge(region_free[j], n // 2 + 1)
                for m in range(2):
                    square(act, m, 2 * t + m, g, 2 * t + m)

        def out_dve(dve, base, g):
            sum_squares_start(dve, g)
            for t in range(4):
                n, j = base + t, t % 2
                split_lo(dve, n + 1, 1 - j)
                dve.wait_ge(S.tile_done, n + 1)
                for m in range(2):
                    x = halves(x_t[:, 2 * t + m, :])
                    ins = dve.scalar_tensor_tensor(x, region(j)[:, 2 * m:2 * m + 2, 0:HALF], 1.0, x, ALU.mult, ALU.add)
                ins.then_inc(region_free[j], 1)
                for m in range(2):
                    sum_square(dve, m, g, 2 * t + m)

        def end_pe(pe):
            for t, at, rows in token_tiles():
                b = 2 * (t % 4)
                if t == 0:
                    pe.wait_ge(S.region_free0, N_TILES // 2)
                    pe.wait_ge(S.region_free1, N_TILES // 2)
                if t == 4:
                    pe.wait_ge(S.y_copied, 1)
                for k in range(KD):
                    last = pe.transpose(psum[0:rows, b + k // 4, (k % 4) * P:(k % 4 + 1) * P], x_t[:, k, at:at + rows], ident[:, :])
                last.then_inc(S.y_turned, 1)

        def end_dve(dve):
            for t, at, rows in token_tiles():
                b = 2 * (t % 4)
                dve.wait_ge(S.y_turned, t + 1)
                dve.tensor_copy(y_nat[0:rows, t, :], psum[0:rows, b:b + 2, :].rearrange("p b n -> p (b n)")).then_inc(S.y_copied, 1)

        def end_sp(sp):
            view = O["y_prompt"].rearrange("a (t p) d -> t p (a d)", p=P)
            for t, at, rows in token_tiles():
                sp.wait_ge(S.y_copied, t + 1)
                dst = view[t] if t < 4 else O["y_sample"].rearrange("b t d -> (b t) d")
                sp.dma_start(dst, y_nat[0:rows, t, :]).then_inc(S.y_stored, 16)
            sp.wait_ge(S.y_stored, 16 * TT)

        def ina_sp(sp):
            view = I["w_in_a"][0].rearrange("(k p) n -> p k n", p=P)
            for t in range(INA_TILES):
                n, j = BASE_INA + t, t % 2
                if t == 0:
                    sp.wait_ge(S.lo_ready, n - 1)
                    dst = raw[j][:, 0:KD * 64].rearrange("p (k n) -> p k n", k=KD)
                    for r in range(2):
                        sp.dma_start(dst[:, :, 32 * r:32 * r + 4], view[:, :, 4 * D_MAIN + 4 * r:4 * D_MAIN + 4 * r + 4]) \
                            .then_inc(raw_loaded[j], 16)
                elif t < INA_TILES - 1:
                    load(sp, n, j, view[:, :, (t - 1) * DA:t * DA], raw[j][:, 0:KD * DA].rearrange("p (k n) -> p k n", k=KD))
                else:
                    load(sp, n, j, view[:, :, 4 * D_MAIN + 8:4 * D_MAIN + 8 + 256], raw[j][:, :].rearrange("p (k n) -> p k n", k=KD))

        def ina_pe(pe, nth):
            for t in range(INA_TILES):
                n, j = BASE_INA + t, t % 2
                if t == 0:
                    w_hi, w_lo = weights(j, (KD, 64))
                    product(pe, n, j, w_hi[:, :, 0:36], w_lo[:, :, 0:36], act_hi, act_lo, KD, 1, 36, ready=(S.nl_ready, 8 * nth, KD))
                elif t <= 8:
                    if t == 2:
                        pe.wait_ge(S.hist_ready, 1)
                    w_hi, w_lo = weights(j, (KD, DA))
                    product(pe, n, j, w_hi, w_lo, act_hi, act_lo, KD, 2, DH)
                elif t <= 16:
                    w_hi, w_lo = weights(j, (KD, DA))
                    natural_product(pe, n, j, w_hi, w_lo, DA)
                else:
                    w_hi, w_lo = weights(j, (KD, 256))
                    product(pe, n, j, w_hi, w_lo, act_hi, act_lo, KD, 2, P)

        def ina_act(act, c):
            for t in range(INA_TILES):
                n, j = BASE_INA + t, t % 2
                free = n // 2 + 1
                if t != 1:
                    split_hi(act, n + 1, 1 - j)
                if t == 0:
                    split_hi(act, n + 2, j)
                    act.wait_ge(S.gate_abs, 1)
                    act.activation(sqt[1][32:36, :], sqt[1][32:36, :], ACT.Exp, scale=-1.0).then_inc(S.act_step, 1)
                    act.wait_ge(S.act_step, c("act_step"))
                    act.activation(sqt[1][32:36, :], sqt[1][32:36, :], ACT.Ln, bias=ones[32:36, 0:1]).then_inc(S.gate_ln, 1)
                    act.wait_ge(S.gate_m, 1)
                    act.activation(rows_t[64:68, 0:TOK], sqt[0][0:4, :], ACT.Exp, scale=-1.0)
                    act.activation(rows_t[32:36, 0:TOK], sqt[1][0:4, :], ACT.Exp)
                    act.activation(rows_t[96:100, TOK:TOK + NSA], rinv[0:4, 0:NSA], ACT.Exp).then_inc(S.gate_rows, 1)
                elif t <= 8:
                    head = t - 1
                    if t > 2:
                        act.wait_ge(S.conv_ready, head - 1)
                    act.wait_ge(S.tile_done, n + 1)
                    src = region(j)[0:DH, :, 0:HALF].rearrange("p (m h) n -> p m h n", h=2)
                    dst = cb[j]
                    act.activation(dst[:, :, 3:3 + HALF], src[:, :, 0, :], ACT.Copy)
                    act.activation(dst[:, :, 3 + HALF:3 + NPR], src[:, :, 1, 0:NPR - HALF], ACT.Copy)
                    for m in range(2):
                        ins = act.activation(cb_sample(j, m)[:, :, 3:3 + NS],
                                             src[:, m, 1, NPR - HALF:HALF].rearrange("p (b t) -> p b t", b=NB), ACT.Copy)
                    ins.then_inc(region_free[j], 1)
                    act.wait_ge(S.conv_ready, head + 1)
                    for m in range(2):
                        ins = act.activation(qk[:, 2 * head + m, :], tmp[m][0:DH, :], ACT.Silu)
                    ins.then_inc(S.qk_silu, 1)
                else:
                    if t >= 17:
                        break
                    head, is_o = (t - 9) % 4, t >= 13
                    act.wait_ge(S.tile_done, n + 1)
                    src = natural_view(j, DA)
                    if is_o:
                        act.activation(o_nat[:, 0:4, head, :], src[:, 0:4, :], ACT.Sigmoid)
                        act.activation(o_nat[0:NSA, 4, head, :], src[0:NSA, 4, :], ACT.Sigmoid).then_inc(region_free[j], 1)
                    else:
                        act.activation(v_nat[:, 0:4, head, 0:DA], src[:, 0:4, :], ACT.Copy)
                        act.activation(v_nat[0:NSA, 4, head, 0:DA], src[0:NSA, 4, :], ACT.Copy).then_inc(region_free[j], 1)
            act.wait_ge(S.tile_done, n + 1)
            act.activation(qm_a[:, :, :].rearrange("p m (h n) -> p (m h) n", h=2), region(1)[:, :, 0:HALF], ACT.Copy) \
                .then_inc(region_free[1], 1)

        def cb_sample(j, m):
            return cb[j][:, m, 3 + NPR:3 + NPR + NB * 11].rearrange("p (b t) -> p b t", b=NB)

        def ina_dve(dve, c):
            def step(ins):
                ins.then_inc(S.dve_step, 1)
                dve.wait_ge(S.dve_step, c("dve_step"))

            def seg(ap):
                return ap.rearrange("p (b t) -> p b t", b=NB)

            for t in range(INA_TILES):
                n, j = BASE_INA + t, t % 2
                if t != 1:
                    split_lo(dve, n + 1, 1 - j)
                if t == 0:
                    gates, lf, b, am, big = sqt[0], sqt[1], rinv, sqt[1], sumsq
                    dve.wait_ge(S.consts_ready, 2)
                    dve.wait_ge(S.a_loaded, A_LOADS)
                    dve.wait_ge(S.tile_done, n + 1)
                    dve.tensor_scalar(halves(gates[0:36, :]), region(0)[0:36, 0:2, 0:HALF], gate_bias[:, :], None, ALU.add) \
                        .then_inc(region_free[0], 1)
                    dve.wait_ge(region_free[0], n // 2 + 1)
                    dve.scalar_tensor_tensor(lf[32:36, :], gates[32:36, :], -1.0, gates[32:36, :], ALU.mult, ALU.max) \
                        .then_inc(S.gate_abs, 1)
                    split_lo(dve, n + 2, j)
                    dve.wait_ge(S.gate_ln, 1)
                    step(dve.scalar_tensor_tensor(lf[32:36, :], gates[32:36, :], 0.0, lf[32:36, :], ALU.min, ALU.subtract))
                    step(dve.tensor_tensor_scan(b[0:4, :], keep_rows[32:36, :], lf[32:36, :], 0.0, ALU.mult, ALU.add))
                    step(dve.tensor_tensor(rows_t[0:4, 0:TOK], gates[0:4, :], b[0:4, :], ALU.subtract))
                    step(dve.tensor_copy(am[0:4, :], rows_t[0:4, 0:TOK]))
                    step(dve.tensor_tensor(am[0:4, NPR:TOK:NS], am[0:4, NPR:TOK:NS], m0_rows[:, :], ALU.max))
                    step(dve.tensor_tensor_scan(big[0:4, :], cut_rows[0:4, :], am[0:4, :], 0.0, ALU.add, ALU.max))
                    dve.tensor_scalar(rows_t[96:100, 0:TOK], big[0:4, :], -1.0, None, ALU.mult)
                    step(dve.tensor_tensor(gates[0:4, :], b[0:4, :], big[0:4, :], ALU.add))
                    dve.tensor_scalar(am[0:4, 0:NPR], rows_t[0:4, 0:NPR], big[0:4, NPR - 1:NPR], None, ALU.subtract)
                    dve.tensor_tensor(seg(am[0:4, NPR:TOK]), seg(rows_t[0:4, NPR:TOK]),
                                      big[0:4, NPR + NS - 1:TOK:NS].unsqueeze(2).broadcast_to([4, NB, NS]), ALU.subtract)
                    dve.tensor_tensor(seg(b[0:4, 0:NSA]), m0_rows[:, :].unsqueeze(2).broadcast_to([4, NB, NS]),
                                      seg(big[0:4, NPR:TOK]), ALU.subtract).then_inc(S.gate_m, 1)
                    dve.wait_ge(S.gate_rows, 1)
                    hist_dve(dve)
                    dve.wait_ge(S.hist_ready, 1)
                elif t <= 8:
                    head = t - 1
                    for m in range(2):
                        k = 2 * head + m
                        if t <= 2:
                            dve.memset(cb[j][:, m, 0:3], 0.0)
                        dve.tensor_copy(cb_sample(j, m)[:, :, 0:3], hist[:, k, :].rearrange("p (b t) -> p b t", t=3))
                    dve.wait_ge(region_free[j], n // 2 + 1)
                    for m in range(2):
                        k = 2 * head + m
                        dve.tensor_copy(tails[:, k, 0:3], cb[j][:, m, NPR:NPR + 3])
                        step(dve.tensor_copy(tails[:, k, 3:27].rearrange("p (b t) -> p b t", t=3), cb_sample(j, m)[:, :, NS:NS + 3]))
                    if head:
                        dve.wait_ge(S.qk_silu, head)
                    for tap in range(4):
                        for m in range(2):
                            k = 2 * head + m
                            taps, bias = cw_t[:, tap * 16 + k:tap * 16 + k + 1], cw_t[:, 64 + k:65 + k]
                            for dst, src in ((tmp[m][0:DH, 0:NPR], cb[j][:, m, tap:tap + NPR]),
                                             (seg(tmp[m][0:DH, NPR:TOK]), cb_sample(j, m)[:, :, tap:tap + NS])):
                                if tap == 0:
                                    ins = dve.tensor_scalar(dst, src, taps, bias, ALU.mult, ALU.add)
                                else:
                                    ins = dve.scalar_tensor_tensor(dst, src, taps, dst, ALU.mult, ALU.add)
                        if tap < 3:
                            step(ins)
                    ins.then_inc(S.conv_ready, 1)
                    dve.wait_ge(S.qk_silu, head + 1)
                    if head >= 4:
                        dve.tensor_scalar(qk[:, 2 * head:2 * head + 2, :], qk[:, 2 * head:2 * head + 2, :],
                                          float(DA) ** -0.5, None, ALU.mult).then_inc(S.k_scaled, 1)

        A_LOADS = 16 * 5

        def ina_pool(pool, c):
            pool.wait_ge(S.tile_done, BASE_INA)
            def step(ins):
                ins.then_inc(S.pool_step, 1)
                pool.wait_ge(S.pool_step, c("pool_step"))

            step(pool.memset(gate_bias[:, :], 0.0))
            step(pool.memset(rows_t[:, :], 0.0))
            for r in range(2):
                pool.dma_start(gate_bias[32 * r:32 * r + 4, :], I["b_gate_a"][:, 4 * r:4 * r + 4].rearrange("a h -> h a"), allow_slow_non_contiguous=True) \
                    .then_inc(S.a_loaded, 16)
            pool.dma_start(m0_rows[:, :], I["state_m"][0].rearrange("b h -> h b"), allow_slow_non_contiguous=True).then_inc(S.a_loaded, 16)
            pool.dma_start(hist_nat, I["state_conv"][0].rearrange("b t f -> (b t) f")).then_inc(S.a_loaded, 16)
            pool.dma_start(n_nat[:, :], I["state_n"][0].rearrange("b h d -> (b h) d")).then_inc(S.a_loaded, 16)
            pool.wait_ge(S.nl_ready, 16)
            step(pool.memset(keep_rows[32:36, :], 1.0))
            step(pool.memset(cut_rows[0:4, :], 0.0))
            step(pool.memset(v_nat[:, :, :, DA:DA + 1], 1.0))
            step(pool.memset(o_nat[64:P, 4, :, :], 0.0))
            step(pool.memset(keep_rows[32:36, NPR:TOK:NS], 0.0))
            pool.memset(cut_rows[0:4, NPR:TOK:NS], NEG).then_inc(S.consts_ready, 1)

        def hist_pe(pe):
            pe.wait_ge(S.a_loaded, A_LOADS)
            pe.wait_ge(region_free[0], BASE_INA // 2)
            for k in range(16):
                pe.transpose(psum[0:DH, 3, 24 * k:24 * k + 24], hist_nat[:, k * DH:(k + 1) * DH], ident[0:24, 0:24])
            for d in range(2):
                last = pe.transpose(psum[0:DH, 3, 384 + 32 * d:416 + 32 * d], n_nat[:, d * DH:(d + 1) * DH], ident[0:32, 0:32])
            last.then_inc(S.hist_turned, 1)

        def hist_dve(dve):
            dve.wait_ge(S.hist_turned, 1)
            dve.tensor_copy(sqt[1][0:DH, 0:384], psum[0:DH, 3, 0:384])
            dve.tensor_copy(n_t[:, :, :].rearrange("p d n -> p (d n)"), psum[0:DH, 3, 384:448]).then_inc(S.hist_ready, 1)

        S_AT = (0, 512, 1024, 1280)
        S_SAMPLE = 1408
        E_SPANS = ((P, 0, 896), (P, 1024, 1408), (NSA, 1408, 1472))

        def turned_rows_pe(pe):
            pe.wait_ge(S.gate_rows, 1)
            pe.wait_ge(region_free[0], BASE_OUTA // 2)
            pe.wait_ge(region_free[1], BASE_OUTA // 2)
            for t in range(TT):
                pe.transpose(flat[:, t * P:(t + 1) * P] if t < 4 else psum[0:NSA, 1, 0:P],
                             rows_t[:, t * P:(t + 1) * P] if t < 4 else rows_t[:, NPR:TOK], ident[:, :])
            for h in range(HA):
                pe.matmul(psum[0:DH, 2, 64 * h:64 * h + 64], ident[96:100, 96 + h:97 + h].broadcast_to([4, DH]),
                          rows_t[96:100, TOK:TOK + NSA], start=True, stop=True)
            pe.matmul(psum[0:NB, 2, 256:260], rows_t[96:100, TOK + NS - 1:TOK + NSA:NS], ident[96:100, 96:100],
                      start=True, stop=True).then_inc(S.cols_turned, 1)
            for k in range(16):
                last = pe.transpose(psum[0:27, 4 + k // 5, DH * (k % 5):DH * (k % 5) + DH], tails[:, k, :], ident[0:DH, 0:DH])
            last.then_inc(S.tails_turned, 1)

        def turned_rows_dve(dve):
            dve.wait_ge(S.cols_turned, 1)
            dve.tensor_copy(cols[:, 0:4, :], psum[:, 0, :].rearrange("p (t n) -> p t n", t=4)[:, :, 0:68])
            dve.memset(cols[:, 4, :], 1.0).then_inc(S.dve_cols, 1)
            dve.wait_ge(S.dve_cols, 1)
            dve.tensor_copy(cols[0:NSA, 4, :], psum[0:NSA, 1, 0:68])
            dve.tensor_copy(sqt[0][0:DH, 0:256], psum[0:DH, 2, 0:256])
            dve.tensor_copy(decay_b[:, :], psum[0:NB, 2, 256:260])
            dve.wait_ge(S.tails_turned, 1)
            dve.tensor_copy(wv_b[0:27, 0:1440].rearrange("p (b n) -> p b n", b=3), psum[0:27, 4:7, 0:480])
            dve.tensor_copy(wv_b[0:27, 1440:1536], psum[0:27, 7, 0:DH]).then_inc(S.tails_ready, 1)
            dve.memset(tmp[0][:, :], 0.0)
            dve.memset(tmp[1][:, :], 0.0).then_inc(S.dve_cols, 1)

        def n_old(h):
            return sqt[1][0:NB, h * DA:(h + 1) * DA] if h < 3 else sumsq[0:NB, 2 * DA:3 * DA]

        def states_sp(sp):
            sp.wait_ge(S.tile_done, BASE_OUTA)
            for g in range(HA * NB // 2):
                if g >= NG:
                    sp.wait_ge(state_stored[g % NG], 32 * (g // NG))
                for i in (2 * g, 2 * g + 1):
                    sp.dma_start(carried(i), I["state_C"][0, i % NB, i // NB].rearrange("(e p) d -> p e d", p=DH)) \
                        .then_inc(state_loaded[g % NG], 16)

        def states_stored(engine):
            for g in range(NG):
                engine.wait_ge(state_stored[g], 16 * HA * NB // NG)

        def mla_pool(pool):
            pool.wait_ge(S.tile_done, BASE_OUTA)
            pool.dma_start(gh_b[:, :], I["g_h_a"][0].rearrange("h d -> (h d)").partition_broadcast(P)).then_inc(S.gh_loaded, 16)
            pool.dma_start(O["m_prompt"][0].rearrange("a h -> h a"), sqt[0][0:4, NPR - 1:NPR], allow_slow_non_contiguous=True).then_inc(S.m_stored, 16)
            pool.dma_start(O["m_sample"][0].rearrange("b h -> h b"), sqt[0][0:4, NPR + NS - 1:TOK:NS], allow_slow_non_contiguous=True).then_inc(S.m_stored, 16)

            pool.wait_ge(S.tails_turned, 1)
            for h in range(HA):
                pool.dma_start(n_old(h), I["state_n"][0, :, h, :]).then_inc(S.gh_loaded, 16)

            pool.wait_ge(S.tails_ready, 1)
            pool.dma_start(O["conv_prompt"][0, 0], wv_b[0:3, :]).then_inc(S.tails_stored, 16)
            pool.dma_start(O["conv_sample"][0].rearrange("b t f -> (b t) f"), wv_b[3:27, :]).then_inc(S.tails_stored, 16)
            for i in range(HA * NB):
                h, b = i // NB, i % NB
                pool.wait_ge(S.state_new, i + 1)
                pool.dma_start(O["C_sample"][0, b, h].rearrange("(e p) d -> p e d", p=DH), carried(i)) \
                    .then_inc(state_stored[i // 2 % NG], 16)
                if b == NB - 1:
                    pool.wait_ge(S.heads_state, h + 1)
                    pool.dma_start(O["C_prompt"][0, 0, h].rearrange("(e p) d -> p e d", p=DH), rinv[0:DH, 0:2 * DA].rearrange("p (e d) -> p e d", e=2)).then_inc(S.head_stored, 16)
                    pool.dma_start(O["n_prompt"][0, :, h], sumsq[0:1, 0:DA]).then_inc(S.head_stored, 16)
                    pool.dma_start(O["n_sample"][0, :, h], sumsq[0:NB, DA:2 * DA]).then_inc(S.head_stored, 16)

        def mla_pe(pe):
            for h in range(HA):
                q, k = (qk[:, o + 2 * h:o + 2 * h + 2, :] for o in (0, 8))
                if h == 0:
                    pe.wait_ge(S.k_scaled, 4)
                    pe.wait_ge(S.tails_ready, 1)
                else:
                    pe.wait_ge(S.h_scaled, h)
                    pe.wait_ge(S.heads_state, h)
                    pe.wait_ge(S.state_new, NB * h)
                big = ident[96:100, 96 + h:97 + h].broadcast_to([4, P])
                pe.matmul(psum[:, 7, :], big, rows_t[96:100, 0:NPR], start=True, stop=True)
                pe.matmul(psum[0:NSA, 3, 0:NSA], big[:, 0:NSA], rows_t[96:100, NPR:TOK], start=True, stop=True)
                for s in range(TT):
                    at, n = (S_AT[s], NPR - P * s) if s < 4 else (S_SAMPLE, NSA)
                    rows = P if s < 4 else NSA
                    for d in range(2):
                        last = pe.matmul(flat[0:rows, at:at + n], k[:, d, s * P:s * P + rows], q[:, d, s * P:s * P + n],
                                         start=(d == 0), stop=(d == 1))
                last.then_inc(S.qk_ready, 1)
                pe.wait_ge(S.w_ready, h + 1)
                pe.wait_ge(S.consts_ready, 2)
                pe.matmul(psum[:, 6, 0:DA + 1], w_pad[:, :], v_nat[0:NSA, 4, h, :], start=True, stop=False,
                          skip_group_check=True)
                for t in range(4):
                    out = psum[:, 4 + t // 2, (t % 2) * 256:(t % 2) * 256 + DA + 1]
                    for s in range(t + 1):
                        last = pe.matmul(out, w_all[:, S_AT[s] + (t - s) * P:S_AT[s] + (t - s + 1) * P], v_nat[:, s, h, :],
                                         start=(s == 0), stop=(s == t))
                last.then_inc(S.num_prompt, 1)
                for s in range(TT):
                    rows = P if s < 4 else NSA
                    for d in range(2):
                        last = pe.transpose(psum[0:rows, s // 2, (s % 2) * 256 + d * DH:(s % 2) * 256 + (d + 1) * DH],
                                            k[:, d, s * P:s * P + rows], ident[0:DH, 0:DH])
                last.then_inc(S.k_turned, 1)

                def turn_state(b):
                    i = h * NB + b
                    pe.wait_ge(state_loaded[i // 2 % NG], 32 * (i // NC + 1))
                    if b or h:
                        pe.wait_ge(S.state_turned_copied, i)
                    for d in range(2):
                        for e in range(2):
                            last = pe.transpose(psum[0:DH, 3, (2 * d + e) * DH:(2 * d + e + 1) * DH],
                                                carried(i)[:, e, d * DH:(d + 1) * DH], ident[0:DH, 0:DH])
                    last.then_inc(S.state_turned, 1)

                turn_state(0)
                pe.wait_ge(S.wv_ready, h + 1)
                for e in range(2):
                    for s in range(4):
                        pe.matmul(psum[0:DH, 0, e * DA:(e + 1) * DA], wv[:, s, e * DH:(e + 1) * DH], k_nat[:, s, :],
                                  start=(s == 0), stop=(s == 3))
                for s in range(4):
                    pe.matmul(psum[0:1, 7, 0:DA], cols[:, s, 32 + h:33 + h], k_nat[:, s, :], start=(s == 0), stop=(s == 3))
                pe.matmul(psum[0:NB, 7, DA:2 * DA], w_end_b[:, :], k_nat[0:NSA, 4, :], start=True, stop=True) \
                    .then_inc(S.prompt_state, 1)
                for b in range(NB):
                    i = h * NB + b
                    pe.wait_ge(S.state_turned_copied, i + 1)
                    for d in range(2):
                        last = pe.matmul(psum[0:NSA, 6, 0:DA + 1], tmp[d][0:DH, b * NSA:(b + 1) * NSA], turned[:, i % 2, d, :],
                                         start=False, stop=(b == NB - 1 and d == 1), skip_group_check=True)
                    last.then_inc(S.num_sample, 1)
                    if b < NB - 1:
                        turn_state(b + 1)
                    if b >= 2:
                        pe.wait_ge(S.state_new, i - 1)
                    for e in range(2):
                        last = pe.matmul(psum[0:DH, 1 + b % 2, e * DA:(e + 1) * DA],
                                         wv_b[0:NSA, b * DA + e * DH:b * DA + (e + 1) * DH], k_nat[0:NSA, 4, :],
                                         start=True, stop=True)
                    last.then_inc(S.update_ready, 1)

        def mla_act(act):
            for h in range(HA):
                act.wait_ge(S.exponents_ready, h + 1)
                for rows, at, to in E_SPANS:
                    ins = act.activation(e_all[0:rows, at:to], e_all[0:rows, at:to], ACT.Exp)
                ins.then_inc(S.exp_ready, 1)
                for b in range(NB):
                    i = h * NB + b
                    act.wait_ge(S.state_turned, i + 1)
                    if i >= 2:
                        act.wait_ge(S.num_sample, i - 1)
                    act.activation(turned[:, i % 2, :, DA:DA + 1], n_t[:, :, b * HA + h:b * HA + h + 1], ACT.Copy)
                    act.activation(turned[:, i % 2, :, 0:DA], psum[0:DH, 3, 0:2 * DA].rearrange("p (d n) -> p d n", d=2),
                                   ACT.Copy).then_inc(S.state_turned_copied, 1)
                act.wait_ge(S.h_scaled, h + 1)
                act.activation(h_sq, h_nat[:, :, :], ACT.Square).then_inc(S.h_squared, 1)
                act.wait_ge(S.h_ms, h + 1)
                act.activation(small[:, 16:21], small[:, 16:21], ACT.Sqrt, scale=1.0 / DA, bias=eps[:, :]).then_inc(S.h_rms, 1)

        def mla_dve(dve, c):
            def step(ins):
                ins.then_inc(S.dve_step, 1)
                dve.wait_ge(S.dve_step, c("dve_step"))

            num = flat[:, 2048:2048 + 5 * 256].rearrange("p (t n) -> p t n", n=256)
            for h in range(HA):
                v = v_nat[:, :, h, :]
                if h == 0:
                    dve.wait_ge(S.dve_cols, 2)
                dve.wait_ge(S.qk_ready, h + 1)
                for s in range(4):
                    at, a = S_AT[s], cols[:, s, h:h + 1]
                    dve.scalar_tensor_tensor(e_all[:, at:at + P], psum[:, 7, s * P:(s + 1) * P], a, causal[:, :], ALU.add, ALU.add)
                    if s < 3:
                        dve.tensor_scalar(e_all[:, at + P:at + NPR - s * P], psum[:, 7, (s + 1) * P:NPR], a, None, ALU.add)
                dve.scalar_tensor_tensor(e_all[0:NSA, S_SAMPLE:S_SAMPLE + NSA], psum[0:NSA, 3, 0:NSA], cols[0:NSA, 4, h:h + 1],
                                         causal_b[:, :], ALU.add, ALU.add).then_inc(S.exponents_ready, 1)
                carry = carry_all[:, h, :]
                for d in range(2):
                    dve.tensor_tensor(tmp[d][0:DH, :].rearrange("p (b x) -> p b x", b=NB)[:, :, 0:NS],
                                      qk[:, 2 * h + d, NPR:TOK].rearrange("p (b t) -> p b t", b=NB),
                                      carry.rearrange("p (b t) -> p b t", b=NB), ALU.mult)
                dve.wait_ge(S.exp_ready, h + 1)
                for rows, at, to in E_SPANS[:2]:
                    dve.tensor_tensor(w_all[0:rows, at:to], e_all[0:rows, at:to], flat[0:rows, at:to], ALU.mult)
                dve.tensor_tensor(w_pad[:, 0:NSA], e_all[0:NSA, S_SAMPLE:S_SAMPLE + NSA], flat[0:NSA, S_SAMPLE:S_SAMPLE + NSA],
                                  ALU.mult).then_inc(S.w_ready, 1)
                w_end = cols[:, :, 32 + h:33 + h]
                dve.wait_ge(S.k_turned, h + 1)
                if h == 0:
                    dve.wait_ge(S.tails_stored, 32)
                k_psum = flat[:, 0:5 * 256].rearrange("p (t n) -> p t n", n=256)
                dve.tensor_copy(k_nat[:, 0:4, :], k_psum[:, 0:4, 0:DA])
                dve.tensor_copy(k_nat[0:NSA, 4, :], k_psum[0:NSA, 4, 0:DA])
                dve.tensor_tensor(wv[:, :, :], v[:, 0:4, 0:DA], w_end[:, 0:4, :].broadcast_to([P, 4, DA]), ALU.mult)
                step(dve.tensor_scalar(w_end_b[:, :], own[:, :], w_end[0:NSA, 4, :], None, ALU.mult))
                dve.tensor_tensor(wv_b[0:NSA, :].rearrange("p (b n) -> p b n", b=NB),
                                  v[0:NSA, 4, 0:DA].unsqueeze(1).broadcast_to([NSA, NB, DA]),
                                  w_end_b[:, :].unsqueeze(2).broadcast_to([NSA, NB, DA]), ALU.mult).then_inc(S.wv_ready, 1)
                dve.wait_ge(S.prompt_state, h + 1)
                if h:
                    dve.wait_ge(S.head_stored, 48 * h)
                else:
                    dve.wait_ge(S.gh_loaded, 16 * (1 + HA))
                dve.tensor_copy(rinv[0:DH, 0:2 * DA], psum[0:DH, 0, 0:2 * DA])
                dve.tensor_copy(sumsq[0:1, 0:DA], psum[0:1, 7, 0:DA])
                dve.scalar_tensor_tensor(sumsq[0:NB, DA:2 * DA], n_old(h), decay_b[:, h:h + 1], psum[0:NB, 7, DA:2 * DA],
                                         ALU.mult, ALU.add).then_inc(S.heads_state, 1)
                for b in range(NB):
                    i = h * NB + b
                    dve.wait_ge(S.update_ready, i + 1)
                    s = carried(i).rearrange("p e d -> p (e d)")
                    dve.scalar_tensor_tensor(s, s, carry[:, b * NS + NS - 1:b * NS + NS], psum[0:DH, 1 + b % 2, 0:2 * DA],
                                             ALU.mult, ALU.add).then_inc(S.state_new, 1)
                den, least = small[:, 24:29], cols[:, :, 64 + h]
                dve.wait_ge(S.num_sample, NB * (h + 1))
                step(dve.tensor_copy(den, num[:, :, DA]))
                step(dve.scalar_tensor_tensor(den, den, -1.0, den, ALU.mult, ALU.max))
                step(dve.tensor_tensor(den, den, least, ALU.max))
                step(dve.reciprocal(den, den))
                dve.tensor_tensor(h_nat[:, :, :], num[:, :, 0:DA], den.unsqueeze(2).broadcast_to([P, TT, DA]), ALU.mult) \
                    .then_inc(S.h_scaled, 1)
                dve.wait_ge(S.h_squared, h + 1)
                dve.tensor_reduce(small[:, 16:21], h_sq, AX, ALU.add).then_inc(S.h_ms, 1)
                dve.wait_ge(S.h_rms, h + 1)
                step(dve.reciprocal(small[:, 16:21], small[:, 16:21]))
                step(dve.tensor_tensor(h_nat[:, :, :], h_nat[:, :, :], small[:, 16:21].unsqueeze(2).broadcast_to([P, TT, DA]), ALU.mult))
                step(dve.tensor_tensor(h_nat[:, :, :], h_nat[:, :, :],
                                       gh_b[:, h * DA:(h + 1) * DA].unsqueeze(1).broadcast_to([P, TT, DA]), ALU.mult))
                dve.tensor_tensor(o_nat[:, :, h, :], o_nat[:, :, h, :], h_nat[:, :, :], ALU.mult).then_inc(S.num_copied, 1)

        def wide(k):
            return spare_lo[:, 640 * (k % 2):640 * (k % 2) + 640]

        def qnorm_pe(pe, at, chunks, nth):
            for k in range(chunks):
                pe.wait_ge(S.q_squared, at + k + 1)
                for t in range(TT):
                    col, tok = 10 * k + 2 * t, t * P if t < 4 else TOK - P
                    last = pe.matmul(psum[:, 0, col:col + 2], sqt[k % 2][:, tok:tok + P], ones_heads[:, 0:P:DM],
                                     start=True, stop=True)
                last.then_inc(S.q_summed, 1)
            for k in range(chunks):
                pe.wait_ge(S.q_wide, at + k + 1)
                if k >= 3:
                    pe.wait_ge(S.q_normed, at + k - 2)
                for t in range(TT):
                    n = P if t < 4 else NSA
                    base = 1024 * (1 + k % 3) + t * P
                    last = pe.matmul(flat[:, base:base + n], wide(k)[:, t * P:(t + 1) * P], ident[:, P - n:P], start=True, stop=True)
                last.then_inc(S.q_spread, 1)

        def qnorm_act(act, at, chunks, nth, src):
            for k in range(chunks):
                if k >= 2:
                    act.wait_ge(S.q_summed, at + k - 1)
                act.activation(sqt[k % 2][:, :], src(k), ACT.Square).then_inc(S.q_squared, 1)
            act.wait_ge(S.q_summed, at + chunks)
            act.activation(tmp[0][:, 0:10 * chunks], psum[:, 0, 0:10 * chunks], ACT.Sqrt, scale=1.0 / DM, bias=eps[:, :]) \
                .then_inc(S.q_rms, 1)
            act.wait_ge(S.q_cols, nth + 1)
            for k in range(chunks):
                if k >= 2:
                    act.wait_ge(S.q_spread, at + k - 1)
                act.activation(wide(k).rearrange("p (x d) -> p x d", d=DM),
                               tmp[0][:, 10 * k:10 * k + 10].unsqueeze(2).broadcast_to([P, 10, DM]), ACT.Copy).then_inc(S.q_wide, 1)

        def qnorm_dve(dve, at, chunks, nth, src, dst, gain_col):
            dve.wait_ge(S.q_rms, nth + 1)
            dve.reciprocal(tmp[0][:, 0:10 * chunks], tmp[0][:, 0:10 * chunks]).then_inc(S.q_cols, 1)
            for k in range(chunks):
                base = 1024 * (1 + k % 3)
                dve.wait_ge(S.q_spread, at + k + 1)
                dve.scalar_tensor_tensor(dst(k), src(k), gain_col(k), flat[:, base:base + TOK], ALU.mult, ALU.mult) \
                    .then_inc(S.q_normed, 1)

        def queries_b(k):
            return MB.qn[:, k, :] if k < 2 else qb_t[:, k - 2, :]

        def place(h):
            return 2 * (h % 2) + h // 2

        def mem_attention_pe(pe, l, B):
            pe.wait_ge(S.q_normed, B.normed)

            def scores(t):
                i = 4 * l + t
                if t >= 2:
                    pe.wait_ge(S.ma_exp, i - 1)
                for h in range(HM):
                    r = slice(64 * (h % 2), 64 * (h % 2) + 64)
                    last = pe.matmul(psum[:, 2 * (t % 2) + h % 2, 256 * (h // 2):256 * (h // 2) + M],
                                     B.qn[r, h // 2, t * P:(t + 1) * P], mk_t[l][r, h // 2, :], start=True, stop=True)
                last.then_inc(S.ma_scores, 1)

            scores(0)
            scores(1)
            for t in range(4):
                i = 4 * l + t
                pe.wait_ge(S.ma_p, i + 1)
                for x in range(8):
                    last = pe.transpose(psum[:, 4 + x // 4, (x % 4) * P:(x % 4 + 1) * P],
                                        B.e[t % 2][:, x // 2, (x % 2) * P:(x % 2 + 1) * P], ident[:, :])
                last.then_inc(S.ma_turned, 1)
                if t + 2 < 4:
                    scores(t + 2)
                pe.wait_ge(S.ma_pt, i + 1)
                if t >= 2:
                    pe.wait_ge(S.ma_out_lo, 5 * l + t - 1)
                for h in range(HM):
                    for m in range(2):
                        last = pe.matmul(psum[64 * (h % 2):64 * (h % 2) + 64, 6 + t % 2, (h // 2) * P:(h // 2 + 1) * P],
                                         mv[l][:, m, h * DM:(h + 1) * DM], B.pt[t % 2][:, 2 * place(h) + m, :],
                                         start=(m == 0), stop=(m == 1))
                last.then_inc(S.ma_out, 1)

            def turn_keys(b):
                pe.wait_ge(ks_loaded[b % 4], 16 * (2 * l + b // 4 + 1))
                if b >= 2:
                    pe.wait_ge(S.ms_kt, NB * l + b - 1)
                for pair in range(2):
                    for m in range(2):
                        last = pe.transpose(psum[:, b % 2, (2 * pair + m) * P:(2 * pair + m + 1) * P],
                                            B.ks[:, b % 4, m, pair * P:(pair + 1) * P], ident[:, :])
                last.then_inc(S.ms_turned, 1)

            turn_keys(0)
            pe.wait_ge(S.ms_qz, l + 1)
            for b in range(NB):
                if b + 1 < NB:
                    turn_keys(b + 1)
                pe.wait_ge(S.ms_kt, NB * l + b + 1)
                for pair in range(2):
                    last = pe.matmul(psum[32 * (b % 4):32 * (b % 4) + 32, 2 + 2 * (b // 4), 0:M], B.qz[:, pair, b, :],
                                     B.kt[:, b % 2, pair, :], start=(pair == 0), stop=(pair == 1))
                last.then_inc(S.ms_scores, 1)
            pe.wait_ge(S.ma_out_lo, 5 * l + 4)
            for g in range(2):
                pe.wait_ge(S.ms_p, 2 * l + g + 1)
                for m in range(2):
                    last = pe.transpose(psum[:, 3 + 2 * g, m * P:(m + 1) * P], B.e[g][:, 0, m * P:(m + 1) * P], ident[:, :])
                last.then_inc(S.ms_pturned, 1)
                pe.wait_ge(S.ms_pt, 2 * l + g + 1)
                if g == 0:
                    pe.wait_ge(S.vs_loaded, 128 * (l + 1))
                for b in range(4 * g, 4 * g + 4):
                    for pair in range(2):
                        at = (b * 2 + pair) * 16
                        row = 32 * (b % 4) + 16 * pair
                        for m in range(2):
                            last = pe.matmul(psum[:, 7, at:at + 16], B.vs[:, b, m, pair * P:(pair + 1) * P],
                                             B.pt[g][:, m, row:row + 16], start=(m == 0), stop=(m == 1))
                last.then_inc(S.ms_out, 1)

        def mem_attention_act(act, l, B):
            scale = float(DM) ** -0.5

            def exponents(t):
                i = 4 * l + t
                if t >= 2:
                    act.wait_ge(S.ma_turned, i - 1)
                act.wait_ge(S.ma_max, i + 1)
                for h in range(HM):
                    x, at = place(h), 32 + 8 * (t % 2)
                    ins = act.activation(B.e[t % 2][:, x, :], psum[:, 2 * (t % 2) + h % 2, 256 * (h // 2):256 * (h // 2) + M],
                                         ACT.Exp, scale=scale, bias=small[:, at + x:at + x + 1],
                                         accum_out=small[:, at + 4 + x:at + 5 + x])
                ins.then_inc(S.ma_exp, 1)

            def mixed_hi(t):
                act.wait_ge(S.ma_out, 4 * l + t + 1)
                act.activation(act_hi[:, 6:8, t * P:(t + 1) * P], psum[:, 6 + t % 2, 0:256].rearrange("p (a n) -> p a n", a=2),
                               ACT.Copy).then_inc(S.ma_out_hi, 1)

            exponents(0)
            for t in range(4):
                if t < 3:
                    exponents(t + 1)
                if t:
                    mixed_hi(t - 1)
                act.wait_ge(S.ma_turned, 4 * l + t + 1)
                act.activation(B.pt[t % 2][:, :, :].rearrange("p x n -> p (x n)"), flat[:, 2048:3072], ACT.Copy).then_inc(S.ma_pt, 1)
            mixed_hi(3)

            def copy_keys(b):
                act.wait_ge(S.ms_turned, NB * l + b + 1)
                if b >= 2:
                    act.wait_ge(S.ms_scores, NB * l + b - 1)
                act.activation(B.kt[:, b % 2, :, :].rearrange("p a m -> p (a m)"), psum[:, b % 2, :], ACT.Copy).then_inc(S.ms_kt, 1)

            def sample_exponents(g):
                act.wait_ge(S.ms_max, 2 * l + g + 1)
                at = 32 + 8 * g
                act.activation(B.e[g][:, 0, :], psum[:, 2 + 2 * g, 0:M], ACT.Exp, scale=scale, bias=small[:, at:at + 1],
                               accum_out=small[:, at + 4:at + 5]).then_inc(S.ms_exp, 1)

            def sample_turned(g):
                act.wait_ge(S.ms_pturned, 2 * l + g + 1)
                act.activation(B.pt[g][:, 0:2, :].rearrange("p x n -> p (x n)"), psum[:, 3 + 2 * g, 0:256], ACT.Copy).then_inc(S.ms_pt, 1)

            for b in range(6):
                copy_keys(b)
            sample_exponents(0)
            for b in range(6, NB):
                copy_keys(b)
            sample_turned(0)
            sample_exponents(1)
            sample_turned(1)
            act.wait_ge(S.ms_out, 2 * l + 2)
            for r in range(2):
                ins = act.activation(sample_mix(act_hi, r, 6, 2), mem_out_view(r), ACT.Copy)
            ins.then_inc(S.ma_out_hi, 1)

        def sample_mix(t, r, c0, n):
            return t[64 * r:64 * r + 64, c0:c0 + n, NPR:TOK].rearrange("p c (b t) -> p c b t", b=NB)

        def mem_out_view(r):
            return psum[64 * r:64 * r + 64, 7, 0:256].rearrange("p (b c x) -> p c b x", b=NB, c=2)[:, :, :, 8 * r:8 * r + 8]

        def mem_attention_dve(dve, l, B, c):
            scale = float(DM) ** -0.5

            def step(ins):
                ins.then_inc(S.dve_step, 1)
                dve.wait_ge(S.dve_step, c("dve_step"))

            step(dve.memset(B.qz[:, :, :, :], 0.0))
            for pair in range(2):
                for r in range(2):
                    h = 2 * pair + r
                    ins = dve.tensor_copy(B.qz[64 * r:64 * r + 64, pair, :, h * NS:(h + 1) * NS],
                                          B.qn[64 * r:64 * r + 64, pair, NPR:TOK].rearrange("p (b t) -> p b t", b=NB))
            ins.then_inc(S.ms_qz, 1)
            def maxima(t):
                dve.wait_ge(S.ma_scores, 4 * l + t + 1)
                top = small[:, 32 + 8 * (t % 2):36 + 8 * (t % 2)]
                s = flat[:, 1024 * (t % 2):1024 * (t % 2) + 1024].rearrange("p (h m) -> p h m", h=HM)
                step(dve.tensor_reduce(top, s, AX, ALU.max))
                dve.tensor_scalar(top, top, -scale, None, ALU.mult).then_inc(S.ma_max, 1)

            def mixed_lo(t):
                dve.wait_ge(S.ma_out_hi, 5 * l + t + 1)
                dve.tensor_tensor(act_lo[:, 6:8, t * P:(t + 1) * P], psum[:, 6 + t % 2, 0:256].rearrange("p (a n) -> p a n", a=2),
                                  act_hi[:, 6:8, t * P:(t + 1) * P].bitcast(F32), ALU.subtract).then_inc(S.ma_out_lo, 1)

            maxima(0)
            for t in range(4):
                if t < 3:
                    maxima(t + 1)
                sums = small[:, 36 + 8 * (t % 2):40 + 8 * (t % 2)]
                dve.wait_ge(S.ma_exp, 4 * l + t + 1)
                step(dve.reciprocal(sums, sums))
                e = B.e[t % 2][:, :, :]
                dve.tensor_tensor(e, e, sums.unsqueeze(2).broadcast_to([P, HM, M]), ALU.mult).then_inc(S.ma_p, 1)
                if t:
                    mixed_lo(t - 1)
            mixed_lo(3)
            for g in range(2):
                i, at = 2 * l + g, 32 + 8 * g
                dve.wait_ge(S.ms_scores, NB * l + 4 * g + 4)
                step(dve.tensor_reduce(small[:, at:at + 1], psum[:, 2 + 2 * g, 0:M], AX, ALU.max))
                dve.tensor_scalar(small[:, at:at + 1], small[:, at:at + 1], -scale, None, ALU.mult).then_inc(S.ms_max, 1)
                dve.wait_ge(S.ms_exp, i + 1)
                step(dve.reciprocal(small[:, at + 4:at + 5], small[:, at + 4:at + 5]))
                dve.tensor_scalar(B.e[g][:, 0, :], B.e[g][:, 0, :], small[:, at + 4:at + 5], None, ALU.mult).then_inc(S.ms_p, 1)
            dve.wait_ge(S.ma_out_hi, 5 * l + 5)
            for r in range(2):
                ins = dve.tensor_tensor(sample_mix(act_lo, r, 6, 2), mem_out_view(r), sample_mix(act_hi, r, 6, 2).bitcast(F32),
                                        ALU.subtract)
            ins.then_inc(S.ma_out_lo, 1)

        def mem_attention_pool(pool, l, B, c):
            if l:
                pool.wait_ge(S.kv_stored, 64)
                pool.wait_ge(S.tile_done, BASE_INB)
            def load_keys(b):
                pool.dma_start(B.ks[:, b % 4, :, :], I["cache_mem_k"][l, b].rearrange("(m p) h d -> p m (h d)", p=P)) \
                    .then_inc(ks_loaded[b % 4], 16)

            for b in range(4):
                load_keys(b)
            for b in range(NB):
                pool.dma_start(B.vs[:, b, :, :], I["cache_mem_v"][l, b].rearrange("(m p) h d -> p m (h d)", p=P)) \
                    .then_inc(S.vs_loaded, 16)
            for b in range(4, NB):
                pool.wait_ge(S.ms_turned, NB * l + b - 3)
                load_keys(b)

        def ha_pe(pe):
            pe.wait_ge(S.num_copied, HA)
            pe.wait_ge(S.ma_out_lo, 5)
            for k in range(6):
                if k >= 3:
                    pe.wait_ge(S.mix_lo, k - 2)
                b = 2 * (k % 3)
                for t, at, rows in token_tiles():
                    last = pe.transpose(psum[:, b, t * P:(t + 1) * P] if t < 4 else psum[:, b + 1, 0:NSA],
                                        o_flat[0:rows, t, k * P:(k + 1) * P], ident[0:rows, 0:rows])
                last.then_inc(S.mix_turned, 1)

        def ha_act(act):
            states_stored(act)
            for k in range(6):
                act.wait_ge(S.mix_turned, k + 1)
                act.activation(act_hi[:, k, :], flat[:, 1024 * (k % 3):1024 * (k % 3) + TOK], ACT.Copy).then_inc(S.mix_hi, 1)

        def ha_dve(dve):
            states_stored(dve)
            for k in range(6):
                dve.wait_ge(S.mix_hi, k + 1)
                dve.tensor_tensor(act_lo[:, k, :], flat[:, 1024 * (k % 3):1024 * (k % 3) + TOK], act_hi[:, k, :].bitcast(F32),
                                  ALU.subtract).then_inc(S.mix_lo, 1)

        def kv_sp(sp):
            view = I["w_kv"].rearrange("(k p) n -> p k n", p=P)
            for t in range(6):
                load(sp, BASE_KV + t, t % 2, view[:, :, t * 256:(t + 1) * 256], raw[t % 2][:, :].rearrange("p (k n) -> p k n", k=KD))

        def kv_pe(pe, nth):
            for t in range(6):
                w_hi, w_lo = weights(t % 2, (KD, 256))
                natural_product(pe, BASE_KV + t, t % 2, w_hi, w_lo, 256, ready=(S.nl_ready, 8 * nth) if t == 0 else None)
            pe.wait_ge(S.k_ready, 3)
            for k in range(6):
                b = 2 * (k % 3)
                if k < 3:
                    pe.wait_ge(S.region_free0, BASE_FFN[2] // 2)
                    pe.wait_ge(S.region_free1, BASE_FFN[2] // 2)
                else:
                    pe.wait_ge(S.kt_copied, k - 2)
                for t, at, rows in token_tiles():
                    last = pe.transpose(psum[:, b, t * P:(t + 1) * P] if t < 4 else psum[:, b + 1, 0:NSA],
                                        kn[0:rows, t, k * P:(k + 1) * P], ident[0:rows, 0:rows])
                last.then_inc(S.kt_turned, 1)
            pe.wait_ge(S.kt_copied, 6)

        def kv_act(act):
            for t in range(6):
                n, j = BASE_KV + t, t % 2
                split_hi(act, n + 1, 1 - j)
                act.wait_ge(S.tile_done, n + 1)
                dst, src = (kn, vn)[t // 3], natural_view(j, 256)
                cols_ = slice((t % 3) * 256, (t % 3) * 256 + 256)
                act.activation(dst[:, 0:4, cols_], src[:, 0:4, :], ACT.Copy)
                act.activation(dst[0:NSA, 4, cols_], src[0:NSA, 4, :], ACT.Copy).then_inc(region_free[j], 1)
                if t < 3:
                    act.wait_ge(S.kn_padded, 1)
                    if t:
                        act.wait_ge(S.k_ms, t)
                    act.wait_ge(region_free[j], n // 2 + 1)
                    act.activation(ksq[:, :, :], kn[:, :, cols_], ACT.Square).then_inc(S.k_squared, 1)
                    act.wait_ge(S.k_ms, t + 1)
                    act.activation(small[:, 40:60], small[:, 40:60], ACT.Sqrt, scale=1.0 / DB, bias=eps[:, :]).then_inc(S.k_rms, 1)

        def kv_dve(dve, c):
            def step(ins):
                ins.then_inc(S.dve_step, 1)
                dve.wait_ge(S.dve_step, c("dve_step"))

            dve.wait_ge(S.tile_done, BASE_KV)
            dve.memset(kn[NSA:P, 4, :], 0.0).then_inc(S.kn_padded, 1)
            for t in range(6):
                n, j = BASE_KV + t, t % 2
                split_lo(dve, n + 1, 1 - j)
                if t < 3:
                    dve.wait_ge(S.k_squared, t + 1)
                    sq = ksq[:, :, :].rearrange("p t (h d) -> p t h d", d=DB)
                    dve.tensor_reduce(small[:, 40:60].rearrange("p (t h) -> p t h", h=4), sq, AX, ALU.add).then_inc(S.k_ms, 1)
                    dve.wait_ge(S.k_rms, t + 1)
                    step(dve.reciprocal(small[:, 40:60], small[:, 40:60]))
                    for i in range(TT):
                        k = kn[:, i, t * 256:(t + 1) * 256].rearrange("p (h d) -> p h d", d=DB)
                        step(dve.tensor_tensor(k, k, small[:, 40 + 4 * i:44 + 4 * i].unsqueeze(2).broadcast_to([P, 4, DB]), ALU.mult))
                        ins = dve.tensor_tensor(k, k, gk_b[:, :].unsqueeze(1).broadcast_to([P, 4, DB]), ALU.mult)
                    ins.then_inc(S.k_ready, 1)
            for k in range(6):
                dve.wait_ge(S.kt_turned, k + 1)
                dve.tensor_copy(kt_b[:, k, :], flat[:, 1024 * (k % 3):1024 * (k % 3) + TOK]).then_inc(S.kt_copied, 1)

        def kv_pool(pool):
            def store(dst_p, dst_s, src):
                pool.dma_start(dst_p.rearrange("a (t p) h d -> p (a t) (h d)", p=P), src[:, 0:4, :]).then_inc(S.kv_stored, 16)
                pool.dma_start(dst_s.rearrange("b t h d -> (b t) (h d)"), src[0:NSA, 4, :]).then_inc(S.kv_stored, 16)
            pool.wait_ge(S.k_ready, 3)
            store(O["k_prompt"], O["k_sample"], kn)
            pool.wait_ge(S.region_free0, BASE_FFN[2] // 2)
            pool.wait_ge(S.region_free1, BASE_FFN[2] // 2)
            store(O["v_prompt"], O["v_sample"], vn)

        def inb_sp(sp):
            view = I["w_in_b"][0].rearrange("(k p) n -> p k n", p=P)
            for t in range(4):
                load(sp, BASE_INB + t, t % 2, view[:, :, t * 256:(t + 1) * 256], raw[t % 2][:, :].rearrange("p (k n) -> p k n", k=KD))

        def inb_pe(pe, nth):
            for t in range(4):
                w_hi, w_lo = weights(t % 2, (KD, 256))
                product(pe, BASE_INB + t, t % 2, w_hi, w_lo, act_hi, act_lo, KD, 2, P, ready=(S.nl_ready, 8 * nth, KD))

        def inb_act(act):
            for t in range(4):
                n, j = BASE_INB + t, t % 2
                split_hi(act, n + 1, 1 - j)
                act.wait_ge(S.tile_done, n + 1)
                dst = qb_t[:, 2 * t:2 * t + 2, :] if t < 3 else MB.qn[:, :, :]
                act.activation(dst.rearrange("p m (h n) -> p (m h) n", h=2), region(j)[:, :, 0:HALF], ACT.Copy) \
                    .then_inc(region_free[j], 1)
            act.wait_ge(S.region_free0, BASE_OUTB // 2)
            act.wait_ge(S.region_free1, BASE_OUTB // 2)

        Z_AT = (896, 1024, 512, 0)
        A_AT = (0, 512, 1024, 896)
        ZW = 1280

        def stick_pe(pe):
            pe.wait_ge(S.ma_out_lo, 10)

            def z(h):
                r = slice(64 * (h % 2), 64 * (h % 2) + 64)
                if h:
                    pe.wait_ge(S.z_read, h)
                for t in range(4):
                    last = pe.matmul(flat[:, Z_AT[t]:Z_AT[t] + (t + 1) * P], qb_t[r, h // 2, t * P:(t + 1) * P],
                                     kt_b[r, h // 2, 0:(t + 1) * P], start=True, stop=True)
                last.then_inc(S.z_ready, 1)

            def outputs(h):
                pe.wait_ge(S.at_ready, h + 1)
                if h == 0:
                    pe.wait_ge(S.vp_loaded, 16)
                if h >= 4 and h % 2 == 0:
                    pe.wait_ge(S.stick_lo, h // 2 - 1)
                for k in range(4):
                    last = pe.matmul(psum[64 * (h % 2):64 * (h % 2) + 64, 6 + (h // 2) % 2, k * P:NPR], vp[:, k, h * DB:(h + 1) * DB],
                                     a_t[:, A_AT[k]:A_AT[k] + NPR - k * P], start=(k == 0), stop=(k == 3), skip_group_check=True)
                last.then_inc(S.stick_out, 1)

            z(0)
            for h in range(HB):
                if h + 1 < HB:
                    z(h + 1)
                if h:
                    outputs(h - 1)
                pe.wait_ge(S.a_ready, h + 1)
                for t in range(4):
                    for k in range(t + 1):
                        at = 1536 + A_AT[k] + (t - k) * P
                        last = pe.transpose(flat[:, at:at + P], keep[h % 2][:, Z_AT[t] + k * P:Z_AT[t] + (k + 1) * P], ident[:, :])
                last.then_inc(S.a_turned, 1)
            outputs(HB - 1)

        def stick_act(act):
            scale = float(DB) ** -0.5
            for h in range(HB):
                act.wait_ge(S.z_ready, h + 1)
                if h >= 2:
                    act.wait_ge(S.a_turned, h - 1)
                act.activation(take[h % 2][:, :], flat[:, 0:ZW], ACT.Sigmoid, scale=scale, bias=b_all[:, h:h + 1])
                act.activation(keep[h % 2][:, :], flat[:, 0:ZW], ACT.Sigmoid, scale=-scale, bias=b_neg[:, h:h + 1]).then_inc(S.z_read, 1)
                if h:
                    stick_act_tail(act, h - 1)
            stick_act_tail(act, HB - 1)

        def stick_act_tail(act, h):
            act.wait_ge(S.a_turned, h + 1)
            if h:
                act.wait_ge(S.stick_out, h)
            act.activation(a_t[:, 0:ZW], flat[:, 1536:1536 + ZW], ACT.Copy).then_inc(S.at_ready, 1)
            if h % 2 == 1 and h > 1:
                stick_hi(act, h // 2 - 1)
            if h == HB - 1:
                stick_hi(act, h // 2)

        def stick_hi(act, p):
            act.wait_ge(S.stick_out, 2 * p + 2)
            act.activation(act_hi[:, p, 0:NPR], psum[:, 6 + p % 2, :], ACT.Copy).then_inc(S.stick_hi, 1)

        def stick_lo(dve, p):
            dve.wait_ge(S.stick_hi, p + 1)
            dve.tensor_tensor(act_lo[:, p, 0:NPR], psum[:, 6 + p % 2, :], act_hi[:, p, 0:NPR].bitcast(F32), ALU.subtract) \
                .then_inc(S.stick_lo, 1)

        def stick_dve(dve, c):
            def step(ins):
                ins.then_inc(S.dve_step, 1)
                dve.wait_ge(S.dve_step, c("dve_step"))

            for h in range(HB):
                tk, kp = take[h % 2], keep[h % 2]
                dve.wait_ge(S.z_read, h + 1)
                three = slice(384, 384 + 3 * 384)
                for x, m, op in ((tk, before, ALU.mult), (kp, not_before, ALU.max)):
                    for at in (384, 768, 1152, 896):
                        ins = dve.tensor_tensor(x[:, at:at + P], x[:, at:at + P], m[:, :], op)
                step(ins)
                for t in range(4):
                    a, n = Z_AT[t], (t + 1) * P
                    ins = dve.tensor_tensor_scan(backwards(rest, a, n), backwards(kp, a, n), zero[:, :].broadcast_to([P, n]), 1.0,
                                                 ALU.mult, ALU.add)
                step(ins)
                dve.tensor_tensor(kp[:, 0:ZW - 1], tk[:, 0:ZW - 1], rest[:, 1:ZW], ALU.mult)
                dve.tensor_copy(kp[:, ZW - 1:ZW], tk[:, ZW - 1:ZW]).then_inc(S.a_ready, 1)
                dve.wait_ge(S.a_ready, h + 1)
                if h % 2 == 1 and h > 4:
                    stick_lo(dve, h // 2 - 2)
            stick_lo(dve, HB // 2 - 2)
            stick_lo(dve, HB // 2 - 1)

        def backwards(t, a, n):
            return t[:, a:a + n][:, ::-1]

        KEYS = PAST + NS

        def pages_pool(pool):
            pool.dma_start(table[:, :], I["page_table"].rearrange("b n -> (b n)").unsqueeze(0)).then_inc(S.table_loaded, 16)
            pool.wait_ge(S.kv_stored, 64)
            pool.wait_ge(S.ma_out_lo, 10)
            pool.dma_start(vp[:, :, :], O["v_prompt"].rearrange("a (t p) h d -> p (a t) (h d)", p=P)).then_inc(S.vp_loaded, 16)
            pool.wait_ge(S.table_loaded, 16)
            for b in range(NB):
                load_keys(pool, b)
                if b:
                    load_values(pool, b - 1)
            load_values(pool, NB - 1)

        def load_pages(pool, b, dst, cache, loaded):
            for g in range(PAST // PAGE):
                page = pool.value_load(table[0:1, 2 * b + g:2 * b + g + 1], min_val=0, max_val=cache.shape[0] - 1)
                pool.dma_start(dst[:, g, :], cache[bass.ds(page, 1), :, :, :].rearrange("a p h d -> (a p) (h d)")) \
                    .then_inc(loaded, 16)

        def load_keys(pool, b):
            if b >= 2:
                pool.wait_ge(S.kpg_turned, b - 1)
            load_pages(pool, b, kpg[b % 2], I["cache_k"], keys_loaded[b % 2])

        def load_values(pool, b):
            if b == 1:
                pool.wait_ge(S.stick_lo, HB // 2)
            if b >= 2:
                pool.wait_ge(S.sb_out, b - 1)
            load_pages(pool, b, vpg[b % 2], I["cache_v"], values_loaded[b % 2])
            pool.dma_start(vnew[b % 2][:, :], O["v_sample"][b].rearrange("t h d -> t (h d)")).then_inc(values_loaded[b % 2], 16)

        def stick_sample_pe(pe):
            def turn_keys(b):
                pe.wait_ge(keys_loaded[b % 2], 32 * (b // 2 + 1))
                if b:
                    pe.wait_ge(S.kpt_ready, b)
                for p in range(6):
                    for g in range(2):
                        at = p * 256 + g * P
                        last = pe.transpose(flat[:, at:at + P], kpg[b % 2][:, g, p * P:(p + 1) * P], ident[:, :])
                last.then_inc(S.kpg_turned, 1)

            def z(b):
                pe.wait_ge(S.kpt_ready, b + 1)
                pe.wait_ge(S.qzb_ready, b + 1)
                if b:
                    pe.wait_ge(S.zs_read, b)
                for at, n, keys in ((0, PAST, lambda p: kpt[:, p, :]),
                                    (PAST, NS, lambda p: kt_b[:, p, NPR + b * NS:NPR + (b + 1) * NS])):
                    for p in range(6):
                        last = pe.matmul(psum[0:96, 3, at:at + n], qzb[b % 2][:, p * 96:(p + 1) * 96], keys(p),
                                         start=(p == 0), stop=(p == 5))
                last.then_inc(S.zs_ready, 1)

            def turn_weights(b):
                pe.wait_ge(S.as_ready, b + 1)
                if b:
                    pe.wait_ge(S.ats_ready, b)
                for g in range(2):
                    pe.transpose(psum[:, 4, g * 96:(g + 1) * 96], keeps[:, g * P:(g + 1) * P], ident[0:96, 0:96])
                pe.transpose(psum[0:NS, 4, 192:288], keeps[:, PAST:KEYS], ident[0:96, 0:96]).then_inc(S.as_turned, 1)

            def outputs(b):
                j = b % 2
                pe.wait_ge(values_loaded[j], 48 * (b // 2 + 1))
                pe.wait_ge(S.ats_ready, b + 1)
                if b >= 2:
                    pe.wait_ge(S.sb_lo, b - 1)
                for p in range(6):
                    out = psum[:, 5 + j, 16 * p:16 * p + 16]
                    for g in range(2):
                        pe.matmul(out, vpg[j][:, g, p * P:(p + 1) * P], a_ts[:, g * 96 + 16 * p:g * 96 + 16 * p + 16], start=(g == 0), stop=False)
                    last = pe.matmul(out, vnew[j][:, p * P:(p + 1) * P], a_ts[0:NS, 192 + 16 * p:208 + 16 * p], start=False, stop=True)
                last.then_inc(S.sb_out, 1)

            pe.wait_ge(S.stick_lo, HB // 2)
            turn_keys(0)
            for b in range(NB):
                z(b)
                if b:
                    turn_weights(b - 1)
                if b + 1 < NB:
                    turn_keys(b + 1)
                if b:
                    outputs(b - 1)
            turn_weights(NB - 1)
            outputs(NB - 1)

        def stick_sample_act(act):
            scale = float(DB) ** -0.5

            def copy_keys(b):
                act.wait_ge(S.kpg_turned, b + 1)
                if b:
                    act.wait_ge(S.zs_ready, b)
                act.activation(kpt[:, :, :].rearrange("p c k -> p (c k)"), flat[:, 0:1536], ACT.Copy).then_inc(S.kpt_ready, 1)

            def copy_weights(b):
                act.wait_ge(S.as_turned, b + 1)
                if b:
                    act.wait_ge(S.sb_out, b)
                act.activation(a_ts[:, 0:192], psum[:, 4, 0:192], ACT.Copy)
                act.activation(a_ts[0:NS, 192:288], psum[0:NS, 4, 192:288], ACT.Copy).then_inc(S.ats_ready, 1)

            def mixed_hi(b):
                act.wait_ge(S.sb_out, b + 1)
                for r in range(2):
                    ins = act.activation(act_hi[64 * r:64 * r + 64, 0:6, NPR + b * NS:NPR + (b + 1) * NS], out_rows(b, r), ACT.Copy)
                ins.then_inc(S.sb_hi, 1)

            copy_keys(0)
            for b in range(NB):
                act.wait_ge(S.zs_ready, b + 1)
                if b:
                    act.wait_ge(S.as_turned, b)
                act.activation(takes[:, :], psum[0:96, 3, 0:KEYS], ACT.Sigmoid, scale=scale, bias=b_rows[:, 0:1])
                act.activation(keeps[:, :], psum[0:96, 3, 0:KEYS], ACT.Sigmoid, scale=-scale, bias=b_rows[:, 1:2]).then_inc(S.zs_read, 1)
                if b:
                    copy_weights(b - 1)
                if b + 1 < NB:
                    copy_keys(b + 1)
                if b:
                    mixed_hi(b - 1)
            copy_weights(NB - 1)
            mixed_hi(NB - 1)

        def out_rows(b, r):
            return psum[64 * r:64 * r + 64, 5 + b % 2, 0:96].rearrange("p (c x) -> p c x", c=6)[:, :, 8 * r:8 * r + 8]

        def stick_sample_dve(dve, c):
            def step(ins):
                ins.then_inc(S.dve_step, 1)
                dve.wait_ge(S.dve_step, c("dve_step"))

            def place_queries(b):
                if b >= 2:
                    dve.wait_ge(S.zs_ready, b - 1)
                for r in range(2):
                    dst = qzb[b % 2][64 * r:64 * r + 64, 0:672].rearrange("p (c x) -> p c x", c=6)[:, :, 8 * r:8 * r + 8]
                    ins = dve.tensor_copy(dst, qb_t[64 * r:64 * r + 64, 0:6, NPR + b * NS:NPR + (b + 1) * NS])
                ins.then_inc(S.qzb_ready, 1)

            def mixed_lo(b):
                dve.wait_ge(S.sb_hi, b + 1)
                for r in range(2):
                    half = slice(64 * r, 64 * r + 64), slice(0, 6), slice(NPR + b * NS, NPR + (b + 1) * NS)
                    ins = dve.tensor_tensor(act_lo[half], out_rows(b, r), act_hi[half].bitcast(F32), ALU.subtract)
                ins.then_inc(S.sb_lo, 1)

            for j in range(2):
                ins = dve.memset(qzb[j][:, :], 0.0)
            step(ins)
            place_queries(0)
            for b in range(NB):
                if b + 1 < NB:
                    place_queries(b + 1)
                dve.wait_ge(S.zs_read, b + 1)
                dve.tensor_tensor(takes[:, PAST:KEYS], takes[:, PAST:KEYS], own_keys[:, 0, :], ALU.mult)
                step(dve.tensor_tensor(keeps[:, PAST:KEYS], keeps[:, PAST:KEYS], own_keys[:, 1, :], ALU.max))
                step(dve.tensor_tensor_scan(rests[:, ::-1], keeps[:, ::-1], zero[0:96, :].broadcast_to([96, KEYS]), 1.0, ALU.mult, ALU.add))
                dve.tensor_tensor(keeps[:, 0:KEYS - 1], takes[:, 0:KEYS - 1], rests[:, 1:KEYS], ALU.mult)
                dve.tensor_copy(keeps[:, KEYS - 1:KEYS], takes[:, KEYS - 1:KEYS]).then_inc(S.as_ready, 1)
                if b:
                    mixed_lo(b - 1)
            mixed_lo(NB - 1)

        block = ctx.enter_context(nc.Block())

        @block.sync
        def _(sp):
            setup_sp(sp)
            mem_sp(sp)
            ffn_sp(sp, 0)
            ina_sp(sp)
            out_sp(sp, BASE_OUTA, 0, (0, 1))
            states_sp(sp)
            out_sp(sp, BASE_OUTA, 0, (2, 3))
            ffn_sp(sp, 1)
            kv_sp(sp)
            ffn_sp(sp, 2)
            inb_sp(sp)
            out_sp(sp, BASE_OUTB, 1, range(4))
            ffn_sp(sp, 3)
            end_sp(sp)

        @block.gpsimd
        def _(pool):
            c = Count()
            setup_pool(pool, c)
            mem_pool(pool, c)
            ina_pool(pool, c)
            mla_pool(pool)
            mem_attention_pool(pool, 0, MA, c)
            kv_pool(pool)
            mem_attention_pool(pool, 1, MB, c)
            pages_pool(pool)
            pool.wait_ge(S.stored, 64)
            pool.wait_ge(S.m_stored, 32)
            pool.wait_ge(S.tails_stored, 32)
            pool.wait_ge(S.head_stored, 48 * HA)
            states_stored(pool)
            pool.wait_ge(S.kv_stored, 64)

        @block.scalar
        def _(act):
            c = Count()
            small_inputs(act)
            setup_act(act)
            mem_act(act)
            ffn_act(act, 0, 1)
            norm_act(act, 1, 1, False)
            ina_act(act, c)
            mla_act(act)
            states_stored(act)
            qnorm_act(act, 0, 2, 0, lambda k: qm_a[:, k, :])
            mem_attention_act(act, 0, MA)
            ha_act(act)
            out_act(act, BASE_OUTA, 2)
            norm_act(act, 2, 2, False)
            ffn_act(act, 1, 3)
            norm_act(act, 3, 3, False)
            kv_act(act)
            norm_act(act, 3, 4, True)
            ffn_act(act, 2, 4)
            norm_act(act, 4, 5, False)
            inb_act(act)
            qnorm_act(act, 2, 8, 1, queries_b)
            mem_attention_act(act, 1, MB)
            stick_act(act)
            stick_sample_act(act)
            out_act(act, BASE_OUTB, 5)
            norm_act(act, 5, 6, False)
            ffn_act(act, 3, None)

        @block.vector
        def _(dve):
            c = Count()
            setup_dve(dve, c)
            mem_dve(dve, c)
            ffn_dve(dve, 0, 1)
            norm_dve(dve, 1, 1, False, gain("mix", 0))
            ina_dve(dve, c)
            turned_rows_dve(dve)
            mla_dve(dve, c)
            qnorm_dve(dve, 0, 2, 0, lambda k: qm_a[:, k, :], lambda k: MA.qn[:, k, :], lambda k: vec_t[:, 72:73])
            mem_attention_dve(dve, 0, MA, c)
            ha_dve(dve)
            out_dve(dve, BASE_OUTA, 2)
            norm_dve(dve, 2, 2, False, gain("ffn2", 0))
            ffn_dve(dve, 1, 3)
            norm_dve(dve, 3, 3, False, gain("kv"), keep=True)
            kv_dve(dve, c)
            norm_dve(dve, 3, 4, True, gain("ffn1", 1))
            ffn_dve(dve, 2, 4)
            norm_dve(dve, 4, 5, False, gain("mix", 1))
            for n in range(BASE_INB, BASE_OUTB):
                split_lo(dve, n + 1, (n + 1) % 2)
            qnorm_dve(dve, 2, 8, 1, queries_b, queries_b, lambda k: vec_t[:, 73:74] if k < 2 else vec_t[:, 74:75])
            mem_attention_dve(dve, 1, MB, c)
            stick_dve(dve, c)
            stick_sample_dve(dve, c)
            out_dve(dve, BASE_OUTB, 5)
            norm_dve(dve, 5, 6, False, gain("ffn2", 1))
            ffn_dve(dve, 3, None)
            end_dve(dve)

        @block.tensor
        def _(pe):
            setup_pe(pe)
            mem_pe(pe)
            ffn_pe(pe, 0, 0)
            hist_pe(pe)
            norm_pe(pe, 1, BASE_INA)
            ina_pe(pe, 1)
            turned_rows_pe(pe)
            mla_pe(pe)
            qnorm_pe(pe, 0, 2, 0)
            mem_attention_pe(pe, 0, MA)
            ha_pe(pe)
            pe.wait_ge(S.mix_lo, 6)
            out_pe(pe, BASE_OUTA)
            norm_pe(pe, 2, BASE_FFN[1])
            ffn_pe(pe, 1, 2)
            norm_pe(pe, 3, BASE_KV)
            kv_pe(pe, 3)
            ffn_pe(pe, 2, 4)
            norm_pe(pe, 4, BASE_INB)
            inb_pe(pe, 5)
            pe.wait_ge(S.region_free0, BASE_OUTB // 2)
            pe.wait_ge(S.region_free1, BASE_OUTB // 2)
            qnorm_pe(pe, 2, 8, 1)
            mem_attention_pe(pe, 1, MB)
            stick_pe(pe)
            stick_sample_pe(pe)
            pe.wait_ge(S.sb_lo, NB)
            out_pe(pe, BASE_OUTB)
            norm_pe(pe, 5, BASE_FFN[3])
            ffn_pe(pe, 3, 6)
            end_pe(pe)


INS = ["x_prompt", "x_sample", "cache_k", "cache_v", "cache_mem_k", "cache_mem_v", "state_C", "state_n", "state_m",
       "state_conv", "page_table", "mem_prompt", "g_ffn1", "w_ffn1_up", "w_ffn1_down", "g_mix", "w_in_a", "b_gate_a",
       "conv_w_a", "conv_b_a", "g_h_a", "g_kv", "w_kv", "g_k_b", "w_in_b", "g_q_b", "b_sb", "g_mem", "w_mem_kv",
       "g_q_mem", "g_k_mem", "w_out", "g_ffn2", "w_ffn2_up", "w_ffn2_down"]
OUTS = [("y_prompt", (1, NPR, D)), ("y_sample", (NB, NS, D)),
        ("k_prompt", (1, NPR, HB, DB)), ("v_prompt", (1, NPR, HB, DB)),
        ("k_sample", (NB, NS, HB, DB)), ("v_sample", (NB, NS, HB, DB)),
        ("mem_k_prompt", (2, 1, M, HM, DM)), ("mem_v_prompt", (2, 1, M, HM, DM)),
        ("conv_prompt", (1, 1, 3, 2 * D_MAIN)), ("C_prompt", (1, 1, HA, DA, DA)), ("n_prompt", (1, 1, HA, DA)),
        ("m_prompt", (1, 1, HA)),
        ("conv_sample", (1, NB, 3, 2 * D_MAIN)), ("C_sample", (1, NB, HA, DA, DA)), ("n_sample", (1, NB, HA, DA)),
        ("m_sample", (1, NB, HA))]


def kernel(**inputs):
    import numpy as np
    from concourse import bacc
    from concourse.bass_utils import run_bass_kernel_spmd

    nc = bacc.Bacc("TRN2", target_bir_lowering=False, num_devices=1)
    arrays, ins, outs = {}, {}, {}
    for name in INS:
        a = np.ascontiguousarray(inputs[name])
        arrays[f"in_{name}"] = a
        ins[name] = nc.dram_tensor(f"in_{name}", a.shape, mybir.dt.from_np(a.dtype), kind="ExternalInput").ap()
    for name, shape in OUTS:
        outs[name] = nc.dram_tensor(f"out_{name}", shape, F32, kind="ExternalOutput").ap()
    build(nc, ins, outs)
    r = run_bass_kernel_spmd(nc, [arrays], core_ids=[0])
    return tuple(r.results[0][f"out_{name}"] for name, _ in OUTS)
```
